# Optimizing a Trainium2 kernel written in Bass

```python
import math
import jax, jax.numpy as jnp
from jax import lax
import numpy as np

D_MODEL = 1024
BATCH = 1
SEQ = 256
DEPTH = 2

N_META = 16
RWKV_HEAD_DIM = 64
RWKV_WIDTH = D_MODEL // 4
RWKV_HEADS = RWKV_WIDTH // RWKV_HEAD_DIM
DECAY_LORA = 32
AAA_LORA = 32
GATE_LORA = 64
DIFF_QK_DIM = 64
DIFF_V_DIM = 2 * DIFF_QK_DIM
DIFF_WIDTH = D_MODEL // 2
DIFF_HEADS = DIFF_WIDTH // DIFF_V_DIM
CONV_WIDTH = D_MODEL - RWKV_WIDTH - DIFF_WIDTH
CONV_K = 3
ROPE_THETA = 500000.0
ROPE_DIM = DIFF_QK_DIM // 4
Q_BLOCK = 128
D_FF = 2816
N_EXPERTS = 8
TOP_K = 2
MOE_BLOCK = 256
N_DENSE = (DEPTH + 1) // 2
N_MOE = DEPTH // 2
NORM_EPS = 1e-6
RWKV_GN_EPS = 64e-5
SUBLN_EPS = 1e-5
NEG_INF = -1e30

RWKV_COLS = 3 * RWKV_WIDTH + DECAY_LORA + AAA_LORA + GATE_LORA
DIFF_COLS = 2 * DIFF_HEADS * 2 * DIFF_QK_DIM + DIFF_HEADS * DIFF_V_DIM
CONV_COLS = 3 * CONV_WIDTH
IN_COLS = RWKV_COLS + DIFF_COLS + CONV_COLS

kernel_name = "hymba_rwkv7_diffattn_shortconv_moe"

def rms_norm(t, g, eps):
    tf = t.astype(jnp.float32)
    tf = tf * lax.rsqrt(jnp.mean(tf * tf, axis=-1, keepdims=True) + eps)
    return (tf * g.astype(jnp.float32)).astype(t.dtype)

def swiglu(t, w_gate, w_up, w_down):
    return (jax.nn.silu(t @ w_gate) * (t @ w_up)) @ w_down

def rope_tables(length):
    inv_freq = ROPE_THETA ** (-jnp.arange(0, ROPE_DIM, 2, dtype=jnp.float32) / ROPE_DIM)
    ang = jnp.arange(length, dtype=jnp.float32)[:, None] * inv_freq[None, :]
    return jnp.cos(ang), jnp.sin(ang)

def apply_partial_rope(t, cos, sin):
    half = ROPE_DIM // 2
    c = cos[None, :, None, None, :].astype(t.dtype)
    s = sin[None, :, None, None, :].astype(t.dtype)
    t1, t2 = t[..., :half], t[..., half:ROPE_DIM]
    return jnp.concatenate([t1 * c - t2 * s, t2 * c + t1 * s, t[..., ROPE_DIM:]], axis=-1)

def rwkv7_time_mix(hx, mu, w0, w_decay_up, a0, w_a_up, w_g_up, k_k, k_a, r_k, gn_g, gn_b):
    b, l, _ = hx.shape
    H, N = RWKV_HEADS, RWKV_HEAD_DIM
    prev = jnp.pad(hx, ((0, 0), (1, 0), (0, 0)))[:, :-1]
    hx = hx + (prev - hx) * mu
    s1 = RWKV_WIDTH
    r, k, v, hw, ha, hg = jnp.split(
        hx, [s1, 2 * s1, 3 * s1, 3 * s1 + DECAY_LORA, 3 * s1 + DECAY_LORA + AAA_LORA], axis=-1)
    w = -jax.nn.softplus(-(w0 + jnp.tanh(hw) @ w_decay_up)) - 0.5
    decay = jnp.exp(-jnp.exp(w.astype(jnp.float32)))
    a = jax.nn.sigmoid(a0 + ha @ w_a_up)
    g = jax.nn.sigmoid(hg) @ w_g_up
    heads = lambda t: t.reshape(b, l, H, N)
    kk = heads(k * k_k).astype(jnp.float32)
    kk = kk / jnp.maximum(jnp.sqrt(jnp.sum(kk * kk, axis=-1, keepdims=True)), 1e-12)
    k = k * (1.0 + (a - 1.0) * k_a)
    r_h, k_h, v_h = heads(r), heads(k), heads(v)
    a_h = heads(a).astype(jnp.float32)
    tm = lambda t: jnp.swapaxes(t.astype(jnp.float32), 0, 1)
    xs = (tm(r_h), tm(heads(decay)), tm(k_h), tm(v_h), tm(-kk), tm(kk * a_h))

    def step(S, inp):
        r_t, w_t, k_t, v_t, a_t, b_t = inp
        sa = jnp.einsum('bhvk,bhk->bhv', S, a_t)
        S = S * w_t[:, :, None, :] + sa[..., None] * b_t[:, :, None, :] + v_t[..., None] * k_t[:, :, None, :]
        return S, jnp.einsum('bhvk,bhk->bhv', S, r_t)

    S0 = jnp.zeros((b, H, N, N), jnp.float32)
    _, y = lax.scan(step, S0, xs)
    y = jnp.swapaxes(y, 0, 1)
    mean = jnp.mean(y, axis=-1, keepdims=True)
    var = jnp.mean(jnp.square(y - mean), axis=-1, keepdims=True)
    y = ((y - mean) * lax.rsqrt(var + RWKV_GN_EPS)).reshape(b, l, RWKV_WIDTH)
    y = (y * gn_g.astype(jnp.float32) + gn_b.astype(jnp.float32)).astype(hx.dtype)
    bonus = jnp.sum(r_h * k_h * r_k, axis=-1, keepdims=True) * v_h
    return (y + bonus.reshape(b, l, RWKV_WIDTH)) * g

def diff_attention(hx, cos, sin, q_norm_g, k_norm_g, lq1, lk1, lq2, lk2, subln_g, lam_init):
    b, l, _ = hx.shape
    H, dk, dv = DIFF_HEADS, DIFF_QK_DIM, DIFF_V_DIM
    qw = H * 2 * dk
    q, k, v = jnp.split(hx, [qw, 2 * qw], axis=-1)
    q = q.reshape(b, l, H, 2, dk)
    k = k.reshape(b, l, H, 2, dk)
    v = v.reshape(b, l, H, dv)
    q = apply_partial_rope(rms_norm(q, q_norm_g, NORM_EPS), cos, sin) * (dk ** -0.5)
    k = apply_partial_rope(rms_norm(k, k_norm_g, NORM_EPS), cos, sin)
    lam = (jnp.exp(jnp.sum(lq1.astype(jnp.float32) * lk1.astype(jnp.float32)))
           - jnp.exp(jnp.sum(lq2.astype(jnp.float32) * lk2.astype(jnp.float32))) + lam_init)
    pad = (-l) % Q_BLOCK
    lp = l + pad
    nb = lp // Q_BLOCK
    qp = jnp.pad(q, ((0, 0), (pad, 0), (0, 0), (0, 0), (0, 0)))
    kp = jnp.pad(k, ((0, 0), (pad, 0), (0, 0), (0, 0), (0, 0)))
    vp = jnp.pad(v, ((0, 0), (pad, 0), (0, 0), (0, 0)))
    qb = jnp.moveaxis(qp.reshape(b, nb, Q_BLOCK, H, 2, dk), 1, 0)
    kpos = jnp.arange(lp)

    def one_block(args):
        qi, i = args
        s = jnp.einsum('bqhcd,bkhcd->bhcqk', qi, kp).astype(jnp.float32)
        qpos = i * Q_BLOCK + jnp.arange(Q_BLOCK)
        mask = (kpos[None, :] <= qpos[:, None]) & (kpos[None, :] >= pad)
        p = jax.nn.softmax(jnp.where(mask, s, NEG_INF), axis=-1)
        pd = p[:, :, 0] - lam * p[:, :, 1]
        return jnp.einsum('bhqk,bkhe->bqhe', pd.astype(vp.dtype), vp)

    o = lax.map(one_block, (qb, jnp.arange(nb)))
    o = jnp.moveaxis(o, 0, 1).reshape(b, lp, H, dv)[:, pad:]
    o = rms_norm(o, subln_g, SUBLN_EPS) * (1.0 - lam_init)
    return o.reshape(b, l, DIFF_WIDTH)

def short_conv(hx, conv_w):
    l = hx.shape[1]
    bg, cg, u = jnp.split(hx, [CONV_WIDTH, 2 * CONV_WIDTH], axis=-1)
    z = jnp.pad(cg * u, ((0, 0), (CONV_K - 1, 0), (0, 0)))
    y = sum(conv_w[j] * z[:, j:j + l] for j in range(CONV_K))
    return bg * y

def moe_swiglu(xt, router_w, w_gate, w_up, w_down):
    T, D = xt.shape
    logits = (xt @ router_w).astype(jnp.float32)
    top_logit, top_idx = lax.top_k(logits, TOP_K)
    gates = jax.nn.softmax(top_logit, axis=-1).astype(xt.dtype)
    TK = T * TOP_K
    flat_e = top_idx.reshape(TK).astype(jnp.int32)
    flat_tok = jnp.repeat(jnp.arange(T, dtype=jnp.int32), TOP_K)
    flat_g = gates.reshape(TK)
    order = jnp.argsort(flat_e * TK + jnp.arange(TK, dtype=jnp.int32))
    se, stok, sg = flat_e[order], flat_tok[order], flat_g[order]
    counts = jnp.bincount(flat_e, length=N_EXPERTS)
    padded = (counts + MOE_BLOCK - 1) // MOE_BLOCK * MOE_BLOCK
    start = jnp.cumsum(counts) - counts
    pend = jnp.cumsum(padded)
    pstart = pend - padded
    dest = pstart[se] + jnp.arange(TK, dtype=jnp.int32) - start[se]
    NB = -(-TK // MOE_BLOCK) + N_EXPERTS
    P = NB * MOE_BLOCK
    row_tok = jnp.full((P,), T, jnp.int32).at[dest].set(stok)
    row_gate = jnp.zeros((P,), xt.dtype).at[dest].set(sg)
    block_expert = jnp.minimum(
        jnp.searchsorted(pend, jnp.arange(NB, dtype=pend.dtype) * MOE_BLOCK, side='right'), N_EXPERTS - 1)
    x_rows = jnp.concatenate([xt, jnp.zeros((1, D), xt.dtype)], axis=0)[row_tok].reshape(NB, MOE_BLOCK, D)

    def expert_block(args):
        xb, e = args
        return swiglu(xb, w_gate[e], w_up[e], w_down[e])

    y_rows = lax.map(expert_block, (x_rows, block_expert)).reshape(P, D)
    return jax.ops.segment_sum(y_rows * row_gate[:, None], row_tok, num_segments=T + 1)[:T]

def setup_inputs(seed: int = 0) -> dict:
    key = jax.random.key(seed)
    keys = iter(jax.random.split(key, 40))
    f32 = jnp.float32

    def normal(shape, scale):
        return jax.random.normal(next(keys), shape, f32) * scale

    def gain(shape):
        return 1.0 + normal(shape, 0.02)

    def uniform(shape, lo, hi):
        return jax.random.uniform(next(keys), shape, f32, lo, hi)

    return {
        "x": normal((BATCH, SEQ, D_MODEL), 1.0),
        "meta_tokens": normal((N_META, D_MODEL), 1.0),
        "mix_norm_g": gain((DEPTH, D_MODEL)),
        "w_in": normal((DEPTH, D_MODEL, IN_COLS), D_MODEL ** -0.5),
        "tm_mu": uniform((DEPTH, RWKV_COLS), 0.0, 1.0),
        "tm_w0": uniform((DEPTH, RWKV_WIDTH), -6.0, 1.0),
        "tm_w_decay_up": normal((DEPTH, DECAY_LORA, RWKV_WIDTH), 0.1),
        "tm_a0": normal((DEPTH, RWKV_WIDTH), 0.1),
        "tm_w_a_up": normal((DEPTH, AAA_LORA, RWKV_WIDTH), 0.1),
        "tm_w_g_up": normal((DEPTH, GATE_LORA, RWKV_WIDTH), GATE_LORA ** -0.5),
        "tm_k_k": 0.85 + normal((DEPTH, RWKV_WIDTH), 0.02),
        "tm_k_a": gain((DEPTH, RWKV_WIDTH)),
        "tm_r_k": normal((DEPTH, RWKV_HEADS, RWKV_HEAD_DIM), 0.1),
        "tm_gn_g": gain((DEPTH, RWKV_WIDTH)),
        "tm_gn_b": normal((DEPTH, RWKV_WIDTH), 0.02),
        "da_q_norm_g": gain((DEPTH, DIFF_QK_DIM)),
        "da_k_norm_g": gain((DEPTH, DIFF_QK_DIM)),
        "da_lambda_q1": normal((DEPTH, DIFF_QK_DIM), 0.1),
        "da_lambda_k1": normal((DEPTH, DIFF_QK_DIM), 0.1),
        "da_lambda_q2": normal((DEPTH, DIFF_QK_DIM), 0.1),
        "da_lambda_k2": normal((DEPTH, DIFF_QK_DIM), 0.1),
        "da_subln_g": gain((DEPTH, DIFF_V_DIM)),
        "sc_conv_w": normal((DEPTH, CONV_K, CONV_WIDTH), CONV_K ** -0.5),
        "w_out": normal((DEPTH, D_MODEL, D_MODEL), D_MODEL ** -0.5),
        "ffn_norm_g": gain((DEPTH, D_MODEL)),
        "ffn_w_gate": normal((N_DENSE, D_MODEL, D_FF), D_MODEL ** -0.5),
        "ffn_w_up": normal((N_DENSE, D_MODEL, D_FF), D_MODEL ** -0.5),
        "ffn_w_down": normal((N_DENSE, D_FF, D_MODEL), D_FF ** -0.5),
        "router_w": normal((N_MOE, D_MODEL, N_EXPERTS), D_MODEL ** -0.5),
        "moe_w_gate": normal((N_MOE, N_EXPERTS, D_MODEL, D_FF), D_MODEL ** -0.5),
        "moe_w_up": normal((N_MOE, N_EXPERTS, D_MODEL, D_FF), D_MODEL ** -0.5),
        "moe_w_down": normal((N_MOE, N_EXPERTS, D_FF, D_MODEL), D_FF ** -0.5),
    }

def reference(x, meta_tokens, mix_norm_g, w_in, tm_mu, tm_w0, tm_w_decay_up, tm_a0, tm_w_a_up,
              tm_w_g_up, tm_k_k, tm_k_a, tm_r_k, tm_gn_g, tm_gn_b, da_q_norm_g, da_k_norm_g,
              da_lambda_q1, da_lambda_k1, da_lambda_q2, da_lambda_k2, da_subln_g, sc_conv_w,
              w_out, ffn_norm_g, ffn_w_gate, ffn_w_up, ffn_w_down, router_w, moe_w_gate,
              moe_w_up, moe_w_down):
    b = x.shape[0]
    meta = jnp.broadcast_to(meta_tokens.astype(x.dtype)[None], (b, N_META, D_MODEL))
    h = jnp.concatenate([meta, x], axis=1)
    l = h.shape[1]
    cos, sin = rope_tables(l)
    for i in range(DEPTH):
        lam_init = 0.8 - 0.6 * math.exp(-0.3 * i)
        proj = rms_norm(h, mix_norm_g[i], NORM_EPS) @ w_in[i]
        p_a = proj[..., :RWKV_COLS]
        p_b = proj[..., RWKV_COLS:RWKV_COLS + DIFF_COLS]
        p_c = proj[..., RWKV_COLS + DIFF_COLS:]
        o_a = rwkv7_time_mix(p_a, tm_mu[i], tm_w0[i], tm_w_decay_up[i], tm_a0[i], tm_w_a_up[i],
                             tm_w_g_up[i], tm_k_k[i], tm_k_a[i], tm_r_k[i], tm_gn_g[i], tm_gn_b[i])
        o_b = diff_attention(p_b, cos, sin, da_q_norm_g[i], da_k_norm_g[i], da_lambda_q1[i],
                             da_lambda_k1[i], da_lambda_q2[i], da_lambda_k2[i], da_subln_g[i], lam_init)
        o_c = short_conv(p_c, sc_conv_w[i])
        h = h + jnp.concatenate([o_a, o_b, o_c], axis=-1) @ w_out[i]
        hn = rms_norm(h, ffn_norm_g[i], NORM_EPS)
        j = i // 2
        if i % 2 == 0:
            f = swiglu(hn, ffn_w_gate[j], ffn_w_up[j], ffn_w_down[j])
        else:
            f = moe_swiglu(hn.reshape(b * l, D_MODEL), router_w[j], moe_w_gate[j], moe_w_up[j],
                           moe_w_down[j]).reshape(b, l, D_MODEL)
        h = h + f
    return h[:, N_META:]


_drawn_inputs = setup_inputs


def setup_inputs(seed=0):
    import zlib

    import numpy as np

    out = dict(_drawn_inputs(seed))
    spreads = {}
    factors = {'tm_w_decay_up': 3.656,
     'tm_a0': 4.274,
     'tm_k_k': 16.226,
     'tm_k_a': 3.287,
     'tm_gn_g': 5.786,
     'tm_gn_b': 12.378,
     'da_k_norm_g': 2.81,
     'da_lambda_q1': 2.749,
     'da_lambda_k2': 3.58,
     'da_subln_g': 3.521,
     'ffn_norm_g': 3.186}
    for name, (base, spread) in spreads.items():
        noise = np.random.default_rng([zlib.crc32(name.encode()), seed]).standard_normal(out[name].shape)
        drawn = base * np.exp(spread * noise) if base else spread * noise
        out[name] = __import__('jax').numpy.asarray(drawn.astype(out[name].dtype))
    for name, factor in factors.items():
        out[name] = (out[name] * factor).astype(out[name].dtype)
    return out
```

```python
import math
from collections import namedtuple
from contextlib import ExitStack

import numpy as np

import concourse.bass as bass
from concourse import mybir

F32 = mybir.dt.float32
I32 = mybir.dt.int32
U32 = mybir.dt.uint32
ALU = mybir.AluOpType
ACT = mybir.ActivationFunctionType
AXX = mybir.AxisListType.X

P = 128
D = 1024
DC = D // P
SEQ = 256
META = 16
T = SEQ + META
TILES = [(0, 128), (128, 128), (256, 16)]
DEPTH = 2
HR, NR = 4, 64
RW = HR * NR
HD, DK = 4, 64
FF = 2816
FC = FF // P
NE = 8
TOPK = 2
IN_COLS = 3200
NCH = IN_COLS // P
RWKV_CH, Q_CH, K_CH, V_CH, BG_CH, CG_CH, U_CH = 0, 7, 11, 15, 19, 21, 23
LAM_INIT = [0.8 - 0.6 * math.exp(-0.3 * i) for i in range(DEPTH)]
NORM_EPS, GN_EPS, SUB_EPS = 1e-6, 64e-5, 1e-5
CH = 32
NCHUNK = -(-T // CH)
E_HALF = math.exp(-0.5)

CAP = 96
MAXO = (T * TOPK) // CAP
NIT = NE + MAXO + 1
NFLAG = NE * (-(-T // CAP) - 1)

SMALL_RING = 5
BIG_RING = 14
SLOT = 2048
PIECE = 2 * P

ROWS = 48
(MIXG, FFNG, MU, W0, A0, KK, KA, RK, GNG, GNB, QG, KG, SUBG, CONV, LAMQ, LAMK) = (
    0, 8, 16, 23, 25, 27, 29, 31, 33, 35, 37, 38, 39, 40, 46, 47)

CONSTS = ["ident", "ones", "blk", "rope", "m16t", "m16", "moff", "m32s", "m32i", "causal", "tri"]
WIDE = ["cos", "sin", "reset", "iota"]


def constants():
    r = np.arange(P)
    a, b = r[:, None], r[None, :]
    c = {
        "ident": a == b,
        "ones": np.ones((P, P)),
        "blk": a // 64 == b // 64,
        "m16t": (a < b) & (a // 16 == b // 16),
        "m16": (b < a) & (a // 16 == b // 16),
        "moff": (b < a) & (a // 32 == b // 32) & (a // 16 != b // 16),
        "m32s": (a < b) & (a // 32 == b // 32),
        "m32i": (a <= b) & (a // 32 == b // 32),
        "causal": np.where(b > a, -1e30, 0.0),
        "tri": a < b,
    }
    rope = np.zeros((P, P))
    for h in (0, 64):
        for d in range(8):
            rope[h + d + 8, h + d] = -1.0
            rope[h + d, h + d + 8] = 1.0
    c["rope"] = rope
    inv = (np.float32(500000.0) ** (-np.arange(0, 16, 2, dtype=np.float32) / np.float32(16))).astype(np.float32)
    ang = np.arange(T, dtype=np.float32)[:, None] * inv[None, :]
    cos, sin = np.ones((P, T), np.float32), np.zeros((P, T), np.float32)
    for h in (0, 8, 64, 72):
        cos[h:h + 8] = np.cos(ang).T
        sin[h:h + 8] = np.sin(ang).T
    reset = np.broadcast_to((np.arange(T) % CH != 0), (P, T))
    iota = np.broadcast_to(np.arange(CAP * -(-T // CAP)), (P, CAP * -(-T // CAP)))
    parts = [np.asarray(c[n], np.float32) for n in CONSTS] + [cos, sin, reset, iota]
    return np.ascontiguousarray(np.concatenate([np.asarray(x, np.float32) for x in parts], axis=1))


def build(nc, A, out):
    ctx = ExitStack()
    with ctx:
        def sb(name, shape, dt=F32):
            return ctx.enter_context(nc.sbuf_tensor(name, shape, dt))

        def sems(*names):
            return namedtuple("Semaphores", names)(*(ctx.enter_context(nc.semaphore(n)) for n in names))

        ps = ctx.enter_context(nc.psum_tensor("ps", [P, 8, 512], F32))
        hT = sb("hT", [P, DC, T])
        hnT = sb("hnT", [P, DC, T])
        ring_small = sb("ring_small", [P, SMALL_RING, SLOT])
        vrow = sb("vrow", [DEPTH * ROWS, P])
        vcol = sb("vcol", [P, DEPTH * ROWS])
        vhalf = sb("vhalf", [P, DEPTH, 4])
        wide = CAP * -(-T // CAP)
        cst = sb("cst", [P, P * len(CONSTS) + 3 * T + wide])
        C = namedtuple("Tables", CONSTS)(*(cst[:, P * k:P * k + P] for k in range(len(CONSTS))))
        o = P * len(CONSTS)
        cosT, sinT, resetT = (cst[:, o + k * T:o + (k + 1) * T] for k in range(3))
        iotaT = cst[:, o + 3 * T:o + 3 * T + wide]
        epsT = sb("epsT", [P, 3])
        msT = sb("msT", [P, 4 * T])
        rsT = sb("rsT", [P, 4 * T])
        small = sb("small", [P, 64])
        ARENA = 33250
        arena = sb("arena", [P, ARENA])
        used = [0]

        def carve(*shape):
            n = int(np.prod(shape))
            v = arena[:, used[0]:used[0] + n]
            used[0] += n
            assert used[0] <= ARENA, used[0]
            if len(shape) == 1:
                return v
            names = "abcd"[:len(shape)]
            return v.rearrange(f"p ({' '.join(names)}) -> p {' '.join(names)}",
                               **{n: s for n, s in zip(names, shape)})

        projT = carve(NCH, T + 2)
        sqT = carve(DC, T)
        oT = carve(DC, T)
        hxT = carve(7, T)
        lora = carve(T)
        lora_w = carve(RW)
        eT, cumT, PtT, AtT, KtT, KhT, aT, gT, kkT, bT, BtT, RtT, bonusT, kks = (carve(2, T) for _ in range(14))
        cvT = kks
        tokAV = carve(3, 2, 256)
        tokBK = carve(2, 2, 256)
        mark = used[0]
        m16, mt16, moff, m2, mt2, ntm, qm = (carve(4, P) for _ in range(7))
        rbm, rkm = ([carve(4, P), carve(4, P), carve(4, TILES[2][1])] for _ in range(2))
        wT = carve(2, T)
        nv = carve(256)
        zTok = carve(3, 256)
        uTok = carve(3, 256)
        stT = carve(NCHUNK, 2, NR)
        pst = carve(2, NR)
        used[0] = mark
        vTok = carve(3, 512)
        prob = carve(2, 2, T)
        pd = carve(2, T)
        scaled = carve(T)
        pT = carve(2, 3, T)
        oat = carve(4, T)
        used[0] = mark
        xTok = carve(3, D)
        used[0] = 0
        hid = carve(FC, T)
        sg = carve(2, T)
        xe = carve(DC, CAP)
        oneh = carve(3, CAP)
        gateh = carve(3, CAP)
        gateT = carve(T)
        yE = carve(D)
        hnTok = carve(3, D)
        router = carve(DC, NE)
        lgS, sel, posx, gates, oh1, oh2, top8 = (carve(3, NE) for _ in range(7))
        fidx, gw = carve(3, 2), carve(3, 2)
        cnt, flag, incl, ev, ov = (carve(NFLAG) for _ in range(5))
        eqg, pick = carve(MAXO, NFLAG), carve(MAXO, NFLAG)
        big = carve(BIG_RING - SMALL_RING, SLOT)
        tab = sb("tab", [1, 2, NIT], I32)
        ntab = sb("ntab", [1, 1], I32)
        fsum = sb("fsum", [1, 2, NIT])
        stat = sb("stat", [P, 2, 6])
        idx8 = sb("idx8", [P, 3, 8], U32)

        def slot(s):
            return ring_small[:, s, :] if s < SMALL_RING else big[:, s - SMALL_RING, :]

        w_in, w_out = A["w_in"], A["w_out"]

        def cols_piece(w, n0, n):
            return w[:, n0:n0 + n].rearrange("(c p) n -> p c n", p=P)

        def rows_piece(w, r0):
            return w[r0:r0 + PIECE, :].rearrange("(c p) n -> p c n", p=P)

        def mixer_loads(l):
            for n0 in range(0, IN_COLS, PIECE):
                n = min(PIECE, IN_COLS - n0)
                yield cols_piece(w_in[l], n0, n), DC * n
            for n0 in range(0, D, PIECE):
                yield cols_piece(w_out[l], n0, PIECE), SLOT

        def ffn_loads(g, u, d):
            for s in range(FF // PIECE):
                yield cols_piece(g, s * PIECE, PIECE), SLOT
                yield cols_piece(u, s * PIECE, PIECE), SLOT
            for s in range(FF // PIECE):
                yield rows_piece(d, s * PIECE), SLOT

        MIXN, FFNN = -(-IN_COLS // PIECE) + D // PIECE, 3 * FF // PIECE
        STATIC = 2 * MIXN + FFNN
        slot_of, prior, filled = [], [], [0] * BIG_RING
        last = [None] * BIG_RING
        load_value = []
        for k in range(STATIC):
            if k < MIXN:
                s = k % SMALL_RING
            elif k < MIXN + FFNN:
                s = (k - MIXN + MIXN % SMALL_RING) % BIG_RING
            else:
                s = (k - STATIC + SMALL_RING) % SMALL_RING
            slot_of.append(s)
            prior.append(last[s])
            last[s] = k
            filled[s] += 1
            load_value.append(filled[s])
        item_prior = []
        for j in range(FFNN):
            before = [k for k in range(-FFNN, j) if (k % FFNN) % BIG_RING == j % BIG_RING]
            item_prior.append(max(before))
        for j in range(BIG_RING):
            assert last[j] is None or last[j] < STATIC + item_prior[j] + 1
        per_item = [len(range(s, FFNN, BIG_RING)) for s in range(BIG_RING)]

        loaded = [ctx.enter_context(nc.semaphore(f"piece_in_slot{s}")) for s in range(BIG_RING)]

        S = sems(
            "consts_in", "params_in", "x_in", "lora_w_in", "out_stored", "router_in",
            "eps_set", "pads_zero", "vcol_mm", "vcol_ready", "vhalf_ready", "dve_chain", "pool_chain",
            "x_mm", "h_ready", "sq_ready", "nsum_mm", "root_ready", "kk_max", "rs_ready", "hn_ready",
            "pieces_used", "proj_mm", "proj_act", "proj_dve",
            "shift_d", "hx_ready", "lora_act", "lora_sig", "lora_mm", "lora_out",
            "decay_ready", "exp_ready", "kk_sq", "kk_mm", "bonus_pre", "bonus_mm", "til_ready",
            "tok_mm", "tok_ready", "mat_mm", "mat_ev", "lvl_mm", "lvl_act", "lvl_dve", "q1_ready",
            "wt_mm", "wt_act", "nv_ready",
            "u_mm", "u_ready", "st_mm", "st_ready", "y_mm", "y_sb",
            "gn_mm", "gn_cent", "gn_sq", "oa_ready", "oc_ready",
            "qk_sq", "qk_mm", "qg_ready", "qcos_ready", "rot_mm", "qk_ready",
            "vt_mm", "vt_ready", "lam_prod", "lam_mm", "lam_exp",
            "sc_mm", "mx_ready", "p_ready", "pd_ready", "pt_mm", "pt_ready", "o_mm", "o_sb", "osq_ready",
            "ob_mm", "ob_ready", "wout_mm",
            "gu_mm", "silu_ready", "hid_ready", "down_mm",
            "hntok_mm", "hntok_ready", "lg_mm", "gap_ready", "gap_exp", "sel_ready", "pos_mm", "table_ready",
            "oneh_ready", "gather_mm", "xe_act", "xe_dve", "gt_mm", "gt_ready", "y_act", "y_dve", "scat_mm",
            "h_item", "out_mm", "out_act", "out_dve",
        )
        block = ctx.enter_context(nc.Block())

        def vc(l, k, n=1):
            return vcol[:, l * ROWS + k:l * ROWS + k + n]

        def bc(ap, n):
            return ap.unsqueeze(1).broadcast_to([ap.shape[0], n, ap.shape[1]])

        def tail(ap, n):
            return ap.unsqueeze(len(ap.shape)).broadcast_to(list(ap.shape) + [n])

        def cur(c0, n=1):
            return projT[:, c0:c0 + n, 2:T + 2]

        def prev(c0, k, n=1):
            return projT[:, c0:c0 + n, 2 - k:T + 2 - k]

        def lvl(per_tile, l, i):
            return (2 * per_tile[0] + per_tile[1]) * l + per_tile[0] * i

        LVM, LVA, LVD = (11, 8), (6, 5), (5, 3)
        NORMS = 7

        @block.sync
        def _(sp):
            sp.dma_start(cst[:], A["consts"]).then_inc(S.consts_in, 16)
            sp.dma_start(xTok[0:META, 0, :], A["meta_tokens"]).then_inc(S.x_in, 16)
            sp.dma_start(xTok[META:P, 0, :], A["x"][0, 0:P - META, :]).then_inc(S.x_in, 16)
            sp.dma_start(xTok[:, 1, :], A["x"][0, P - META:2 * P - META, :]).then_inc(S.x_in, 16)
            sp.dma_start(xTok[0:META, 2, :], A["x"][0, 2 * P - META:SEQ, :]).then_inc(S.x_in, 16)

            k = 0
            for stage in (mixer_loads(0),
                          ffn_loads(A["ffn_w_gate"][0], A["ffn_w_up"][0], A["ffn_w_down"][0]),
                          mixer_loads(1)):
                for src, width in stage:
                    s = slot_of[k]
                    if prior[k] is not None:
                        sp.wait_ge(S.pieces_used, prior[k] + 1)
                    if MIXN <= k < MIXN + FFNN and SMALL_RING <= s:
                        sp.wait_ge(S.h_ready, 2 * DC)
                    dst = slot(s)[:, 0:width].rearrange("p (c n) -> p c n", c=src.shape[1])
                    sp.dma_start(dst, src).then_inc(loaded[s], 16)
                    k += 1

            def item_loads(i, expert):
                pieces = ffn_loads(*(A[n][0, expert] for n in ("moe_w_gate", "moe_w_up", "moe_w_down")))
                for j, (src, width) in enumerate(pieces):
                    sp.wait_ge(S.pieces_used, i * FFNN + (STATIC + item_prior[j] + 1))
                    if j == SMALL_RING:
                        sp.wait_ge(S.h_ready, 4 * DC)
                    dst = slot(j % BIG_RING).rearrange("p (c n) -> p c n", c=src.shape[1])
                    sp.dma_start(dst, src).then_inc(loaded[j % BIG_RING], 16)

            with sp.Fori(0, NE) as i:
                item_loads(i, i)
            sp.wait_ge(S.table_ready, 1)
            n_items = sp.value_load(ntab[0:1, 0:1], min_val=NE, max_val=NE + MAXO)
            with sp.If(n_items > NE):
                with sp.Fori(NE, n_items) as i:
                    expert = sp.value_load(tab[0:1, 0, bass.ds(i, 1)], min_val=0, max_val=NE - 1)
                    item_loads(i, expert)
            for i, (dst, rows) in enumerate(((out[0, 0:P - META, :], (META, P)),
                                             (out[0, P - META:2 * P - META, :], (0, P)),
                                             (out[0, 2 * P - META:SEQ, :], (0, META)))):
                sp.wait_ge(S.out_act, i + 1)
                sp.wait_ge(S.out_dve, i + 1)
                sp.dma_start(dst, xTok[rows[0]:rows[1], i, :]).then_inc(S.out_stored, 16)
            sp.wait_ge(S.out_stored, 48)

        @block.gpsimd
        def _(pool):
            done = [0]

            def step(ins):
                done[0] += 1
                ins.then_inc(S.pool_chain, 1)
                pool.wait_ge(S.pool_chain, done[0])

            for k, eps in enumerate((NORM_EPS, GN_EPS, SUB_EPS)):
                pool.memset(epsT[:, k:k + 1], eps).then_inc(S.eps_set, 1)

            for l in range(DEPTH):
                pool.wait_ge(S.h_ready, DC * (2 * l + 1))
                pool.memset(projT[:, :, 0:2], 0.0).then_inc(S.pads_zero, 1)
                pool.wait_ge(S.pads_zero, l + 1)
                pool.wait_ge(S.proj_act, 13 * l + 4)
                pool.wait_ge(S.proj_dve, 12 * l + 3)
                pool.tensor_tensor(sqT[:, 0:7, :], prev(RWKV_CH, 1, 7), cur(RWKV_CH, 7),
                                   ALU.subtract).then_inc(S.shift_d, 1)
                pool.wait_ge(S.proj_act, 13 * l + 13)
                pool.wait_ge(S.proj_dve, 12 * l + 12)
                step(pool.tensor_tensor(cur(CG_CH, 2), cur(CG_CH, 2), cur(U_CH, 2), ALU.mult))
                for j in range(3):
                    for c in range(2):
                        ins = pool.tensor_scalar((cvT if j else oT[:, 6:8, :])[:, c, :], prev(CG_CH + c, 2 - j)[:, 0, :],
                                                 vc(l, CONV + 2 * j + c), None, ALU.mult)
                        if c == 1:
                            step(ins)
                    if j:
                        step(pool.tensor_tensor(oT[:, 6:8, :], oT[:, 6:8, :], cvT, ALU.add))
                pool.tensor_tensor(oT[:, 6:8, :], oT[:, 6:8, :], cur(BG_CH, 2), ALU.mult).then_inc(S.oc_ready, 1)
                for c in range(2):
                    pool.wait_ge(S.qg_ready, 8 * l + 4 * c + 4)
                    pool.tensor_tensor(cur(Q_CH + 4 * c, 4), hnT[:, 4 * c:4 * c + 4, :], bc(cosT, 4),
                                       ALU.mult).then_inc(S.qcos_ready, 1)

        @block.scalar
        def _(act):
            n_par = 0
            for l in range(DEPTH):
                b = l * ROWS

                def chunks(v):
                    return v.rearrange("(c p) -> c p", p=P)

                for off, n, src in (
                    (MIXG, 8, chunks(A["mix_norm_g"][l])), (FFNG, 8, chunks(A["ffn_norm_g"][l])),
                    (MU, 7, chunks(A["tm_mu"][l])), (W0, 2, chunks(A["tm_w0"][l])), (A0, 2, chunks(A["tm_a0"][l])),
                    (KK, 2, chunks(A["tm_k_k"][l])), (KA, 2, chunks(A["tm_k_a"][l])),
                    (RK, 2, A["tm_r_k"][l].rearrange("(c a) n -> c (a n)", a=2)),
                    (GNG, 2, chunks(A["tm_gn_g"][l])), (GNB, 2, chunks(A["tm_gn_b"][l])),
                    (SUBG, 1, chunks(A["da_subln_g"][l])),
                    (CONV, 6, A["sc_conv_w"][l].rearrange("j (c p) -> (j c) p", p=P)),
                ):
                    act.dma_start(vrow[b + off:b + off + n, :], src).then_inc(S.params_in, 16)
                    n_par += 1
                for row, half, name in ((QG, 0, "da_q_norm_g"), (QG, 1, "da_q_norm_g"), (KG, 0, "da_k_norm_g"),
                                        (KG, 1, "da_k_norm_g"), (LAMQ, 0, "da_lambda_q1"), (LAMQ, 1, "da_lambda_q2"),
                                        (LAMK, 0, "da_lambda_k1"), (LAMK, 1, "da_lambda_k2")):
                    act.dma_start(vrow[b + row:b + row + 1, 64 * half:64 * half + 64],
                                  A[name][l:l + 1, :]).then_inc(S.params_in, 16)
                    n_par += 1
            assert n_par == N_PARAMS
            act.wait_ge(S.eps_set, 3)
            act.wait_ge(S.lam_mm, 2)
            act.activation(small[:, 2:4], ps[:, 0, 0:2], ACT.Exp).then_inc(S.lam_exp, 1)
            act.activation(small[:, 4:6], ps[:, 1, 0:2], ACT.Exp).then_inc(S.lam_exp, 1)

            def squares(idx):
                for k in range(2):
                    act.wait_ge(S.h_ready, DC * idx + 4 * (k + 1))
                    act.activation(sqT[:, 4 * k:4 * k + 4, :], hT[:, 4 * k:4 * k + 4, :],
                                   ACT.Square).then_inc(S.sq_ready, 1)

            def root(banks, n, scale, eps):
                act.activation(msT[:, 0:n * T].rearrange("p (c t) -> p c t", c=n), ps[:, banks:banks + n, 0:T],
                               ACT.Sqrt, scale=scale, bias=epsT[:, eps:eps + 1]).then_inc(S.root_ready, 1)

            def norm_root(idx):
                act.wait_ge(S.nsum_mm, idx + 1)
                root(7, 1, 1.0 / D, 0)

            def rwkv_lora(l):
                act.wait_ge(S.hx_ready, 7 * l + 1)
                act.activation(lora[0:32, :], hxT[0:32, 6, :], ACT.Tanh).then_inc(S.lora_act, 1)
                act.activation(lora[64:128, :], hxT[64:128, 6, :], ACT.Tanh, scale=0.5).then_inc(S.lora_act, 1)
                act.activation(lora[32:64, :], hxT[32:64, 6, :], ACT.Copy).then_inc(S.lora_act, 1)

            def rwkv_lora_out(l):
                act.wait_ge(S.vhalf_ready, DEPTH)
                for k, dst in ((0, eT), (1, aT)):
                    act.wait_ge(S.lora_mm, 3 * l + k + 1)
                    for p in range(2):
                        act.activation(dst[:, p, :], ps[:, 2 + 2 * k + p, 0:T], ACT.Tanh, scale=0.5,
                                       bias=vhalf[:, l, 2 * k + p:2 * k + p + 1]).then_inc(S.lora_out, 1)
                act.wait_ge(S.lora_mm, 3 * l + 3)
                act.activation(gT, ps[:, 6:8, 0:T], ACT.Copy).then_inc(S.lora_out, 1)

            def rwkv_exp(l):
                act.wait_ge(S.decay_ready, l + 1)
                act.activation(PtT, cumT, ACT.Exp, scale=-1.0).then_inc(S.exp_ready, 1)
                act.activation(AtT, AtT, ACT.Exp, scale=-1.0).then_inc(S.exp_ready, 1)
                act.activation(KtT, cumT, ACT.Exp).then_inc(S.exp_ready, 1)
                act.activation(KhT[:, :, 0:256], KhT[:, :, 0:256], ACT.Exp).then_inc(S.exp_ready, 1)

            def rwkv_tok(l):
                k = 0
                for i, (t0, n) in enumerate(TILES):
                    for bank, dst in ((2, tokAV), (3, tokBK))[:2 if i < 2 else 1]:
                        k += 1
                        act.wait_ge(S.tok_mm, 5 * l + k)
                        act.activation(dst[0:n, i], ps[0:n, bank, :].rearrange("p (a b) -> p a b", a=2),
                                       ACT.Copy).then_inc(S.tok_ready, 1)

            def rwkv_levels(l, i):
                t0, n = TILES[i]
                g = 3 * l + i
                at = lvl(LVM, l, i)

                def copy(dst, bank, need):
                    act.wait_ge(S.lvl_mm, at + need)
                    act.activation(dst[0:n, :, 0:n], ps[0:n, bank, :].rearrange("p (h t) -> p h t", h=4)[:, :, 0:n],
                                   ACT.Copy).then_inc(S.lvl_act, 1)

                copy(mt2, 4, 1)
                copy(m2, 5, 2)
                act.wait_ge(S.q1_ready, g + 1)
                copy(mt16, 4, 4)
                copy(m16, 5, 5)
                copy(m2, 5, 7)
                if i < 2:
                    copy(mt2, 4, 9)
                act.wait_ge(S.wt_mm, 3 * g + 1)
                act.activation(wT[:, :, t0:t0 + n], ps[:, 4, 0:256].rearrange("p (a t) -> p a t", a=2)[:, :, 0:n],
                               ACT.Copy).then_inc(S.wt_act, 1)
                act.wait_ge(S.wt_mm, 3 * g + 3)
                act.activation(zTok[0:n, i], ps[0:n, 6, 0:256], ACT.Copy).then_inc(S.wt_act, 1)

            def group_norm(l):
                act.wait_ge(S.y_mm, l + 1)
                act.activation(eT[0:64], ps[0:64, 4:8:2, 0:T], ACT.Copy).then_inc(S.y_sb, 1)
                act.activation(eT[64:128], ps[64:128, 5:8:2, 0:T], ACT.Copy).then_inc(S.y_sb, 1)
                act.wait_ge(S.gn_cent, l + 1)
                act.activation(cumT, eT, ACT.Square).then_inc(S.gn_sq, 1)
                act.wait_ge(S.gn_mm, 2 * l + 2)
                root(2, 2, 1.0 / NR, 1)

            def attention(l):
                for k in range(2):
                    act.activation(sqT[:, 4 * k:4 * k + 4, :], cur(Q_CH + 4 * k, 4), ACT.Square).then_inc(S.qk_sq, 1)
                for k, g in ((0, QG), (1, KG)):
                    for c in range(4):
                        act.activation(hnT[:, 4 * k + c, :], cur(Q_CH + 4 * k + c)[:, 0, :], ACT.Copy,
                                       scale=vc(l, g)).then_inc(S.qg_ready, 1)
                for i, (t0, n) in enumerate(TILES):
                    act.wait_ge(S.vt_mm, 3 * l + i + 1)
                    act.activation(vTok[0:n, i], ps[0:n, 6, :], ACT.Copy).then_inc(S.vt_ready, 1)
                for k in range(2):
                    act.wait_ge(S.qk_mm, 2 * l + k + 1)
                    act.wait_ge(S.rs_ready, NORMS * l + 3 + k)
                    root(4 * k, 4, 1.0 / DK, 0)
                for u in range(12):
                    h, i = u // 3, u % 3
                    t0, n = TILES[i]
                    b, m = u % 2, t0 + n
                    act.wait_ge(S.mx_ready, 12 * l + u + 1)
                    for c in range(2):
                        act.activation(prob[0:n, b, c, 0:m], ps[0:n, 2 * b + c, 0:m], ACT.Exp, scale=DK ** -0.5,
                                       bias=stat[0:n, b, c:c + 1],
                                       accum_out=stat[0:n, b, 2 + c:3 + c]).then_inc(S.p_ready, 1)
                    if i == 0 and h:
                        output(l, h - 1)
                output(l, 3)
                act.wait_ge(S.ob_mm, l + 1)
                root(0, 4, 1.0 / P, 2)

            def output(l, h):
                act.wait_ge(S.o_mm, 4 * l + h + 1)
                act.activation(oat[:, h, :], ps[:, 7, 0:T], ACT.Copy).then_inc(S.o_sb, 1)
                act.wait_ge(S.o_sb, 4 * l + h + 1)
                act.activation(sqT[:, h, :], oat[:, h, :], ACT.Square).then_inc(S.osq_ready, 1)

            def silu(f, n, need):
                act.wait_ge(S.gu_mm, need)
                act.activation(sg[:, f % 2, 0:n], ps[:, f % 2, 0:n], ACT.Silu).then_inc(S.silu_ready, 1)

            for l in range(DEPTH):
                act.wait_ge(S.h_ready, DC * (2 * l + 1))
                act.dma_start(lora_w[0:32, :], A["tm_w_decay_up"][l]).then_inc(S.lora_w_in, 16)
                act.dma_start(lora_w[32:64, :], A["tm_w_a_up"][l]).then_inc(S.lora_w_in, 16)
                act.dma_start(lora_w[64:128, :], A["tm_w_g_up"][l]).then_inc(S.lora_w_in, 16)
                squares(2 * l)
                norm_root(2 * l)
                for n in range(0, NCH, 2):
                    act.wait_ge(S.proj_mm, NCH * l + n + 1)
                    act.activation(projT[:, n, 2:T + 2], ps[:, 0, 0:T], ACT.Copy).then_inc(S.proj_act, 1)
                    if n == 6:
                        rwkv_lora(l)
                    if n == 10:
                        rwkv_lora_out(l)
                    if n == 16:
                        rwkv_exp(l)
                        act.wait_ge(S.kk_max, l + 1)
                        act.activation(msT[:, 0:2 * T], msT[:, 0:2 * T], ACT.Sqrt).then_inc(S.root_ready, 1)
                rwkv_tok(l)
                for i in range(3):
                    rwkv_levels(l, i)
                group_norm(l)
                attention(l)
                squares(2 * l + 1)
                norm_root(2 * l + 1)
                if l == 0:
                    for f in range(FC):
                        silu(f, T, f + 1)

            act.wait_ge(S.hn_ready, 4 * DC)
            act.dma_start(router, A["router_w"][0].rearrange("(c p) e -> p c e", p=P)).then_inc(S.router_in, 16)
            for k in range(0, 6, 2):
                act.wait_ge(S.hntok_mm, k + 1)
                i, half = k // 2, k % 2
                n = TILES[i][1]
                act.activation(hnTok[0:n, i, 0:512], ps[0:n, 2, :], ACT.Copy).then_inc(S.hntok_ready, 1)
                act.wait_ge(S.hntok_mm, k + 2)
                act.activation(hnTok[0:n, i, 512:1024], ps[0:n, 3, :], ACT.Copy).then_inc(S.hntok_ready, 1)
            act.wait_ge(S.gap_ready, 1)
            act.activation(gw[:, :, 1], gw[:, :, 1], ACT.Exp).then_inc(S.gap_exp, 1)
            act.wait_ge(S.table_ready, 1)
            n_items = act.value_load(ntab[0:1, 0:1], min_val=NE, max_val=NE + MAXO)
            with act.Fori(0, n_items) as i:
                act.wait_ge(S.gather_mm, 2 * i + 1)
                act.activation(xe[:, 0:4, :], ps[:, 6, 0:4 * CAP].rearrange("p (c t) -> p c t", c=4),
                               ACT.Copy).then_inc(S.xe_act, 1)
                act.wait_ge(S.gt_mm, i + 1)
                act.activation(gateT[0:CAP, :], ps[0:CAP, 4, 0:T], ACT.Copy).then_inc(S.gt_ready, 1)
                for f in range(FC):
                    silu(f, CAP, FC * i + (FC + f + 1))
                act.wait_ge(S.down_mm, 2 * i + DC + 1)
                act.activation(yE[0:CAP, 0:512], ps[0:CAP, 4, :], ACT.Copy).then_inc(S.y_act, 1)
            for i, (t0, n) in enumerate(TILES):
                act.wait_ge(S.out_mm, 2 * i + 1)
                act.activation(xTok[0:n, i, 0:512], ps[0:n, 2 * (i % 2), :], ACT.Copy).then_inc(S.out_act, 1)

        @block.vector
        def _(dve):
            done = [0]

            def step(ins):
                done[0] += 1
                ins.then_inc(S.dve_chain, 1)
                dve.wait_ge(S.dve_chain, done[0])

            def inverse(k, n):
                dve.wait_ge(S.root_ready, k)
                dve.reciprocal(rsT[:, 0:n * T], msT[:, 0:n * T]).then_inc(S.rs_ready, 1)
                dve.wait_ge(S.rs_ready, k)

            def rs(n):
                return rsT[:, 0:n * T].rearrange("p (c t) -> p c t", c=n)

            def norm(idx, g):
                l = idx // 2
                inverse(NORMS * l + (1 if idx % 2 == 0 else 7), 1)
                for c in range(DC):
                    dve.scalar_tensor_tensor(out=hnT[:, c, :], in0=hT[:, c, :], scalar=vc(l, g + c), in1=rsT[:, 0:T],
                                             op0=ALU.mult, op1=ALU.mult).then_inc(S.hn_ready, 1)

            def hx(l, c):
                dve.scalar_tensor_tensor(out=hxT[:, c, :], in0=sqT[:, c, :], scalar=vc(l, MU + c),
                                         in1=cur(c)[:, 0, :], op0=ALU.mult, op1=ALU.add).then_inc(S.hx_ready, 1)

            R, K, V = hxT[:, 0:2, :], hxT[:, 2:4, :], hxT[:, 4:6, :]

            def prep(l, n):
                if n == 5:
                    dve.wait_ge(S.shift_d, l + 1)
                    hx(l, 6)
                if n == 7:
                    hx(l, 2)
                    hx(l, 3)
                    dve.wait_ge(S.lora_act, 3 * l + 2)
                    dve.tensor_scalar(lora[64:128, :], lora[64:128, :], 0.5, 0.5, ALU.mult,
                                      ALU.add).then_inc(S.lora_sig, 1)
                if n == 9:
                    for c in (0, 1, 4, 5):
                        hx(l, c)
                if n == 11:
                    dve.wait_ge(S.lora_out, 5 * l + 4)
                    step(dve.tensor_scalar(eT, eT, 0.5 * E_HALF, 0.5 * E_HALF, ALU.mult, ALU.add))
                    step(dve.tensor_scalar(aT, aT, 0.5, 0.5, ALU.mult, ALU.add))
                    for p in range(2):
                        step(dve.tensor_tensor_scan(cumT[:, p, :], resetT, eT[:, p, :], 0.0, ALU.mult, ALU.add))
                if n == 13:
                    dve.tensor_tensor(AtT, cumT, eT, ALU.subtract)
                    for p in range(2):
                        c32 = cumT[:, p, 0:256].rearrange("p (c t) -> p c t", t=CH)
                        ins = dve.tensor_tensor(KhT[:, p, 0:256].rearrange("p (c t) -> p c t", t=CH), c32,
                                                c32[:, :, CH - 1:CH].broadcast_to([P, 8, CH]), ALU.subtract)
                    ins.then_inc(S.decay_ready, 1)
                    dve.wait_ge(S.hx_ready, 7 * l + 7)
                    for p in range(2):
                        step(dve.tensor_scalar(kkT[:, p, :], K[:, p, :], vc(l, KK + p), None, ALU.mult))
                    dve.tensor_tensor(kks, kkT, kkT, ALU.mult).then_inc(S.kk_sq, 1)
                if n == 15:
                    for p in range(2):
                        step(dve.tensor_scalar(bT[:, p, :], aT[:, p, :], -1.0, vc(l, KA + p), ALU.add, ALU.mult))
                    step(dve.scalar_tensor_tensor(out=K, in0=bT, scalar=1.0, in1=K, op0=ALU.add, op1=ALU.mult))
                    dve.wait_ge(S.kk_mm, l + 1)
                    dve.tensor_scalar(msT[:, 0:2 * T].rearrange("p (c t) -> p c t", c=2), ps[:, 2:4, 0:T], 1e-24, None,
                                      ALU.max).then_inc(S.kk_max, 1)
                if n == 17:
                    for p in range(2):
                        ins = dve.scalar_tensor_tensor(out=bonusT[:, p, :], in0=R[:, p, :], scalar=vc(l, RK + p),
                                                       in1=K[:, p, :], op0=ALU.mult, op1=ALU.mult)
                    ins.then_inc(S.bonus_pre, 1)
                    inverse(NORMS * l + 2, 2)
                    step(dve.tensor_tensor(kkT, kkT, rs(2), ALU.mult))
                    step(dve.tensor_tensor(bT, kkT, aT, ALU.mult))
                if n == 19:
                    dve.wait_ge(S.exp_ready, 4 * l + 4)
                    dve.scalar_tensor_tensor(out=AtT, in0=kkT, scalar=-1.0, in1=AtT, op0=ALU.mult,
                                             op1=ALU.mult).then_inc(S.til_ready, 1)
                    dve.tensor_tensor(BtT, bT, KtT, ALU.mult).then_inc(S.til_ready, 1)
                    dve.tensor_tensor(RtT, R, PtT, ALU.mult).then_inc(S.til_ready, 1)
                if n == 21:
                    dve.wait_ge(S.til_ready, 6 * l + 2)
                    dve.tensor_tensor(KtT, K, KtT, ALU.mult).then_inc(S.til_ready, 1)
                    dve.wait_ge(S.bonus_mm, l + 1)
                    dve.tensor_tensor(bonusT, ps[:, 4:6, 0:T], V, ALU.mult)
                if n == 23:
                    dve.tensor_tensor(bT[:, :, 0:256], bT[:, :, 0:256], KhT[:, :, 0:256],
                                      ALU.mult).then_inc(S.til_ready, 1)
                    dve.tensor_tensor(KhT[:, :, 0:256], K[:, :, 0:256], KhT[:, :, 0:256],
                                      ALU.mult).then_inc(S.til_ready, 1)

            def quad(bank, n):
                return ps[0:n, bank, :].rearrange("p (h t) -> p h t", h=4)[:, :, 0:n]

            def masked(dst, bank, mask, n):
                for q in range(2):
                    ins = dve.tensor_tensor(dst[0:n, q::2, 0:n],
                                            ps[0:n, bank + q, 0:256].rearrange("p (a t) -> p a t", a=2)[:, :, 0:n],
                                            bc(mask[0:n, 0:n], 2), ALU.mult)
                ins.then_inc(S.mat_ev, 1)

            def matrices(l, i):
                n = TILES[i][1]
                g = 3 * l + i
                at = 5 * g
                dve.wait_ge(S.mat_mm, at + 1)
                masked(mt16, 2, C.m16t, n)
                dve.wait_ge(S.mat_mm, at + 2)
                masked(m16, 4, C.m16, n)
                masked(moff, 4, C.moff, n)
                dve.wait_ge(S.mat_ev, 6 * g + 1)
                dve.tensor_tensor(qm[0:n, :, 0:n], mt16[0:n, :, 0:n], bc(C.ident[0:n, 0:n], 4),
                                  ALU.add).then_inc(S.q1_ready, 1)
                dve.wait_ge(S.mat_mm, at + 3)
                masked(ntm, 6, C.m32s, n)
                dve.wait_ge(S.mat_mm, at + 4)
                masked(rbm[i], 2, C.m32i, n)
                dve.wait_ge(S.mat_mm, at + 5)
                masked(rkm[i], 2, C.m32i, n)
                lm, ld = lvl(LVM, l, i), lvl(LVD, l, i)

                def add_to_q(need, have):
                    dve.wait_ge(S.lvl_mm, lm + need)
                    if have:
                        dve.wait_ge(S.lvl_dve, ld + have)
                    dve.tensor_tensor(qm[0:n, :, 0:n], quad(6, n), qm[0:n, :, 0:n], ALU.add).then_inc(S.lvl_dve, 1)

                add_to_q(3, 0)
                add_to_q(6, 1)
                add_to_q(8, 2)
                if i < 2:
                    dve.wait_ge(S.lvl_mm, lm + 10)
                    dve.tensor_copy(m16[0:n, :, 0:n], quad(5, n)).then_inc(S.lvl_dve, 1)
                    add_to_q(11, 3)
                dve.wait_ge(S.wt_mm, 3 * g + 2)
                dve.tensor_copy(nv[0:n, :], ps[0:n, 5, 0:256]).then_inc(S.nv_ready, 1)

            def chain(l):
                dve.wait_ge(S.wt_act, 6 * l + 6)
                for c in range(NCHUNK):
                    i, r, n = c // 4, CH * (c % 4), min(CH, T - CH * c)
                    if c == 0:
                        dve.tensor_copy(uTok[0:n, 0, :], zTok[0:n, 0, :]).then_inc(S.u_ready, 1)
                    else:
                        dve.wait_ge(S.u_mm, 8 * l + c)
                        for q in range(2):
                            u, z = (x[r:r + n, i, :].rearrange("p (a q v) -> p q a v", q=2, v=NR)[:, q]
                                    for x in (uTok, zTok))
                            ins = dve.tensor_tensor(u, ps[r:r + n, 2 + q, 0:128].rearrange("p (a v) -> p a v", a=2), z,
                                                    ALU.add)
                        ins.then_inc(S.u_ready, 1)
                    if c == NCHUNK - 1:
                        break
                    new = ps[:, 0, 0:2 * NR].rearrange("p (a v) -> p a v", a=2)
                    if c == 0:
                        dve.wait_ge(S.st_mm, 8 * l + 1)
                        dve.tensor_copy(stT[:, 1], new).then_inc(S.st_ready, 1)
                    else:
                        step(dve.tensor_tensor(pst, stT[:, c], tail(PtT[:, :, CH * c + CH - 1], NR), ALU.mult))
                        dve.wait_ge(S.st_mm, 8 * l + c + 1)
                        dve.tensor_tensor(stT[:, c + 1], new, pst, ALU.add).then_inc(S.st_ready, 1)
                    dve.wait_ge(S.st_ready, 8 * l + c + 1)

            def group_norm(l):
                dve.wait_ge(S.gn_mm, 2 * l + 1)
                dve.scalar_tensor_tensor(out=eT, in0=ps[:, 0:2, 0:T], scalar=-1.0 / NR, in1=eT, op0=ALU.mult,
                                         op1=ALU.add).then_inc(S.gn_cent, 1)
                inverse(NORMS * l + 3, 2)
                step(dve.tensor_tensor(eT, eT, rs(2), ALU.mult))
                for p in range(2):
                    step(dve.tensor_scalar(eT[:, p, :], eT[:, p, :], vc(l, GNG + p), vc(l, GNB + p), ALU.mult, ALU.add))
                step(dve.tensor_tensor(eT, eT, bonusT, ALU.add))
                dve.tensor_tensor(oT[:, 0:2, :], eT, gT, ALU.mult).then_inc(S.oa_ready, 1)

            def qk_norm_rope(l):
                for k in range(2):
                    x = cur(Q_CH + 4 * k, 4)
                    y = hnT[:, 4 * k:4 * k + 4, :]
                    dve.wait_ge(S.rot_mm, 2 * l + k + 1)
                    dve.wait_ge(S.qcos_ready, 2 * l + k + 1)
                    step(dve.tensor_tensor(y, ps[:, 4 * k:4 * k + 4, 0:T], bc(sinT, 4), ALU.mult))
                    step(dve.tensor_tensor(x, x, y, ALU.add))
                    inverse(NORMS * l + 4 + k, 4)
                    dve.tensor_tensor(x, x, rs(4), ALU.mult).then_inc(S.qk_ready, 1)

            def softmax(l):
                def maxima(u):
                    i = u % 3
                    t0, n = TILES[i]
                    b, m = u % 2, t0 + n
                    dve.wait_ge(S.sc_mm, 12 * l + u + 1)
                    step(dve.tensor_reduce(stat[0:n, b, 4:6], ps[0:n, 2 * b:2 * b + 2, 0:m], AXX, ALU.max))
                    dve.tensor_scalar(stat[0:n, b, 0:2], stat[0:n, b, 4:6], -DK ** -0.5, None,
                                      ALU.mult).then_inc(S.mx_ready, 1)

                def difference(u):
                    i = u % 3
                    t0, n = TILES[i]
                    b, m = u % 2, t0 + n
                    dve.wait_ge(S.p_ready, 24 * l + 2 * u + 2)
                    step(dve.reciprocal(stat[0:n, b, 2:4], stat[0:n, b, 2:4]))
                    step(dve.tensor_scalar(stat[0:n, b, 3:4], stat[0:n, b, 3:4], small[0:n, 6 + l:7 + l], None, ALU.mult))
                    step(dve.tensor_scalar(scaled[0:n, 0:m], prob[0:n, b, 1, 0:m], stat[0:n, b, 3:4], None, ALU.mult))
                    if u >= 2:
                        dve.wait_ge(S.pt_mm, 12 * l + u - 1)
                    dve.scalar_tensor_tensor(out=pd[0:n, b, 0:m], in0=prob[0:n, b, 0, 0:m], scalar=stat[0:n, b, 2:3],
                                             in1=scaled[0:n, 0:m], op0=ALU.mult,
                                             op1=ALU.subtract).then_inc(S.pd_ready, 1)

                def turned(u):
                    h, i = u // 3, u % 3
                    t0, n = TILES[i]
                    dve.wait_ge(S.pt_mm, 12 * l + u + 1)
                    if i == 0 and h >= 2:
                        dve.wait_ge(S.o_mm, 4 * l + h - 1)
                    w = min(i + 1, 2)
                    ins = dve.tensor_copy(pT[:, h % 2, 0:w, t0:t0 + n],
                                          ps[:, 6, :].rearrange("p (k t) -> p k t", t=P)[:, 0:w, 0:n])
                    if i == 2:
                        ins = dve.tensor_copy(pT[0:n, h % 2, 2, t0:t0 + n], ps[0:n, 6, 2 * P:2 * P + n])
                    ins.then_inc(S.pt_ready, 1)

                for u in range(14):
                    if u < 12:
                        maxima(u)
                    if 1 <= u < 13:
                        difference(u - 1)
                    if u >= 2:
                        turned(u - 2)
                inverse(NORMS * l + 6, 4)
                dve.scalar_tensor_tensor(out=oT[:, 2:6, :], in0=oat, scalar=small[:, 8 + l:9 + l], in1=rs(4),
                                         op0=ALU.mult, op1=ALU.mult).then_inc(S.ob_ready, 1)

            def hidden(f, n, need):
                dve.wait_ge(S.silu_ready, need)
                dve.tensor_tensor(hid[:, f, 0:n], ps[:, 2 + f % 2, 0:n], sg[:, f % 2, 0:n],
                                  ALU.mult).then_inc(S.hid_ready, 1)

            for c in range(DC):
                dve.wait_ge(S.x_mm, c + 1)
                dve.tensor_copy(hT[:, c, :], ps[:, c % 2, 0:T]).then_inc(S.h_ready, 1)
            dve.wait_ge(S.vcol_mm, 1)
            dve.tensor_copy(vcol[:], ps[:, 2, 0:DEPTH * ROWS]).then_inc(S.vcol_ready, 1)
            dve.wait_ge(S.vcol_ready, 1)
            for l in range(DEPTH):
                dve.tensor_scalar(vhalf[:, l, :], vc(l, W0, 4), 0.5, None, ALU.mult).then_inc(S.vhalf_ready, 1)
                dve.tensor_scalar(small[:, 8 + l:9 + l], vc(l, SUBG), 1.0 - LAM_INIT[l], None, ALU.mult)
                dve.tensor_tensor(small[:, l:l + 1], vc(l, LAMQ), vc(l, LAMK), ALU.mult).then_inc(S.lam_prod, 1)
            dve.wait_ge(S.lam_exp, 2)
            step(dve.tensor_tensor(small[:, 6:8], small[:, 2:4], small[:, 4:6], ALU.subtract))
            for l in range(DEPTH):
                step(dve.tensor_scalar(small[:, 6 + l:7 + l], small[:, 6 + l:7 + l], LAM_INIT[l], None, ALU.add))

            for l in range(DEPTH):
                norm(2 * l, MIXG)
                for n in range(1, NCH, 2):
                    dve.wait_ge(S.proj_mm, NCH * l + n + 1)
                    dve.tensor_copy(projT[:, n, 2:T + 2], ps[:, 1, 0:T]).then_inc(S.proj_dve, 1)
                    prep(l, n)
                for i in range(3):
                    matrices(l, i)
                chain(l)
                group_norm(l)
                qk_norm_rope(l)
                softmax(l)
                for c in range(DC):
                    dve.wait_ge(S.wout_mm, DC * l + c + 1)
                    dve.tensor_tensor(hT[:, c, :], ps[:, c % 2, 0:T], hT[:, c, :], ALU.add).then_inc(S.h_ready, 1)
                norm(2 * l + 1, FFNG)
                if l == 0:
                    for f in range(FC):
                        hidden(f, T, f + 1)
                    for c in range(DC):
                        dve.wait_ge(S.down_mm, c + 1)
                        dve.tensor_tensor(hT[:, c, :], ps[:, c, 0:T], hT[:, c, :], ALU.add).then_inc(S.h_ready, 1)

            step(dve.memset(lgS, 0.0))
            dve.wait_ge(S.lg_mm, 1)
            step(dve.tensor_copy(lgS[:, 0:2, :], ps[:, 0, 0:2 * NE].rearrange("p (i e) -> p i e", e=NE)))
            step(dve.tensor_copy(lgS[0:META, 2, :], ps[0:META, 0, 2 * NE:3 * NE]))
            for i in range(3):
                step(dve.max(top8[:, i, :], lgS[:, i, :]))
                step(dve.max_index(idx8[:, i, :], top8[:, i, :], lgS[:, i, :]))
            dve.tensor_tensor(gw[:, :, 1], top8[:, :, 1], top8[:, :, 0], ALU.subtract).then_inc(S.gap_ready, 1)
            step(dve.tensor_copy(fidx, idx8[:, :, 0:2]))
            for j, oh in ((0, oh1), (1, oh2)):
                step(dve.tensor_tensor(oh, bc(iotaT[:, 0:NE], 3), tail(fidx[:, :, j], NE), ALU.is_equal))
            dve.tensor_tensor(sel, oh1, oh2, ALU.add).then_inc(S.sel_ready, 1)
            dve.wait_ge(S.gap_exp, 1)
            step(dve.tensor_scalar(gw[:, :, 0], gw[:, :, 1], 1.0, None, ALU.add))
            step(dve.reciprocal(gw[:, :, 0], gw[:, :, 0]))
            step(dve.tensor_tensor(gw[:, :, 1], gw[:, :, 1], gw[:, :, 0], ALU.mult))
            for j, oh in ((0, oh1), (1, oh2)):
                step(dve.tensor_tensor(oh, oh, tail(gw[:, :, j], NE), ALU.mult))
            step(dve.tensor_tensor(gates, oh1, oh2, ALU.add))
            dve.wait_ge(S.pos_mm, 1)
            step(dve.memset(posx, 0.0))
            step(dve.tensor_copy(posx[:, 0:2, :], ps[:, 1, 0:2 * NE].rearrange("p (i e) -> p i e", e=NE)))
            step(dve.tensor_copy(posx[0:META, 2, :], ps[0:META, 1, 2 * NE:3 * NE]))
            step(dve.scalar_tensor_tensor(out=posx, in0=posx, scalar=1.0, in1=sel, op0=ALU.add, op1=ALU.mult))
            step(dve.tensor_scalar(posx, posx, -1.0, None, ALU.add))
            step(dve.tensor_copy(cnt[0:1, 0:NE], ps[0:1, 1, 3 * NE:4 * NE]))
            for r in range(NFLAG // NE):
                step(dve.tensor_scalar(flag[0:1, NE * r:NE * r + NE], cnt[0:1, 0:NE], float(CAP * (r + 1)), None,
                                       ALU.is_gt))
                step(dve.tensor_copy(ev[0:1, NE * r:NE * r + NE], iotaT[0:1, 0:NE]))
                step(dve.memset(ov[0:1, NE * r:NE * r + NE], float(CAP * (r + 1))))
            step(dve.tensor_tensor_scan(incl[0:1, :], C.ones[0:1, 0:NFLAG], flag[0:1, :], 0.0, ALU.mult, ALU.add))
            step(dve.memset(fsum[:], 0.0))
            step(dve.tensor_scalar(fsum[0:1, 1, NIT - 1:NIT], incl[0:1, NFLAG - 1:NFLAG], float(NE), None, ALU.add))
            step(dve.tensor_copy(ntab[:], fsum[0:1, 1, NIT - 1:NIT]))
            step(dve.memset(fsum[0:1, 1, NIT - 1:NIT], 0.0))
            step(dve.tensor_tensor(incl[0:1, :], incl[0:1, :], flag[0:1, :], ALU.mult))
            step(dve.tensor_tensor(eqg[0:1], bc(incl[0:1, :], MAXO), tail(iotaT[0:1, 1:1 + MAXO], NFLAG), ALU.is_equal))
            step(dve.tensor_copy(fsum[0:1, 0, 0:NE], iotaT[0:1, 0:NE]))
            for row, values in ((0, ev), (1, ov)):
                step(dve.tensor_tensor(pick[0:1], eqg[0:1], bc(values[0:1, :], MAXO), ALU.mult))
                step(dve.tensor_reduce(fsum[0:1, row, NE:NE + MAXO], pick[0:1], AXX, ALU.add))
            dve.tensor_copy(tab[:], fsum[:]).then_inc(S.table_ready, 1)
            dve.wait_ge(S.table_ready, 1)

            def one_hot(k):
                e = dve.value_load(tab[0:1, 0, bass.ds(k, 1)], min_val=0, max_val=NE - 1)
                first = dve.value_load(tab[0:1, 1, bass.ds(k, 1)], min_val=0, max_val=wide - CAP)
                for i, (t0, n) in enumerate(TILES):
                    slots = iotaT[0:n, bass.ds(first, CAP)]
                    place = posx[0:n, i, bass.ds(e, 1)]
                    dve.tensor_scalar(oneh[0:n, i, :], slots, place, None, ALU.is_equal)
                    ins = dve.tensor_scalar(gateh[0:n, i, :], slots, place, gates[0:n, i, bass.ds(e, 1)],
                                            ALU.is_equal, ALU.mult)
                ins.then_inc(S.oneh_ready, 1)

            one_hot(0)
            n_items = dve.value_load(ntab[0:1, 0:1], min_val=NE, max_val=NE + MAXO)
            with dve.Fori(0, n_items) as i:
                dve.wait_ge(S.gather_mm, 2 * i + 2)
                dve.tensor_copy(xe[:, 4:8, :], ps[:, 7, 0:4 * CAP].rearrange("p (c t) -> p c t", c=4)
                                ).then_inc(S.xe_dve, 1)
                dve.wait_ge(S.gt_mm, i + 1)
                one_hot(i + 1)
                for f in range(FC):
                    hidden(f, CAP, FC * i + (FC + f + 1))
                dve.wait_ge(S.down_mm, 2 * i + DC + 2)
                dve.tensor_copy(yE[0:CAP, 512:1024], ps[0:CAP, 5, :]).then_inc(S.y_dve, 1)
                for c in range(DC):
                    dve.wait_ge(S.scat_mm, DC * i + (c + 1))
                    dve.tensor_tensor(hT[:, c, :], ps[:, 6 + c % 2, 0:T], hT[:, c, :], ALU.add).then_inc(S.h_item, 1)
            for i, (t0, n) in enumerate(TILES):
                dve.wait_ge(S.out_mm, 2 * i + 2)
                dve.tensor_copy(xTok[0:n, i, 512:1024], ps[0:n, 2 * (i % 2) + 1, :]).then_inc(S.out_dve, 1)

        @block.tensor
        def _(pe):
            mm = pe.matmul
            used_pieces = [0]

            def group(out, pairs, start=True, stop=True, **kw):
                pairs = list(pairs)
                for k, (a, b) in enumerate(pairs):
                    ins = mm(out, a, b, start=start and k == 0, stop=stop and k == len(pairs) - 1, **kw)
                return ins

            def piece_view(k, n):
                return slot(slot_of[k])[:, 0:DC * n].rearrange("p (c n) -> p c n", c=DC)

            def norm_sum(idx):
                for c in range(DC):
                    if c % 4 == 0:
                        pe.wait_ge(S.sq_ready, 2 * idx + c // 4 + 1)
                    ins = mm(ps[:, 7, 0:T], C.ones, sqT[:, c, :], start=c == 0, stop=c == DC - 1)
                ins.then_inc(S.nsum_mm, 1)

            def project(l, n):
                k = (MIXN + FFNN) * l + n // 2
                width = min(PIECE, IN_COLS - PIECE * (n // 2))
                w = piece_view(k, width)
                if n % 2 == 0:
                    pe.wait_ge(loaded[slot_of[k]], 16 * load_value[k])
                    if n:
                        pe.wait_ge(S.proj_act, 13 * l + n // 2)
                elif n > 1:
                    pe.wait_ge(S.proj_dve, 12 * l + n // 2)
                for c in range(DC):
                    if n == 0:
                        pe.wait_ge(S.hn_ready, 2 * DC * l + c + 1)
                    ins = mm(ps[:, n % 2, 0:T], w[:, c, P * (n % 2):P * (n % 2) + P], hnT[:, c, :],
                             start=c == 0, stop=c == DC - 1)
                ins.then_inc(S.proj_mm, 1)
                if n % 2 == 1 or n == NCH - 1:
                    pe.wait_ge(S.proj_mm, NCH * l + n + 1)
                    pe.sem_inc(S.pieces_used, 1)

            def rwkv_lora(l):
                pe.wait_ge(S.lora_w_in, 48 * (l + 1))
                pe.wait_ge(S.lora_act, 3 * l + 3)
                pe.wait_ge(S.lora_sig, l + 1)
                for k, (a, b) in enumerate(((0, 32), (32, 64), (64, 128))):
                    for p in range(2):
                        ins = mm(ps[:, 2 + 2 * k + p, 0:T], lora_w[a:b, P * p:P * p + P], lora[a:b, :],
                                 start=True, stop=True)
                    ins.then_inc(S.lora_mm, 1)

            def head_sums(bank, x, signal):
                for p in range(x.shape[1]):
                    ins = mm(ps[:, bank + p, 0:T], C.blk, x[:, p, :], start=True, stop=True)
                ins.then_inc(signal, 1)

            def token_rows(l):
                V = hxT[:, 4:6, :]
                k = 0
                for i, (t0, n) in enumerate(TILES):
                    for bank, (x, y) in ((2, (AtT, V)), (3, (bT, KhT)))[:2 if i < 2 else 1]:
                        if k == 0:
                            pe.wait_ge(S.til_ready, 6 * l + 6)
                        if i:
                            pe.wait_ge(S.tok_ready, 5 * l + k - 1)
                        for j, z in enumerate((x, y)):
                            for p in range(2):
                                ins = pe.transpose(ps[0:n, bank, 256 * j + P * p:256 * j + P * p + P],
                                                   z[:, p, t0:t0 + n], C.ident)
                        ins.then_inc(S.tok_mm, 1)
                        k += 1

            def matrices(l, i):
                t0, n = TILES[i]
                g = 3 * l + i
                lm, la, ld = lvl(LVM, l, i), lvl(LVA, l, i), lvl(LVD, l, i)

                def products(bank, x, y):
                    for p in range(2):
                        for q in range(2):
                            ins = mm(ps[0:n, bank + q, P * p:P * p + n], x[64 * q:64 * q + 64, p, t0:t0 + n],
                                     y[64 * q:64 * q + 64, p, t0:t0 + n], start=True, stop=True)
                    ins.then_inc(S.mat_mm, 1)

                def quad(bank, x, y):
                    for h in range(4):
                        ins = mm(ps[0:n, bank, P * h:P * h + n], x[0:n, h, 0:n], y[0:n, h, 0:n], start=True, stop=True)
                    ins.then_inc(S.lvl_mm, 1)

                pe.wait_ge(S.tok_ready, 5 * l + 5)
                if i:
                    pe.wait_ge(S.wt_act, 2 * g)
                    pe.wait_ge(S.mat_ev, 6 * g)
                    pe.wait_ge(S.nv_ready, g)
                products(2, BtT, AtT)
                products(4, AtT, BtT)
                products(6, KtT, AtT)
                pe.wait_ge(S.mat_ev, 6 * g + 1)
                products(2, BtT, RtT)
                pe.wait_ge(S.mat_ev, 6 * g + 3)
                quad(4, m16, mt16)
                quad(5, mt16, m16)
                pe.wait_ge(S.mat_ev, 6 * g + 5)
                products(2, KtT, RtT)
                pe.wait_ge(S.q1_ready, g + 1)
                pe.wait_ge(S.lvl_act, la + 2)
                quad(6, m2, qm)
                quad(4, m2, mt2)
                quad(5, mt2, m2)
                pe.wait_ge(S.lvl_act, la + 4)
                pe.wait_ge(S.lvl_dve, ld + 1)
                quad(6, m16, qm)
                quad(5, mt16, m16)
                pe.wait_ge(S.lvl_act, la + 5)
                pe.wait_ge(S.lvl_dve, ld + 2)
                quad(6, m2, qm)
                if i < 2:
                    pe.wait_ge(S.lvl_dve, ld + 3)
                    for h in range(4):
                        ins = pe.transpose(ps[0:n, 4, P * h:P * h + n], qm[0:n, h, 0:n], C.ident[0:n, 0:n])
                    ins.then_inc(S.lvl_mm, 1)
                    quad(5, moff, qm)
                    pe.wait_ge(S.lvl_act, la + 6)
                    pe.wait_ge(S.lvl_dve, ld + 4)
                    quad(6, mt2, m16)
                    pe.wait_ge(S.lvl_dve, ld + 5)
                else:
                    pe.wait_ge(S.lvl_dve, ld + 3)
                for h in range(4):
                    p, q = h // 2, 64 * (h % 2)
                    ins = mm(ps[q:q + 64, 4, P * p:P * p + n], tokAV[0:n, i, 0, 64 * h:64 * h + 64], qm[0:n, h, 0:n],
                             start=True, stop=True)
                ins.then_inc(S.wt_mm, 1)
                for h in range(4):
                    ins = mm(ps[0:n, 5, 64 * h:64 * h + 64], ntm[0:n, h, 0:n], tokAV[0:n, i, 1, 64 * h:64 * h + 64],
                             start=True, stop=True)
                ins.then_inc(S.wt_mm, 1)
                pe.wait_ge(S.nv_ready, g + 1)
                for h in range(4):
                    ins = mm(ps[0:n, 6, 64 * h:64 * h + 64], qm[0:n, h, 0:n], nv[0:n, 64 * h:64 * h + 64],
                             start=True, stop=True)
                ins.then_inc(S.wt_mm, 1)

            def chain(l):
                for c in range(NCHUNK):
                    i, r, n = c // 4, CH * (c % 4), min(CH, T - CH * c)
                    if c:
                        pe.wait_ge(S.st_ready, 8 * l + c)
                        for h in range(4):
                            p, q = h // 2, 64 * (h % 2)
                            ins = mm(ps[r:r + n, 2 + h % 2, 64 * p:64 * p + 64], wT[q:q + 64, p, CH * c:CH * c + n],
                                     stT[q:q + 64, c, p, :], start=True, stop=True)
                        ins.then_inc(S.u_mm, 1)
                    if c == NCHUNK - 1:
                        break
                    for h in range(4):
                        p, q = h // 2, 64 * (h % 2)
                        mm(ps[q:q + 64, 0, 64 * p:64 * p + 64], tokBK[r:r + n, i, 1, 64 * h:64 * h + 64],
                           tokAV[r:r + n, i, 1, 64 * h:64 * h + 64], start=p == 0, stop=False, skip_group_check=True)
                    pe.wait_ge(S.u_ready, NCHUNK * l + c + 1)
                    for h in range(4):
                        p, q = h // 2, 64 * (h % 2)
                        ins = mm(ps[q:q + 64, 0, 64 * p:64 * p + 64], tokBK[r:r + n, i, 0, 64 * h:64 * h + 64],
                                 uTok[r:r + n, i, 64 * h:64 * h + 64], start=False, stop=True, skip_group_check=True)
                    ins.then_inc(S.st_mm, 1)

            def outputs(l):
                pe.wait_ge(S.u_ready, NCHUNK * (l + 1))
                for h in range(4):
                    p, q = h // 2, 64 * (h % 2)
                    for i, (t0, n) in enumerate(TILES):
                        mm(ps[q:q + 64, 4 + h, t0:t0 + n], tokAV[0:n, i, 1, 64 * h:64 * h + 64], rkm[i][0:n, h, 0:n],
                           start=i == 0, stop=False, skip_group_check=True)
                        mm(ps[q:q + 64, 4 + h, t0:t0 + n], uTok[0:n, i, 64 * h:64 * h + 64], rbm[i][0:n, h, 0:n],
                           start=False, stop=False, skip_group_check=True)
                    for c in range(1, NCHUNK):
                        t0, n = CH * c, min(CH, T - CH * c)
                        ins = mm(ps[q:q + 64, 4 + h, t0:t0 + n], stT[q:q + 64, c, p, :], RtT[q:q + 64, p, t0:t0 + n],
                                 start=False, stop=True, skip_group_check=True)
                ins.then_inc(S.y_mm, 1)
                pe.wait_ge(S.y_sb, 2 * l + 2)
                head_sums(0, eT, S.gn_mm)
                pe.wait_ge(S.gn_sq, l + 1)
                head_sums(2, cumT, S.gn_mm)

            def attention(l):
                for i, (t0, n) in enumerate(TILES):
                    if i:
                        pe.wait_ge(S.vt_ready, 3 * l + i)
                    else:
                        pe.wait_ge(S.oa_ready, l + 1)
                    for h in range(4):
                        ins = pe.transpose(ps[0:n, 6, P * h:P * h + P], cur(V_CH + h)[:, 0, t0:t0 + n], C.ident)
                    ins.then_inc(S.vt_mm, 1)
                for k in range(2):
                    pe.wait_ge(S.qk_sq, 2 * l + k + 1)
                    if k:
                        pe.wait_ge(S.vt_ready, 3 * l + 3)
                    head_sums(4 * k, sqT[:, 4 * k:4 * k + 4, :], S.qk_mm)
                for k in range(2):
                    pe.wait_ge(S.qg_ready, 8 * l + 4 * k + 4)
                    pe.wait_ge(S.root_ready, NORMS * l + 4 + k)
                    for c in range(4):
                        ins = mm(ps[:, 4 * k + c, 0:T], C.rope, hnT[:, 4 * k + c, :], start=True, stop=True)
                    ins.then_inc(S.rot_mm, 1)

                def scores(u):
                    h, i = u // 3, u % 3
                    t0, n = TILES[i]
                    b, m = u % 2, t0 + n
                    if u >= 2:
                        pe.wait_ge(S.p_ready, 24 * l + 2 * u - 2)
                    for c in range(2):
                        q = 64 * c
                        mm(ps[0:n, 2 * b + c, 0:m], projT[q:q + 64, Q_CH + h, 2 + t0:2 + t0 + n],
                           projT[q:q + 64, K_CH + h, 2:2 + m], start=True, stop=False, skip_group_check=True)
                        ins = mm(ps[0:n, 2 * b + c, t0:m], C.ident[0:n, 0:n], C.causal[0:n, 0:n],
                                 start=False, stop=True, skip_group_check=True)
                    ins.then_inc(S.sc_mm, 1)

                def turn(u):
                    h, i = u // 3, u % 3
                    t0, n = TILES[i]
                    pe.wait_ge(S.pd_ready, 12 * l + u + 1)
                    if u:
                        pe.wait_ge(S.pt_ready, 12 * l + u)
                    for k in range(i + 1):
                        k0, kn = TILES[k]
                        ins = pe.transpose(ps[0:kn, 6, P * k:P * k + n], pd[0:n, u % 2, k0:k0 + kn], C.ident[0:n, 0:n])
                    ins.then_inc(S.pt_mm, 1)

                def values(h):
                    pe.wait_ge(S.pt_ready, 12 * l + 3 * h + 3)
                    if h:
                        pe.wait_ge(S.o_sb, 4 * l + h)
                    for k, (k0, kn) in enumerate(TILES):
                        ins = mm(ps[:, 7, k0:T], vTok[0:kn, k, P * h:P * h + P], pT[0:kn, h % 2, k, k0:T],
                                 start=k == 0, stop=k == 2, skip_group_check=True)
                    ins.then_inc(S.o_mm, 1)

                pe.wait_ge(S.qk_ready, 2 * l + 2)
                for u in range(14):
                    if u < 12:
                        scores(u)
                    if 1 <= u < 13:
                        turn(u - 1)
                    if u >= 3 and u % 3 == 1:
                        values(u // 3 - 1)
                pe.wait_ge(S.osq_ready, 4 * l + 4)
                for h in range(4):
                    ins = mm(ps[:, h, 0:T], C.ones, sqT[:, h, :], start=True, stop=True)
                ins.then_inc(S.ob_mm, 1)

            def project_out(l):
                pe.wait_ge(S.oa_ready, l + 1)
                pe.wait_ge(S.oc_ready, l + 1)
                pe.wait_ge(S.ob_ready, l + 1)
                for d in range(DC):
                    k = (MIXN + FFNN) * l + -(-IN_COLS // PIECE) + d // 2
                    w = piece_view(k, PIECE)
                    if d % 2 == 0:
                        pe.wait_ge(loaded[slot_of[k]], 16 * load_value[k])
                    if d >= 2:
                        pe.wait_ge(S.h_ready, DC * (2 * l + 1) + d - 1)
                    ins = group(ps[:, d % 2, 0:T], ((w[:, c, P * (d % 2):P * (d % 2) + P], oT[:, c, :])
                                                    for c in range(DC)))
                    ins.then_inc(S.wout_mm, 1)
                    if d % 2:
                        pe.wait_ge(S.wout_mm, DC * l + d + 1)
                        pe.sem_inc(S.pieces_used, 1)

            def gate_up(x, n, before, piece, ready):
                for f in range(FC):
                    half = P * (f % 2)
                    for z in range(2):
                        w, is_in, in_value = piece(2 * (f // 2) + z)
                        w = w.rearrange("p (c n) -> p c n", c=DC)
                        if f % 2 == 0:
                            pe.wait_ge(is_in, in_value)
                        if f >= 2 and z == 0:
                            pe.wait_ge(S.hid_ready, before + (f - 1))
                        for c in range(DC):
                            if f == 0:
                                ready(z, c)
                            ins = mm(ps[:, 2 * z + f % 2, 0:n], w[:, c, half:half + P], x[:, c, 0:n],
                                     start=c == 0, stop=c == DC - 1)
                        if f % 2 == 1 and z == 0:
                            ins.then_inc(S.pieces_used, 1)
                    ins.then_inc(S.gu_mm, 1)
                    if f % 2 == 1:
                        pe.wait_ge(S.gu_mm, before + (f + 1))
                        pe.sem_inc(S.pieces_used, 1)

            pe.wait_ge(S.consts_in, 16)
            pe.wait_ge(S.x_in, 64)
            for c in range(DC):
                if c >= 2:
                    pe.wait_ge(S.h_ready, c - 1)
                for i, (t0, n) in enumerate(TILES):
                    ins = pe.transpose(ps[:, c % 2, t0:t0 + n], xTok[0:n, i, P * c:P * c + P], C.ident[0:n, 0:n])
                ins.then_inc(S.x_mm, 1)
            pe.wait_ge(S.params_in, 16 * N_PARAMS)
            nr = DEPTH * ROWS
            pe.transpose(ps[:, 2, 0:nr], vrow[0:nr, :], C.ident[0:nr, 0:nr]).then_inc(S.vcol_mm, 1)
            pe.wait_ge(S.lam_prod, DEPTH)
            mm(ps[:, 0, 0:DEPTH], C.ones[0:64, :], small[0:64, 0:DEPTH], start=True, stop=True).then_inc(S.lam_mm, 1)
            mm(ps[:, 1, 0:DEPTH], C.ones[64:P, :], small[64:P, 0:DEPTH], start=True, stop=True).then_inc(S.lam_mm, 1)

            for l in range(DEPTH):
                norm_sum(2 * l)
                if l == 0:
                    pe.wait_ge(S.lam_exp, 2)
                for n in range(NCH):
                    project(l, n)
                    if n == 9:
                        rwkv_lora(l)
                    if n == 15:
                        pe.wait_ge(S.kk_sq, l + 1)
                        pe.wait_ge(S.lora_out, 5 * l + 5)
                        head_sums(2, kks, S.kk_mm)
                    if n == 19:
                        pe.wait_ge(S.bonus_pre, l + 1)
                        head_sums(4, bonusT, S.bonus_mm)
                token_rows(l)
                for i in range(3):
                    matrices(l, i)
                chain(l)
                outputs(l)
                attention(l)
                project_out(l)
                norm_sum(2 * l + 1)
                if l == 0:
                    def piece(j):
                        k = MIXN + j
                        return slot(slot_of[k]), loaded[slot_of[k]], 16 * load_value[k]

                    gate_up(hnT, T, 0, piece,
                            lambda z, c: pe.wait_ge(S.hn_ready, DC + c + 1) if z == 0 else None)
                    pe.wait_ge(S.hid_ready, FC)
                    for f in range(FC):
                        w, is_in, in_value = piece(FC + f // 2)
                        w = w.rearrange("p (c n) -> p c n", c=2)
                        if f % 2 == 0:
                            pe.wait_ge(is_in, in_value)
                        for d in range(DC):
                            ins = mm(ps[:, d, 0:T], w[:, f % 2, P * d:P * d + P], hid[:, f, :],
                                     start=f == 0, stop=f == FC - 1)
                            if f == FC - 1:
                                ins.then_inc(S.down_mm, 1)
                        if f % 2 and f < FC - 1:
                            ins.then_inc(S.pieces_used, 1)
                    pe.wait_ge(S.down_mm, DC)
                    pe.sem_inc(S.pieces_used, 1)

            pe.wait_ge(S.hn_ready, 4 * DC)
            pe.wait_ge(S.router_in, 16)
            for i, (t0, n) in enumerate(TILES):
                ins = group(ps[0:n, 0, NE * i:NE * i + NE], ((hnT[:, c, t0:t0 + n], router[:, c, :])
                                                             for c in range(DC)))
            ins.then_inc(S.lg_mm, 1)
            for k in range(6):
                i, half = k // 2, k % 2
                t0, n = TILES[i]
                if k >= 2:
                    pe.wait_ge(S.hntok_ready, k - 1)
                for c in range(4):
                    ins = pe.transpose(ps[0:n, 2 + half, P * c:P * c + P], hnT[:, 4 * half + c, t0:t0 + n], C.ident)
                ins.then_inc(S.hntok_mm, 1)
            pe.wait_ge(S.sel_ready, 1)
            for i, (t0, n) in enumerate(TILES):
                group(ps[0:n, 1, NE * i:NE * i + NE],
                      [(C.ones[:, 0:n], sel[:, j, :]) for j in range(i)] + [(C.tri[0:n, 0:n], sel[0:n, i, :])])
            group(ps[0:1, 1, 3 * NE:4 * NE], [(C.ones[0:n, 0:1], sel[0:n, i, :]) for i, (t0, n) in enumerate(TILES)]
                  ).then_inc(S.pos_mm, 1)

            pe.wait_ge(S.hntok_ready, 6)
            pe.wait_ge(S.table_ready, 1)
            n_items = pe.value_load(ntab[0:1, 0:1], min_val=NE, max_val=NE + MAXO)
            with pe.Fori(0, n_items) as it:
                def piece(j):
                    s = j % BIG_RING
                    return slot(s), loaded[s], it * (16 * per_item[s]) + 16 * (filled[s] + j // BIG_RING + 1)

                pe.wait_ge(S.oneh_ready, it + 1)
                for c in range(DC):
                    ins = group(ps[:, 6 + c // 4, CAP * (c % 4):CAP * (c % 4) + CAP],
                                ((hnTok[0:n, i, P * c:P * c + P], oneh[0:n, i, :])
                                 for i, (t0, n) in enumerate(TILES)))
                    if c % 4 == 3:
                        ins.then_inc(S.gather_mm, 1)
                for i, (t0, n) in enumerate(TILES):
                    ins = pe.transpose(ps[0:CAP, 4, t0:t0 + n], gateh[0:n, i, :], C.ident[0:n, 0:n])
                ins.then_inc(S.gt_mm, 1)

                def ready(z, c):
                    if z == 0 and c == 0:
                        pe.wait_ge(S.xe_act, it + 1)
                    if z == 0 and c == 4:
                        pe.wait_ge(S.xe_dve, it + 1)

                gate_up(xe, CAP, it * FC + FC, piece, ready)
                pe.wait_ge(S.gt_ready, it + 1)
                for f in range(FC):
                    w, is_in, in_value = piece(FC + f // 2)
                    w = w.rearrange("p (c n) -> p c n", c=2)
                    if f % 2 == 0:
                        pe.wait_ge(is_in, in_value)
                    if f == 0:
                        pe.wait_ge(S.hid_ready, it * FC + (2 * FC - 2))
                    if f == FC - 2:
                        pe.wait_ge(S.hid_ready, it * FC + 2 * FC)
                    for z in range(2):
                        ins = mm(ps[0:CAP, 4 + z, :], hid[:, f, 0:CAP], w[:, f % 2, 512 * z:512 * z + 512],
                                 start=f == 0, stop=f == FC - 1)
                        if f == FC - 1:
                            ins.then_inc(S.down_mm, 1)
                    if f % 2 and f < FC - 1:
                        ins.then_inc(S.pieces_used, 1)
                pe.wait_ge(S.down_mm, 2 * it + (DC + 2))
                pe.sem_inc(S.pieces_used, 1)
                for c in range(DC):
                    if c == 0:
                        pe.wait_ge(S.y_act, it + 1)
                    if c == 4:
                        pe.wait_ge(S.y_dve, it + 1)
                    if c >= 2:
                        pe.wait_ge(S.h_item, DC * it + (c - 1))
                    mm(ps[:, 6 + c % 2, 0:T], yE[0:CAP, P * c:P * c + P], gateT[0:CAP, :],
                       start=True, stop=True).then_inc(S.scat_mm, 1)
                pe.wait_ge(S.h_item, DC * it + DC)

            for i, (t0, n) in enumerate(TILES):
                if i == 2:
                    pe.wait_ge(S.out_act, 1)
                    pe.wait_ge(S.out_dve, 1)
                for half in range(2):
                    for c in range(4):
                        ins = pe.transpose(ps[0:n, 2 * (i % 2) + half, P * c:P * c + P], hT[:, 4 * half + c, t0:t0 + n],
                                           C.ident)
                    ins.then_inc(S.out_mm, 1)


N_PARAMS = DEPTH * 20

_OUT = (1, SEQ, D)


def kernel(**inputs):
    import concourse.bacc as _bacc
    from concourse.bass_utils import run_bass_kernel_spmd as _run

    nc = _bacc.Bacc("TRN2", target_bir_lowering=False, num_devices=1)
    arrays, A = {}, {}
    for name, value in list(inputs.items()) + [("consts", constants())]:
        a = np.ascontiguousarray(value)
        arrays[f"in_{name}"] = a
        A[name] = nc.dram_tensor(f"in_{name}", a.shape, mybir.dt.from_np(a.dtype), kind="ExternalInput").ap()
    out = nc.dram_tensor("out_0", _OUT, F32, kind="ExternalOutput").ap()
    build(nc, A, out)
    r = _run(nc, [arrays], core_ids=[0])
    return r.results[0]["out_0"]
```

```python
import math
from collections import namedtuple
from contextlib import ExitStack

import numpy as np

import concourse.bass as bass
from concourse import mybir

F32 = mybir.dt.float32
F32R = mybir.dt.float32r
I32 = mybir.dt.int32
U32 = mybir.dt.uint32
ALU = mybir.AluOpType
ACT = mybir.ActivationFunctionType
AXX = mybir.AxisListType.X

P = 128
D = 1024
DC = D // P
SEQ = 256
META = 16
T = SEQ + META
TILES = [(0, 128), (128, 128), (256, 16)]
DEPTH = 2
HR, NR = 4, 64
RW = HR * NR
HD, DK = 4, 64
FF = 2816
FC = FF // P
NE = 8
TOPK = 2
IN_COLS = 3200
NCH = IN_COLS // P
RWKV_CH, Q_CH, K_CH, V_CH, BG_CH, CG_CH, U_CH = 0, 7, 11, 15, 19, 21, 23
LAM_INIT = [0.8 - 0.6 * math.exp(-0.3 * i) for i in range(DEPTH)]
NORM_EPS, GN_EPS, SUB_EPS = 1e-6, 64e-5, 1e-5
CH = 32
NCHUNK = -(-T // CH)
E_HALF = math.exp(-0.5)

CAP = 96
MAXO = (T * TOPK) // CAP
NIT = NE + MAXO + 1
NFLAG = NE * (-(-T // CAP) - 1)

SMALL_RING = 5
BIG_RING = 6
PARTS = 3
SLOT = 2048
PIECE = 2 * P

ROWS = 48
(MIXG, FFNG, MU, W0, A0, KK, KA, RK, GNG, GNB, QG, KG, SUBG, CONV, LAMQ, LAMK) = (
    0, 8, 16, 23, 25, 27, 29, 31, 33, 35, 37, 38, 39, 40, 46, 47)

CONSTS = ["ident", "ones", "blk", "rope", "m16t", "m16", "moff", "m32s", "m32i", "causal", "tri"]
WIDE = ["cos", "sin", "reset", "iota"]


def constants():
    r = np.arange(P)
    a, b = r[:, None], r[None, :]
    c = {
        "ident": a == b,
        "ones": np.ones((P, P)),
        "blk": a // 64 == b // 64,
        "m16t": (a < b) & (a // 16 == b // 16),
        "m16": (b < a) & (a // 16 == b // 16),
        "moff": (b < a) & (a // 32 == b // 32) & (a // 16 != b // 16),
        "m32s": (a < b) & (a // 32 == b // 32),
        "m32i": (a <= b) & (a // 32 == b // 32),
        "causal": np.where(b > a, -1e30, 0.0),
        "tri": a < b,
    }
    rope = np.zeros((P, P))
    for h in (0, 64):
        for d in range(8):
            rope[h + d + 8, h + d] = -1.0
            rope[h + d, h + d + 8] = 1.0
    c["rope"] = rope
    inv = (np.float32(500000.0) ** (-np.arange(0, 16, 2, dtype=np.float32) / np.float32(16))).astype(np.float32)
    ang = np.arange(T, dtype=np.float32)[:, None] * inv[None, :]
    cos, sin = np.ones((P, T), np.float32), np.zeros((P, T), np.float32)
    for h in (0, 8, 64, 72):
        cos[h:h + 8] = np.cos(ang).T
        sin[h:h + 8] = np.sin(ang).T
    reset = np.broadcast_to((np.arange(T) % CH != 0), (P, T))
    iota = np.broadcast_to(np.arange(CAP * -(-T // CAP)), (P, CAP * -(-T // CAP)))
    parts = [np.asarray(c[n], np.float32) for n in CONSTS] + [cos, sin, reset, iota]
    return np.ascontiguousarray(np.concatenate([np.asarray(x, np.float32) for x in parts], axis=1))


def build(nc, A, out):
    ctx = ExitStack()
    with ctx:
        def sb(name, shape, dt=F32):
            return ctx.enter_context(nc.sbuf_tensor(name, shape, dt))

        def sems(*names):
            return namedtuple("Semaphores", names)(*(ctx.enter_context(nc.semaphore(n)) for n in names))

        ps = ctx.enter_context(nc.psum_tensor("ps", [P, 8, 512], F32))
        hT = sb("hT", [P, DC, T])
        hnT = sb("hnT", [P, DC, T])
        ring_small = sb("ring_small", [P, SMALL_RING, SLOT])
        vrow = sb("vrow", [DEPTH * ROWS, P])
        vcol = sb("vcol", [P, DEPTH * ROWS])
        vhalf = sb("vhalf", [P, DEPTH, 4])
        wide = CAP * -(-T // CAP)
        cst = sb("cst", [P, P * len(CONSTS) + 3 * T + wide])
        C = namedtuple("Tables", CONSTS)(*(cst[:, P * k:P * k + P] for k in range(len(CONSTS))))
        o = P * len(CONSTS)
        cosT, sinT, resetT = (cst[:, o + k * T:o + (k + 1) * T] for k in range(3))
        iotaT = cst[:, o + 3 * T:o + 3 * T + wide]
        epsT = sb("epsT", [P, 3])
        msT = sb("msT", [P, 4 * T])
        rsT = sb("rsT", [P, 4 * T])
        small = sb("small", [P, 64])
        router = sb("router", [P, DC, NE])
        ARENA = 33216
        arena_at = nc.sbuf_base
        arena = sb("arena", [P, ARENA])
        used = [0]

        def carve(*shape):
            n = int(np.prod(shape))
            v = arena[:, used[0]:used[0] + n]
            used[0] += n
            assert used[0] <= ARENA, used[0]
            if len(shape) == 1:
                return v
            names = "abcd"[:len(shape)]
            return v.rearrange(f"p ({' '.join(names)}) -> p {' '.join(names)}",
                               **{n: s for n, s in zip(names, shape)})

        projT = carve(NCH, T + 2)
        sqT = carve(DC, T)
        oT = carve(DC, T)
        hxT = carve(7, T)
        lora = carve(T)
        lora_w = carve(RW)
        eT, cumT, PtT, AtT, KtT, KhT, aT, gT, kkT, bT, BtT, RtT, bonusT, kks = (carve(2, T) for _ in range(14))
        cvT = kks
        tokAV = carve(3, 2, 256)
        tokBK = carve(2, 2, 256)
        mark = used[0]
        m16, mt16, moff, m2, mt2, ntm, qm = (carve(4, P) for _ in range(7))
        rbm, rkm = ([carve(4, P), carve(4, P), carve(4, TILES[2][1])] for _ in range(2))
        wT = carve(2, T)
        nv = carve(256)
        zTok = carve(3, 256)
        uTok = carve(3, 256)
        stT = carve(NCHUNK, 2, NR)
        pst = carve(2, NR)
        used[0] = mark
        vTok = carve(3, 512)
        prob = carve(2, 2, T)
        pd = carve(2, T)
        scaled = carve(T)
        pT = carve(2, 3, T)
        oat = carve(4, T)
        used[0] = mark
        xTok = carve(3, D)

        def carve_parts(name, *shape):
            o = used[0]
            carve(int(np.prod(shape)))
            return nc.alloc_sbuf_tensor_at(name, [P, *shape], F32R, offset=arena_at + 4 * o)

        used[0] = 0
        big = carve(BIG_RING - SMALL_RING, SLOT)
        w_hi, w_lo = carve_parts("w_hi", PARTS, SLOT), carve_parts("w_lo", PARTS, SLOT)
        mark = used[0]
        xd_hi, xd_lo = carve_parts("xd_hi", DC, T), carve_parts("xd_lo", DC, T)
        hd_hi, hd_lo = carve_parts("hd_hi", FC, T), carve_parts("hd_lo", FC, T)
        sgd = carve(2, 2, T)
        hmd = sgd
        used[0] = mark
        xm_hi, xm_lo = carve_parts("xm_hi", DC, CAP), carve_parts("xm_lo", DC, CAP)
        hm_hi, hm_lo = carve_parts("hm_hi", FC, CAP), carve_parts("hm_lo", FC, CAP)
        y_hi, y_lo = carve_parts("y_hi", D), carve_parts("y_lo", D)
        ohT = carve_parts("ohT", T)
        sgm = carve(2, PIECE)
        hmTok = carve(2, PIECE)
        hnTok = carve(3, D)
        oneh = carve(3, CAP)
        gsel = carve(3, 1)
        gslot = carve(1)
        lgS, sel, posx, gates, oh1, oh2, top8 = (carve(3, NE) for _ in range(7))
        fidx, gw = carve(3, 2), carve(3, 2)
        cnt, flag, incl, ev, ov = (carve(NFLAG) for _ in range(5))
        eqg, pick = carve(MAXO, NFLAG), carve(MAXO, NFLAG)
        tab = sb("tab", [1, 2, NIT], I32)
        ntab = sb("ntab", [1, 1], I32)
        fsum = sb("fsum", [1, 2, NIT])
        stat = sb("stat", [P, 2, 6])
        idx8 = sb("idx8", [P, 3, 8], U32)

        def slot(s):
            return ring_small[:, s, :] if s < SMALL_RING else big[:, s - SMALL_RING, :]

        w_in, w_out = A["w_in"], A["w_out"]

        def cols_piece(w, n0, n):
            return w[:, n0:n0 + n].rearrange("(c p) n -> p c n", p=P)

        def rows_piece(w, r0):
            return w[r0:r0 + PIECE, :].rearrange("(c p) n -> p c n", p=P)

        def mixer_loads(l):
            for n0 in range(0, IN_COLS, PIECE):
                n = min(PIECE, IN_COLS - n0)
                yield cols_piece(w_in[l], n0, n), DC * n
            for n0 in range(0, D, PIECE):
                yield cols_piece(w_out[l], n0, PIECE), SLOT

        def ffn_loads(g, u, d):
            for s in range(FF // PIECE):
                yield cols_piece(g, s * PIECE, PIECE), SLOT
                yield cols_piece(u, s * PIECE, PIECE), SLOT
            for s in range(FF // PIECE):
                yield rows_piece(d, s * PIECE), SLOT

        MIXN, FFNN = -(-IN_COLS // PIECE) + D // PIECE, 3 * FF // PIECE
        STATIC = 2 * MIXN + FFNN
        slot_of, prior, filled = [], [], [0] * BIG_RING
        last = [None] * BIG_RING
        load_value = []
        for k in range(STATIC):
            if k < MIXN:
                s = k % SMALL_RING
            elif k < MIXN + FFNN:
                s = (k - MIXN + MIXN % SMALL_RING) % BIG_RING
            else:
                s = (k - STATIC + SMALL_RING) % SMALL_RING
            slot_of.append(s)
            prior.append(last[s])
            last[s] = k
            filled[s] += 1
            load_value.append(filled[s])
        item_prior = [max(k for k in range(-FFNN, j) if (k % FFNN) % BIG_RING == j % BIG_RING) for j in range(FFNN)]
        per_item = [len(range(s, FFNN, BIG_RING)) for s in range(BIG_RING)]

        assert FFNN % PARTS == 0

        loaded = [ctx.enter_context(nc.semaphore(f"piece_in_slot{s}")) for s in range(BIG_RING)]

        S = sems(
            "consts_in", "params_in", "x_in", "lora_w_in", "out_stored", "router_in",
            "eps_set", "pads_zero", "vcol_mm", "vcol_ready", "vhalf_ready", "dve_chain", "pool_chain",
            "x_mm", "h_ready", "sq_ready", "nsum_mm", "root_ready", "kk_max", "rs_ready", "hn_ready",
            "proj_mm", "proj_act", "proj_dve",
            "shift_d", "hx_ready", "lora_act", "lora_sig", "lora_mm", "lora_out",
            "decay_ready", "exp_ready", "kk_sq", "kk_mm", "bonus_pre", "bonus_mm", "til_ready",
            "tok_mm", "tok_ready", "mat_mm", "mat_ev", "lvl_mm", "lvl_act", "lvl_dve", "q1_ready",
            "wt_mm", "wt_act", "nv_ready",
            "u_mm", "u_ready", "st_mm", "st_ready", "y_mm", "y_sb",
            "gn_mm", "gn_cent", "gn_sq", "oa_ready", "oc_ready",
            "qk_sq", "qk_mm", "qg_ready", "qcos_ready", "rot_mm", "qk_ready",
            "vt_mm", "vt_ready", "lam_prod", "lam_mm", "lam_exp",
            "sc_mm", "mx_ready", "p_ready", "pd_ready", "pt_mm", "pt_ready", "o_mm", "o_sb", "osq_ready",
            "ob_mm", "ob_ready", "wout_mm",
            "hi_ready", "lo_ready", "parts_used", "xd_hi_ready", "xd_lo_ready",
            "silu_ready", "hid_prod", "hd_hi_ready", "hd_lo_ready", "down_mm",
            "msilu_ready", "mhid_prod", "ht_mm", "hm_hi_ready", "hm_lo_ready",
            "hntok_mm", "hntok_ready", "lg_mm", "gap_ready", "gap_exp", "sel_ready", "pos_mm", "table_ready",
            "oneh_ready", "gather_mm", "xm_hi_ready", "xm_lo_ready", "oht_mm", "oht_ready", "gslot_mm", "gslot_ready",
            "y_hi_ready", "y_lo_ready", "scat_mm",
            "h_item", "out_mm", "out_act", "out_dve",
        )

        def freed(k):
            if MIXN <= k < MIXN + FFNN:
                return S.lo_ready, k - MIXN + 1
            l, q = (0, k) if k < MIXN else (1, k - MIXN - FFNN)
            n_in = -(-IN_COLS // PIECE)
            if q < n_in:
                return S.proj_mm, NCH * l + min(2 * q + 2, NCH)
            return S.wout_mm, DC * l + 2 * (q - n_in) + 2
        block = ctx.enter_context(nc.Block())

        def vc(l, k, n=1):
            return vcol[:, l * ROWS + k:l * ROWS + k + n]

        def bc(ap, n):
            return ap.unsqueeze(1).broadcast_to([ap.shape[0], n, ap.shape[1]])

        def tail(ap, n):
            return ap.unsqueeze(len(ap.shape)).broadcast_to(list(ap.shape) + [n])

        def cur(c0, n=1):
            return projT[:, c0:c0 + n, 2:T + 2]

        def prev(c0, k, n=1):
            return projT[:, c0:c0 + n, 2 - k:T + 2 - k]

        def lvl(per_tile, l, i):
            return (2 * per_tile[0] + per_tile[1]) * l + per_tile[0] * i

        LVM, LVA, LVD = (11, 8), (6, 5), (5, 3)
        NORMS = 7

        @block.sync
        def _(sp):
            sp.dma_start(cst[:], A["consts"]).then_inc(S.consts_in, 16)
            sp.dma_start(xTok[0:META, 0, :], A["meta_tokens"]).then_inc(S.x_in, 16)
            sp.dma_start(xTok[META:P, 0, :], A["x"][0, 0:P - META, :]).then_inc(S.x_in, 16)
            sp.dma_start(xTok[:, 1, :], A["x"][0, P - META:2 * P - META, :]).then_inc(S.x_in, 16)
            sp.dma_start(xTok[0:META, 2, :], A["x"][0, 2 * P - META:SEQ, :]).then_inc(S.x_in, 16)

            k = 0
            for stage in (mixer_loads(0),
                          ffn_loads(A["ffn_w_gate"][0], A["ffn_w_up"][0], A["ffn_w_down"][0]),
                          mixer_loads(1)):
                for src, width in stage:
                    s = slot_of[k]
                    if prior[k] is not None:
                        sp.wait_ge(*freed(prior[k]))
                    if MIXN <= k < MIXN + FFNN and SMALL_RING <= s:
                        sp.wait_ge(S.h_ready, 2 * DC)
                    dst = slot(s)[:, 0:width].rearrange("p (c n) -> p c n", c=src.shape[1])
                    sp.dma_start(dst, src).then_inc(loaded[s], 16)
                    k += 1

            def item_loads(i, expert, first, end):
                pieces = list(ffn_loads(*(A[n][0, expert] for n in ("moe_w_gate", "moe_w_up", "moe_w_down"))))
                for j in range(first, end):
                    src = pieces[j][0]
                    if j != 2 * FFNN // 3:
                        after = item_prior[j + 1 if j + 1 == 2 * FFNN // 3 else j]
                        sp.wait_ge(S.lo_ready, i * FFNN + (FFNN + after + 1))
                    dst = slot(j % BIG_RING).rearrange("p (c n) -> p c n", c=src.shape[1])
                    sp.dma_start(dst, src).then_inc(loaded[j % BIG_RING], 16)

            sp.wait_ge(S.wout_mm, 2 * DC)
            item_loads(0, 0, 0, PARTS)
            with sp.Fori(0, NE - 1) as i:
                item_loads(i, i, PARTS, SMALL_RING)
                sp.wait_ge(S.h_ready, 4 * DC)
                item_loads(i, i, SMALL_RING, FFNN)
                item_loads(i + 1, i + 1, 0, PARTS)
            sp.wait_ge(S.table_ready, 1)
            n_items = sp.value_load(ntab[0:1, 0:1], min_val=NE, max_val=NE + MAXO)
            with sp.Fori(NE - 1, n_items) as i:
                expert = sp.value_load(tab[0:1, 0, bass.ds(i, 1)], min_val=0, max_val=NE - 1)
                item_loads(i, expert, PARTS, FFNN)
                expert = sp.value_load(tab[0:1, 0, bass.ds(i + 1, 1)], min_val=0, max_val=NE - 1)
                item_loads(i + 1, expert, 0, PARTS)
            for i, (dst, rows) in enumerate(((out[0, 0:P - META, :], (META, P)),
                                             (out[0, P - META:2 * P - META, :], (0, P)),
                                             (out[0, 2 * P - META:SEQ, :], (0, META)))):
                sp.wait_ge(S.out_act, i + 1)
                sp.wait_ge(S.out_dve, i + 1)
                sp.dma_start(dst, xTok[rows[0]:rows[1], i, :]).then_inc(S.out_stored, 16)
            sp.wait_ge(S.out_stored, 48)

        @block.gpsimd
        def _(pool):
            done = [0]

            def step(ins):
                done[0] += 1
                ins.then_inc(S.pool_chain, 1)
                pool.wait_ge(S.pool_chain, done[0])

            for k, eps in enumerate((NORM_EPS, GN_EPS, SUB_EPS)):
                pool.memset(epsT[:, k:k + 1], eps).then_inc(S.eps_set, 1)

            for l in range(DEPTH):
                pool.wait_ge(S.h_ready, DC * (2 * l + 1))
                pool.memset(projT[:, :, 0:2], 0.0).then_inc(S.pads_zero, 1)
                pool.wait_ge(S.pads_zero, l + 1)
                pool.wait_ge(S.proj_act, 13 * l + 4)
                pool.wait_ge(S.proj_dve, 12 * l + 3)
                pool.tensor_tensor(sqT[:, 0:7, :], prev(RWKV_CH, 1, 7), cur(RWKV_CH, 7),
                                   ALU.subtract).then_inc(S.shift_d, 1)
                pool.wait_ge(S.proj_act, 13 * l + 13)
                pool.wait_ge(S.proj_dve, 12 * l + 12)
                step(pool.tensor_tensor(cur(CG_CH, 2), cur(CG_CH, 2), cur(U_CH, 2), ALU.mult))
                for j in range(3):
                    for c in range(2):
                        ins = pool.tensor_scalar((cvT if j else oT[:, 6:8, :])[:, c, :], prev(CG_CH + c, 2 - j)[:, 0, :],
                                                 vc(l, CONV + 2 * j + c), None, ALU.mult)
                        if c == 1:
                            step(ins)
                    if j:
                        step(pool.tensor_tensor(oT[:, 6:8, :], oT[:, 6:8, :], cvT, ALU.add))
                pool.tensor_tensor(oT[:, 6:8, :], oT[:, 6:8, :], cur(BG_CH, 2), ALU.mult).then_inc(S.oc_ready, 1)
                for c in range(2):
                    pool.wait_ge(S.qg_ready, 8 * l + 4 * c + 4)
                    pool.tensor_tensor(cur(Q_CH + 4 * c, 4), hnT[:, 4 * c:4 * c + 4, :], bc(cosT, 4),
                                       ALU.mult).then_inc(S.qcos_ready, 1)

        @block.scalar
        def _(act):
            def params(q, l):
                b = l * ROWS

                def chunks(v):
                    return v.rearrange("(c p) -> c p", p=P)

                for off, n, src in (
                    (MIXG, 8, chunks(A["mix_norm_g"][l])), (FFNG, 8, chunks(A["ffn_norm_g"][l])),
                    (MU, 7, chunks(A["tm_mu"][l])), (W0, 2, chunks(A["tm_w0"][l])), (A0, 2, chunks(A["tm_a0"][l])),
                    (KK, 2, chunks(A["tm_k_k"][l])), (KA, 2, chunks(A["tm_k_a"][l])),
                    (RK, 2, A["tm_r_k"][l].rearrange("(c a) n -> c (a n)", a=2)),
                    (GNG, 2, chunks(A["tm_gn_g"][l])), (GNB, 2, chunks(A["tm_gn_b"][l])),
                    (SUBG, 1, chunks(A["da_subln_g"][l])),
                    (CONV, 6, A["sc_conv_w"][l].rearrange("j (c p) -> (j c) p", p=P)),
                ):
                    q.dma_start(vrow[b + off:b + off + n, :], src).then_inc(S.params_in, 16)
                for row, half, name in ((QG, 0, "da_q_norm_g"), (QG, 1, "da_q_norm_g"), (KG, 0, "da_k_norm_g"),
                                        (KG, 1, "da_k_norm_g"), (LAMQ, 0, "da_lambda_q1"), (LAMQ, 1, "da_lambda_q2"),
                                        (LAMK, 0, "da_lambda_k1"), (LAMK, 1, "da_lambda_k2")):
                    q.dma_start(vrow[b + row:b + row + 1, 64 * half:64 * half + 64],
                                A[name][l:l + 1, :]).then_inc(S.params_in, 16)

            for l in range(DEPTH):
                params(act, l)
            act.dma_start(router[:], A["router_w"][0].rearrange("(c p) e -> p c e", p=P)).then_inc(S.router_in, 16)
            act.wait_ge(S.eps_set, 3)

            def lambdas():
                act.wait_ge(S.lam_mm, 2)
                act.activation(small[:, 2:4], ps[:, 3, 0:2], ACT.Exp).then_inc(S.lam_exp, 1)
                act.activation(small[:, 4:6], ps[:, 4, 0:2], ACT.Exp).then_inc(S.lam_exp, 1)

            def squares(idx):
                for k in range(2):
                    act.wait_ge(S.h_ready, DC * idx + 4 * (k + 1))
                    act.activation(sqT[:, 4 * k:4 * k + 4, :], hT[:, 4 * k:4 * k + 4, :],
                                   ACT.Square).then_inc(S.sq_ready, 1)

            def root(banks, n, scale, eps):
                act.activation(msT[:, 0:n * T].rearrange("p (c t) -> p c t", c=n), ps[:, banks:banks + n, 0:T],
                               ACT.Sqrt, scale=scale, bias=epsT[:, eps:eps + 1]).then_inc(S.root_ready, 1)

            def norm_root(idx):
                act.wait_ge(S.nsum_mm, idx + 1)
                root(7, 1, 1.0 / D, 0)

            def rwkv_lora(l):
                act.wait_ge(S.hx_ready, 7 * l + 1)
                act.activation(lora[0:32, :], hxT[0:32, 6, :], ACT.Tanh).then_inc(S.lora_act, 1)
                act.activation(lora[64:128, :], hxT[64:128, 6, :], ACT.Tanh, scale=0.5).then_inc(S.lora_act, 1)
                act.activation(lora[32:64, :], hxT[32:64, 6, :], ACT.Copy).then_inc(S.lora_act, 1)

            def rwkv_lora_out(l):
                act.wait_ge(S.vhalf_ready, DEPTH)
                for k, dst in ((0, eT), (1, aT)):
                    act.wait_ge(S.lora_mm, 3 * l + k + 1)
                    for p in range(2):
                        act.activation(dst[:, p, :], ps[:, 2 + 2 * k + p, 0:T], ACT.Tanh, scale=0.5,
                                       bias=vhalf[:, l, 2 * k + p:2 * k + p + 1]).then_inc(S.lora_out, 1)
                act.wait_ge(S.lora_mm, 3 * l + 3)
                act.activation(gT, ps[:, 6:8, 0:T], ACT.Copy).then_inc(S.lora_out, 1)

            def rwkv_exp(l):
                act.wait_ge(S.decay_ready, l + 1)
                act.activation(PtT, cumT, ACT.Exp, scale=-1.0).then_inc(S.exp_ready, 1)
                act.activation(AtT, AtT, ACT.Exp, scale=-1.0).then_inc(S.exp_ready, 1)
                act.activation(KtT, cumT, ACT.Exp).then_inc(S.exp_ready, 1)
                act.activation(KhT[:, :, 0:256], KhT[:, :, 0:256], ACT.Exp).then_inc(S.exp_ready, 1)

            def rwkv_tok(l):
                k = 0
                for i, (t0, n) in enumerate(TILES):
                    for bank, dst in ((2, tokAV), (3, tokBK))[:2 if i < 2 else 1]:
                        k += 1
                        act.wait_ge(S.tok_mm, 5 * l + k)
                        act.activation(dst[0:n, i], ps[0:n, bank, :].rearrange("p (a b) -> p a b", a=2),
                                       ACT.Copy).then_inc(S.tok_ready, 1)

            def rwkv_levels(l, i):
                t0, n = TILES[i]
                g = 3 * l + i
                at = lvl(LVM, l, i)

                def copy(dst, bank, need):
                    act.wait_ge(S.lvl_mm, at + need)
                    act.activation(dst[0:n, :, 0:n], ps[0:n, bank, :].rearrange("p (h t) -> p h t", h=4)[:, :, 0:n],
                                   ACT.Copy).then_inc(S.lvl_act, 1)

                copy(mt2, 4, 1)
                copy(m2, 5, 2)
                act.wait_ge(S.q1_ready, g + 1)
                copy(mt16, 4, 4)
                copy(m16, 5, 5)
                copy(m2, 5, 7)
                if i < 2:
                    copy(mt2, 4, 9)
                act.wait_ge(S.wt_mm, 3 * g + 1)
                act.activation(wT[:, :, t0:t0 + n], ps[:, 4, 0:256].rearrange("p (a t) -> p a t", a=2)[:, :, 0:n],
                               ACT.Copy).then_inc(S.wt_act, 1)
                act.wait_ge(S.wt_mm, 3 * g + 3)
                act.activation(zTok[0:n, i], ps[0:n, 6, 0:256], ACT.Copy).then_inc(S.wt_act, 1)

            def group_norm(l):
                act.wait_ge(S.y_mm, l + 1)
                act.activation(eT[0:64], ps[0:64, 4:8:2, 0:T], ACT.Copy).then_inc(S.y_sb, 1)
                act.activation(eT[64:128], ps[64:128, 5:8:2, 0:T], ACT.Copy).then_inc(S.y_sb, 1)
                act.wait_ge(S.gn_cent, l + 1)
                act.activation(cumT, eT, ACT.Square).then_inc(S.gn_sq, 1)
                act.wait_ge(S.gn_mm, 2 * l + 2)
                root(2, 2, 1.0 / NR, 1)

            def attention(l):
                for k in range(2):
                    act.activation(sqT[:, 4 * k:4 * k + 4, :], cur(Q_CH + 4 * k, 4), ACT.Square).then_inc(S.qk_sq, 1)
                for k, g in ((0, QG), (1, KG)):
                    for c in range(4):
                        act.activation(hnT[:, 4 * k + c, :], cur(Q_CH + 4 * k + c)[:, 0, :], ACT.Copy,
                                       scale=vc(l, g)).then_inc(S.qg_ready, 1)
                for i, (t0, n) in enumerate(TILES):
                    act.wait_ge(S.vt_mm, 3 * l + i + 1)
                    act.activation(vTok[0:n, i], ps[0:n, 6, :], ACT.Copy).then_inc(S.vt_ready, 1)
                for k in range(2):
                    act.wait_ge(S.qk_mm, 2 * l + k + 1)
                    act.wait_ge(S.rs_ready, NORMS * l + 3 + k)
                    root(4 * k, 4, 1.0 / DK, 0)
                for u in range(12):
                    h, i = u // 3, u % 3
                    t0, n = TILES[i]
                    b, m = u % 2, t0 + n
                    act.wait_ge(S.mx_ready, 12 * l + u + 1)
                    for c in range(2):
                        act.activation(prob[0:n, b, c, 0:m], ps[0:n, 2 * b + c, 0:m], ACT.Exp, scale=DK ** -0.5,
                                       bias=stat[0:n, b, c:c + 1],
                                       accum_out=stat[0:n, b, 2 + c:3 + c]).then_inc(S.p_ready, 1)
                    if i == 0 and h:
                        output(l, h - 1)
                output(l, 3)
                act.wait_ge(S.ob_mm, l + 1)
                root(0, 4, 1.0 / P, 2)

            def output(l, h):
                act.wait_ge(S.o_mm, 4 * l + h + 1)
                act.activation(oat[:, h, :], ps[:, 7, 0:T], ACT.Copy).then_inc(S.o_sb, 1)
                act.wait_ge(S.o_sb, 4 * l + h + 1)
                act.activation(sqT[:, h, :], oat[:, h, :], ACT.Square).then_inc(S.osq_ready, 1)

            def high(g, slot_no, value, parts):
                act.wait_ge(loaded[slot_no], value)
                if parts is not None:
                    act.wait_ge(S.parts_used, parts)
                act.activation(w_hi[:, g % PARTS, :], slot(slot_no), ACT.Copy).then_inc(S.hi_ready, 1)

            def dense_high(j):
                k = MIXN + j
                high(j, slot_of[k], 16 * load_value[k], j - PARTS + 1 if j >= PARTS else None)

            for l in range(DEPTH):
                act.wait_ge(S.h_ready, DC * (2 * l + 1))
                act.dma_start(lora_w[0:32, :], A["tm_w_decay_up"][l]).then_inc(S.lora_w_in, 16)
                act.dma_start(lora_w[32:64, :], A["tm_w_a_up"][l]).then_inc(S.lora_w_in, 16)
                act.dma_start(lora_w[64:128, :], A["tm_w_g_up"][l]).then_inc(S.lora_w_in, 16)
                squares(2 * l)
                norm_root(2 * l)
                if l == 0:
                    lambdas()
                for n in range(0, NCH, 2):
                    act.wait_ge(S.proj_mm, NCH * l + n + 1)
                    act.activation(projT[:, n, 2:T + 2], ps[:, 0, 0:T], ACT.Copy).then_inc(S.proj_act, 1)
                    if n == 6:
                        rwkv_lora(l)
                    if n == 10:
                        rwkv_lora_out(l)
                    if n == 16:
                        rwkv_exp(l)
                        act.wait_ge(S.kk_max, l + 1)
                        act.activation(msT[:, 0:2 * T], msT[:, 0:2 * T], ACT.Sqrt).then_inc(S.root_ready, 1)
                rwkv_tok(l)
                for i in range(3):
                    rwkv_levels(l, i)
                group_norm(l)
                attention(l)
                squares(2 * l + 1)
                if l == 0:
                    dense_high(0)
                    norm_root(1)
                    dense_high(1)
                    dense_high(2)
                    for c in range(DC):
                        act.wait_ge(S.hn_ready, DC + c + 1)
                        act.activation(xd_hi[:, c, :], hnT[:, c, :], ACT.Copy).then_inc(S.xd_hi_ready, 1)
                    for j in range(FFNN):
                        s = j // 2
                        if j % 2 and s < FC // 2:
                            act.wait_ge(S.parts_used, j + 1)
                            if s >= 2:
                                act.wait_ge(S.hd_lo_ready, s - 1)
                            b = 4 * (s % 2)
                            act.activation(sgd[:, s % 2], ps[:, b:b + 2, 0:T], ACT.Silu).then_inc(S.silu_ready, 1)
                        if j + PARTS < FFNN:
                            dense_high(j + PARTS)
                        if j % 2 and s < FC // 2:
                            act.wait_ge(S.hid_prod, s + 1)
                            act.activation(hd_hi[:, 2 * s:2 * s + 2, :], hmd[:, s % 2],
                                           ACT.Copy).then_inc(S.hd_hi_ready, 1)
                else:
                    norm_root(3)

            def item_high(i, j):
                q = j % BIG_RING
                high(j, q, i * (16 * per_item[q]) + 16 * (filled[q] + j // BIG_RING + 1),
                     i * FFNN + (FFNN + j - PARTS + 1))

            for k in range(0, 6, 2):
                act.wait_ge(S.hntok_mm, k + 1)
                i = k // 2
                n = TILES[i][1]
                act.activation(hnTok[0:n, i, 0:512], ps[0:n, 2, :], ACT.Copy).then_inc(S.hntok_ready, 1)
                act.wait_ge(S.hntok_mm, k + 2)
                act.activation(hnTok[0:n, i, 512:1024], ps[0:n, 3, :], ACT.Copy).then_inc(S.hntok_ready, 1)
            act.wait_ge(S.gap_ready, 1)
            act.activation(gw[:, :, 1], gw[:, :, 1], ACT.Exp).then_inc(S.gap_exp, 1)
            for j in range(PARTS):
                item_high(0, j)

            def gathered_high(i):
                for half in range(2):
                    act.wait_ge(S.gather_mm, 2 * i + (half + 1))
                    act.activation(xm_hi[:, 4 * half:4 * half + 4, :],
                                   ps[:, 4 + half, 0:4 * CAP].rearrange("p (c t) -> p c t", c=4),
                                   ACT.Copy).then_inc(S.xm_hi_ready, 1)

            def slots_turned(i):
                act.wait_ge(S.oht_mm, i + 1)
                act.activation(ohT[0:CAP, :], ps[0:CAP, 6, 0:T], ACT.Copy).then_inc(S.oht_ready, 1)

            gathered_high(0)
            slots_turned(0)
            act.wait_ge(S.table_ready, 1)
            n_items = act.value_load(ntab[0:1, 0:1], min_val=NE, max_val=NE + MAXO)
            with act.Fori(0, n_items) as i:
                for j in range(FFNN):
                    s = j // 2
                    if j + PARTS < FFNN:
                        item_high(i, j + PARTS)
                    elif j < FFNN - 1:
                        item_high(i + 1, j + PARTS - FFNN)
                    if j % 2 and s < FC // 2:
                        act.wait_ge(S.parts_used, i * FFNN + (FFNN + j + 1))
                        if s >= 2:
                            act.wait_ge(S.mhid_prod, i * (FC // 2) + (s - 1))
                        act.activation(sgm[0:CAP, s % 2, :], ps[0:CAP, s % 2, 0:PIECE],
                                       ACT.Silu).then_inc(S.msilu_ready, 1)
                    if j % 2 and 1 <= s <= FC // 2:
                        act.wait_ge(S.ht_mm, i * (FC // 2) + s)
                        act.activation(hm_hi[:, 2 * s - 2:2 * s, :],
                                       ps[:, 4 + (s - 1) % 2, 0:2 * CAP].rearrange("p (c t) -> p c t", c=2),
                                       ACT.Copy).then_inc(S.hm_hi_ready, 1)
                act.wait_ge(S.parts_used, i * FFNN + 2 * FFNN)
                for z in range(2):
                    act.activation(y_hi[0:CAP, 512 * z:512 * z + 512], ps[0:CAP, 6 + z, :], ACT.Copy,
                                   scale=gslot[0:CAP, :]).then_inc(S.y_hi_ready, 1)
                item_high(i + 1, PARTS - 1)
                gathered_high(i + 1)
                slots_turned(i + 1)
            for i, (t0, n) in enumerate(TILES):
                act.wait_ge(S.out_mm, 2 * i + 1)
                act.activation(xTok[0:n, i, 0:512], ps[0:n, 2 * (i % 2), :], ACT.Copy).then_inc(S.out_act, 1)

        @block.vector
        def _(dve):
            done = [0]

            def step(ins):
                done[0] += 1
                ins.then_inc(S.dve_chain, 1)
                dve.wait_ge(S.dve_chain, done[0])

            def inverse(k, n):
                dve.wait_ge(S.root_ready, k)
                dve.reciprocal(rsT[:, 0:n * T], msT[:, 0:n * T]).then_inc(S.rs_ready, 1)
                dve.wait_ge(S.rs_ready, k)

            def rs(n):
                return rsT[:, 0:n * T].rearrange("p (c t) -> p c t", c=n)

            def norm(idx, g):
                l = idx // 2
                inverse(NORMS * l + (1 if idx % 2 == 0 else 7), 1)
                for c in range(DC):
                    dve.scalar_tensor_tensor(out=hnT[:, c, :], in0=hT[:, c, :], scalar=vc(l, g + c), in1=rsT[:, 0:T],
                                             op0=ALU.mult, op1=ALU.mult).then_inc(S.hn_ready, 1)

            def hx(l, c):
                dve.scalar_tensor_tensor(out=hxT[:, c, :], in0=sqT[:, c, :], scalar=vc(l, MU + c),
                                         in1=cur(c)[:, 0, :], op0=ALU.mult, op1=ALU.add).then_inc(S.hx_ready, 1)

            R, K, V = hxT[:, 0:2, :], hxT[:, 2:4, :], hxT[:, 4:6, :]

            def prep(l, n):
                if n == 5:
                    dve.wait_ge(S.shift_d, l + 1)
                    hx(l, 6)
                if n == 7:
                    hx(l, 2)
                    hx(l, 3)
                    dve.wait_ge(S.lora_act, 3 * l + 2)
                    dve.tensor_scalar(lora[64:128, :], lora[64:128, :], 0.5, 0.5, ALU.mult,
                                      ALU.add).then_inc(S.lora_sig, 1)
                if n == 9:
                    for c in (0, 1, 4, 5):
                        hx(l, c)
                if n == 11:
                    dve.wait_ge(S.lora_out, 5 * l + 4)
                    step(dve.tensor_scalar(eT, eT, 0.5 * E_HALF, 0.5 * E_HALF, ALU.mult, ALU.add))
                    step(dve.tensor_scalar(aT, aT, 0.5, 0.5, ALU.mult, ALU.add))
                    for p in range(2):
                        step(dve.tensor_tensor_scan(cumT[:, p, :], resetT, eT[:, p, :], 0.0, ALU.mult, ALU.add))
                if n == 13:
                    dve.tensor_tensor(AtT, cumT, eT, ALU.subtract)
                    for p in range(2):
                        c32 = cumT[:, p, 0:256].rearrange("p (c t) -> p c t", t=CH)
                        ins = dve.tensor_tensor(KhT[:, p, 0:256].rearrange("p (c t) -> p c t", t=CH), c32,
                                                c32[:, :, CH - 1:CH].broadcast_to([P, 8, CH]), ALU.subtract)
                    ins.then_inc(S.decay_ready, 1)
                    dve.wait_ge(S.hx_ready, 7 * l + 7)
                    for p in range(2):
                        step(dve.tensor_scalar(kkT[:, p, :], K[:, p, :], vc(l, KK + p), None, ALU.mult))
                    dve.tensor_tensor(kks, kkT, kkT, ALU.mult).then_inc(S.kk_sq, 1)
                if n == 15:
                    for p in range(2):
                        step(dve.tensor_scalar(bT[:, p, :], aT[:, p, :], -1.0, vc(l, KA + p), ALU.add, ALU.mult))
                    step(dve.scalar_tensor_tensor(out=K, in0=bT, scalar=1.0, in1=K, op0=ALU.add, op1=ALU.mult))
                    dve.wait_ge(S.kk_mm, l + 1)
                    dve.tensor_scalar(msT[:, 0:2 * T].rearrange("p (c t) -> p c t", c=2), ps[:, 2:4, 0:T], 1e-24, None,
                                      ALU.max).then_inc(S.kk_max, 1)
                if n == 17:
                    for p in range(2):
                        ins = dve.scalar_tensor_tensor(out=bonusT[:, p, :], in0=R[:, p, :], scalar=vc(l, RK + p),
                                                       in1=K[:, p, :], op0=ALU.mult, op1=ALU.mult)
                    ins.then_inc(S.bonus_pre, 1)
                    inverse(NORMS * l + 2, 2)
                    step(dve.tensor_tensor(kkT, kkT, rs(2), ALU.mult))
                    step(dve.tensor_tensor(bT, kkT, aT, ALU.mult))
                if n == 19:
                    dve.wait_ge(S.exp_ready, 4 * l + 4)
                    dve.scalar_tensor_tensor(out=AtT, in0=kkT, scalar=-1.0, in1=AtT, op0=ALU.mult,
                                             op1=ALU.mult).then_inc(S.til_ready, 1)
                    dve.tensor_tensor(BtT, bT, KtT, ALU.mult).then_inc(S.til_ready, 1)
                    dve.tensor_tensor(RtT, R, PtT, ALU.mult).then_inc(S.til_ready, 1)
                if n == 21:
                    dve.wait_ge(S.til_ready, 6 * l + 2)
                    dve.tensor_tensor(KtT, K, KtT, ALU.mult).then_inc(S.til_ready, 1)
                    dve.wait_ge(S.bonus_mm, l + 1)
                    dve.tensor_tensor(bonusT, ps[:, 4:6, 0:T], V, ALU.mult)
                if n == 23:
                    dve.tensor_tensor(bT[:, :, 0:256], bT[:, :, 0:256], KhT[:, :, 0:256],
                                      ALU.mult).then_inc(S.til_ready, 1)
                    dve.tensor_tensor(KhT[:, :, 0:256], K[:, :, 0:256], KhT[:, :, 0:256],
                                      ALU.mult).then_inc(S.til_ready, 1)

            def quad(bank, n):
                return ps[0:n, bank, :].rearrange("p (h t) -> p h t", h=4)[:, :, 0:n]

            def masked(dst, bank, mask, n):
                for q in range(2):
                    ins = dve.tensor_tensor(dst[0:n, q::2, 0:n],
                                            ps[0:n, bank + q, 0:256].rearrange("p (a t) -> p a t", a=2)[:, :, 0:n],
                                            bc(mask[0:n, 0:n], 2), ALU.mult)
                ins.then_inc(S.mat_ev, 1)

            def matrices(l, i):
                n = TILES[i][1]
                g = 3 * l + i
                at = 5 * g
                dve.wait_ge(S.mat_mm, at + 1)
                masked(mt16, 2, C.m16t, n)
                dve.wait_ge(S.mat_mm, at + 2)
                masked(m16, 4, C.m16, n)
                masked(moff, 4, C.moff, n)
                dve.wait_ge(S.mat_ev, 6 * g + 1)
                dve.tensor_tensor(qm[0:n, :, 0:n], mt16[0:n, :, 0:n], bc(C.ident[0:n, 0:n], 4),
                                  ALU.add).then_inc(S.q1_ready, 1)
                dve.wait_ge(S.mat_mm, at + 3)
                masked(ntm, 6, C.m32s, n)
                dve.wait_ge(S.mat_mm, at + 4)
                masked(rbm[i], 2, C.m32i, n)
                dve.wait_ge(S.mat_mm, at + 5)
                masked(rkm[i], 2, C.m32i, n)
                lm, ld = lvl(LVM, l, i), lvl(LVD, l, i)

                def add_to_q(need, have):
                    dve.wait_ge(S.lvl_mm, lm + need)
                    if have:
                        dve.wait_ge(S.lvl_dve, ld + have)
                    dve.tensor_tensor(qm[0:n, :, 0:n], quad(6, n), qm[0:n, :, 0:n], ALU.add).then_inc(S.lvl_dve, 1)

                add_to_q(3, 0)
                add_to_q(6, 1)
                add_to_q(8, 2)
                if i < 2:
                    dve.wait_ge(S.lvl_mm, lm + 10)
                    dve.tensor_copy(m16[0:n, :, 0:n], quad(5, n)).then_inc(S.lvl_dve, 1)
                    add_to_q(11, 3)
                dve.wait_ge(S.wt_mm, 3 * g + 2)
                dve.tensor_copy(nv[0:n, :], ps[0:n, 5, 0:256]).then_inc(S.nv_ready, 1)

            def chain(l):
                dve.wait_ge(S.wt_act, 6 * l + 6)
                for c in range(NCHUNK):
                    i, r, n = c // 4, CH * (c % 4), min(CH, T - CH * c)
                    if c == 0:
                        dve.tensor_copy(uTok[0:n, 0, :], zTok[0:n, 0, :]).then_inc(S.u_ready, 1)
                    else:
                        dve.wait_ge(S.u_mm, 8 * l + c)
                        for q in range(2):
                            u, z = (x[r:r + n, i, :].rearrange("p (a q v) -> p q a v", q=2, v=NR)[:, q]
                                    for x in (uTok, zTok))
                            ins = dve.tensor_tensor(u, ps[r:r + n, 2 + q, 0:128].rearrange("p (a v) -> p a v", a=2), z,
                                                    ALU.add)
                        ins.then_inc(S.u_ready, 1)
                    if c == NCHUNK - 1:
                        break
                    new = ps[:, 0, 0:2 * NR].rearrange("p (a v) -> p a v", a=2)
                    if c == 0:
                        dve.wait_ge(S.st_mm, 8 * l + 1)
                        dve.tensor_copy(stT[:, 1], new).then_inc(S.st_ready, 1)
                    else:
                        step(dve.tensor_tensor(pst, stT[:, c], tail(PtT[:, :, CH * c + CH - 1], NR), ALU.mult))
                        dve.wait_ge(S.st_mm, 8 * l + c + 1)
                        dve.tensor_tensor(stT[:, c + 1], new, pst, ALU.add).then_inc(S.st_ready, 1)
                    dve.wait_ge(S.st_ready, 8 * l + c + 1)

            def group_norm(l):
                dve.wait_ge(S.gn_mm, 2 * l + 1)
                dve.scalar_tensor_tensor(out=eT, in0=ps[:, 0:2, 0:T], scalar=-1.0 / NR, in1=eT, op0=ALU.mult,
                                         op1=ALU.add).then_inc(S.gn_cent, 1)
                inverse(NORMS * l + 3, 2)
                step(dve.tensor_tensor(eT, eT, rs(2), ALU.mult))
                for p in range(2):
                    step(dve.tensor_scalar(eT[:, p, :], eT[:, p, :], vc(l, GNG + p), vc(l, GNB + p), ALU.mult, ALU.add))
                step(dve.tensor_tensor(eT, eT, bonusT, ALU.add))
                dve.tensor_tensor(oT[:, 0:2, :], eT, gT, ALU.mult).then_inc(S.oa_ready, 1)

            def qk_norm_rope(l):
                for k in range(2):
                    x = cur(Q_CH + 4 * k, 4)
                    y = hnT[:, 4 * k:4 * k + 4, :]
                    dve.wait_ge(S.rot_mm, 2 * l + k + 1)
                    dve.wait_ge(S.qcos_ready, 2 * l + k + 1)
                    step(dve.tensor_tensor(y, ps[:, 4 * k:4 * k + 4, 0:T], bc(sinT, 4), ALU.mult))
                    step(dve.tensor_tensor(x, x, y, ALU.add))
                    inverse(NORMS * l + 4 + k, 4)
                    dve.tensor_tensor(x, x, rs(4), ALU.mult).then_inc(S.qk_ready, 1)

            def softmax(l):
                def maxima(u):
                    i = u % 3
                    t0, n = TILES[i]
                    b, m = u % 2, t0 + n
                    dve.wait_ge(S.sc_mm, 12 * l + u + 1)
                    step(dve.tensor_reduce(stat[0:n, b, 4:6], ps[0:n, 2 * b:2 * b + 2, 0:m], AXX, ALU.max))
                    dve.tensor_scalar(stat[0:n, b, 0:2], stat[0:n, b, 4:6], -DK ** -0.5, None,
                                      ALU.mult).then_inc(S.mx_ready, 1)

                def difference(u):
                    i = u % 3
                    t0, n = TILES[i]
                    b, m = u % 2, t0 + n
                    dve.wait_ge(S.p_ready, 24 * l + 2 * u + 2)
                    step(dve.reciprocal(stat[0:n, b, 2:4], stat[0:n, b, 2:4]))
                    step(dve.tensor_scalar(stat[0:n, b, 3:4], stat[0:n, b, 3:4], small[0:n, 6 + l:7 + l], None, ALU.mult))
                    step(dve.tensor_scalar(scaled[0:n, 0:m], prob[0:n, b, 1, 0:m], stat[0:n, b, 3:4], None, ALU.mult))
                    if u >= 2:
                        dve.wait_ge(S.pt_mm, 12 * l + u - 1)
                    dve.scalar_tensor_tensor(out=pd[0:n, b, 0:m], in0=prob[0:n, b, 0, 0:m], scalar=stat[0:n, b, 2:3],
                                             in1=scaled[0:n, 0:m], op0=ALU.mult,
                                             op1=ALU.subtract).then_inc(S.pd_ready, 1)

                def turned(u):
                    h, i = u // 3, u % 3
                    t0, n = TILES[i]
                    dve.wait_ge(S.pt_mm, 12 * l + u + 1)
                    if i == 0 and h >= 2:
                        dve.wait_ge(S.o_mm, 4 * l + h - 1)
                    w = min(i + 1, 2)
                    ins = dve.tensor_copy(pT[:, h % 2, 0:w, t0:t0 + n],
                                          ps[:, 6, :].rearrange("p (k t) -> p k t", t=P)[:, 0:w, 0:n])
                    if i == 2:
                        ins = dve.tensor_copy(pT[0:n, h % 2, 2, t0:t0 + n], ps[0:n, 6, 2 * P:2 * P + n])
                    ins.then_inc(S.pt_ready, 1)

                for u in range(14):
                    if u < 12:
                        maxima(u)
                    if 1 <= u < 13:
                        difference(u - 1)
                    if u >= 2:
                        turned(u - 2)
                inverse(NORMS * l + 6, 4)
                dve.scalar_tensor_tensor(out=oT[:, 2:6, :], in0=oat, scalar=small[:, 8 + l:9 + l], in1=rs(4),
                                         op0=ALU.mult, op1=ALU.mult).then_inc(S.ob_ready, 1)

            def low(g, slot_no):
                dve.tensor_tensor(w_lo[:, g % PARTS, :], slot(slot_no), w_hi[:, g % PARTS, :],
                                  ALU.subtract).then_inc(S.lo_ready, 1)

            def dense_low(j):
                dve.wait_ge(S.hi_ready, j + 1)
                low(j, slot_of[MIXN + j])

            def item_low(i, j):
                dve.wait_ge(S.hi_ready, i * FFNN + (FFNN + j + 1))
                low(j, j % BIG_RING)

            for c in range(DC):
                dve.wait_ge(S.x_mm, c + 1)
                dve.tensor_copy(hT[:, c, :], ps[:, c % 2, 0:T]).then_inc(S.h_ready, 1)
            dve.wait_ge(S.vcol_mm, 1)
            dve.tensor_copy(vcol[:], ps[:, 2, 0:DEPTH * ROWS]).then_inc(S.vcol_ready, 1)
            dve.wait_ge(S.vcol_ready, 1)
            for l in range(DEPTH):
                dve.tensor_scalar(vhalf[:, l, :], vc(l, W0, 4), 0.5, None, ALU.mult).then_inc(S.vhalf_ready, 1)
                dve.tensor_scalar(small[:, 8 + l:9 + l], vc(l, SUBG), 1.0 - LAM_INIT[l], None, ALU.mult)
                dve.tensor_tensor(small[:, l:l + 1], vc(l, LAMQ), vc(l, LAMK), ALU.mult).then_inc(S.lam_prod, 1)
            dve.wait_ge(S.lam_exp, 2)
            step(dve.tensor_tensor(small[:, 6:8], small[:, 2:4], small[:, 4:6], ALU.subtract))
            for l in range(DEPTH):
                step(dve.tensor_scalar(small[:, 6 + l:7 + l], small[:, 6 + l:7 + l], LAM_INIT[l], None, ALU.add))

            for l in range(DEPTH):
                norm(2 * l, MIXG)
                for n in range(1, NCH, 2):
                    dve.wait_ge(S.proj_mm, NCH * l + n + 1)
                    dve.tensor_copy(projT[:, n, 2:T + 2], ps[:, 1, 0:T]).then_inc(S.proj_dve, 1)
                    prep(l, n)
                for i in range(3):
                    matrices(l, i)
                chain(l)
                group_norm(l)
                qk_norm_rope(l)
                softmax(l)
                for c in range(DC):
                    dve.wait_ge(S.wout_mm, DC * l + c + 1)
                    dve.tensor_tensor(hT[:, c, :], ps[:, c % 2, 0:T], hT[:, c, :], ALU.add).then_inc(S.h_ready, 1)
                norm(2 * l + 1, FFNG)
                if l == 0:
                    dense_low(0)
                    for c in range(DC):
                        dve.wait_ge(S.xd_hi_ready, c + 1)
                        dve.tensor_tensor(xd_lo[:, c, :], hnT[:, c, :], xd_hi[:, c, :],
                                          ALU.subtract).then_inc(S.xd_lo_ready, 1)
                    dense_low(1)
                    dense_low(2)
                    for j in range(FFNN):
                        s = j // 2
                        if j % 2 and s < FC // 2:
                            b = 4 * (s % 2) + 2
                            dve.wait_ge(S.silu_ready, s + 1)
                            dve.tensor_tensor(hmd[:, s % 2], ps[:, b:b + 2, 0:T], sgd[:, s % 2],
                                              ALU.mult).then_inc(S.hid_prod, 1)
                        if j + PARTS < FFNN:
                            dense_low(j + PARTS)
                        if j % 2 and s < FC // 2:
                            dve.wait_ge(S.hd_hi_ready, s + 1)
                            dve.tensor_tensor(hd_lo[:, 2 * s:2 * s + 2, :], hmd[:, s % 2], hd_hi[:, 2 * s:2 * s + 2, :],
                                              ALU.subtract).then_inc(S.hd_lo_ready, 1)
                    for c in range(DC):
                        if c < DC - 1:
                            dve.wait_ge(S.down_mm, c + 1)
                        else:
                            dve.wait_ge(S.parts_used, FFNN)
                        dve.tensor_tensor(hT[:, c, :], ps[:, c, 0:T], hT[:, c, :], ALU.add).then_inc(S.h_ready, 1)

            step(dve.memset(lgS, 0.0))
            dve.wait_ge(S.lg_mm, 1)
            step(dve.tensor_copy(lgS[:, 0:2, :], ps[:, 0, 0:2 * NE].rearrange("p (i e) -> p i e", e=NE)))
            step(dve.tensor_copy(lgS[0:META, 2, :], ps[0:META, 0, 2 * NE:3 * NE]))
            for i in range(3):
                step(dve.max(top8[:, i, :], lgS[:, i, :]))
                step(dve.max_index(idx8[:, i, :], top8[:, i, :], lgS[:, i, :]))
            dve.tensor_tensor(gw[:, :, 1], top8[:, :, 1], top8[:, :, 0], ALU.subtract).then_inc(S.gap_ready, 1)
            step(dve.tensor_copy(fidx, idx8[:, :, 0:2]))
            for j, oh in ((0, oh1), (1, oh2)):
                step(dve.tensor_tensor(oh, bc(iotaT[:, 0:NE], 3), tail(fidx[:, :, j], NE), ALU.is_equal))
            dve.tensor_tensor(sel, oh1, oh2, ALU.add).then_inc(S.sel_ready, 1)
            dve.wait_ge(S.gap_exp, 1)
            step(dve.tensor_scalar(gw[:, :, 0], gw[:, :, 1], 1.0, None, ALU.add))
            step(dve.reciprocal(gw[:, :, 0], gw[:, :, 0]))
            step(dve.tensor_tensor(gw[:, :, 1], gw[:, :, 1], gw[:, :, 0], ALU.mult))
            for j, oh in ((0, oh1), (1, oh2)):
                step(dve.tensor_tensor(oh, oh, tail(gw[:, :, j], NE), ALU.mult))
            step(dve.tensor_tensor(gates, oh1, oh2, ALU.add))
            dve.wait_ge(S.pos_mm, 1)
            step(dve.memset(posx, 0.0))
            step(dve.tensor_copy(posx[:, 0:2, :], ps[:, 1, 0:2 * NE].rearrange("p (i e) -> p i e", e=NE)))
            step(dve.tensor_copy(posx[0:META, 2, :], ps[0:META, 1, 2 * NE:3 * NE]))
            step(dve.scalar_tensor_tensor(out=posx, in0=posx, scalar=1.0, in1=sel, op0=ALU.add, op1=ALU.mult))
            step(dve.tensor_scalar(posx, posx, -1.0, None, ALU.add))
            step(dve.tensor_copy(cnt[0:1, 0:NE], ps[0:1, 1, 3 * NE:4 * NE]))
            for r in range(NFLAG // NE):
                step(dve.tensor_scalar(flag[0:1, NE * r:NE * r + NE], cnt[0:1, 0:NE], float(CAP * (r + 1)), None,
                                       ALU.is_gt))
                step(dve.tensor_copy(ev[0:1, NE * r:NE * r + NE], iotaT[0:1, 0:NE]))
                step(dve.memset(ov[0:1, NE * r:NE * r + NE], float(CAP * (r + 1))))
            step(dve.tensor_tensor_scan(incl[0:1, :], C.ones[0:1, 0:NFLAG], flag[0:1, :], 0.0, ALU.mult, ALU.add))
            step(dve.memset(fsum[:], 0.0))
            step(dve.tensor_scalar(fsum[0:1, 1, NIT - 1:NIT], incl[0:1, NFLAG - 1:NFLAG], float(NE), None, ALU.add))
            step(dve.tensor_copy(ntab[:], fsum[0:1, 1, NIT - 1:NIT]))
            step(dve.memset(fsum[0:1, 1, NIT - 1:NIT], 0.0))
            step(dve.tensor_tensor(incl[0:1, :], incl[0:1, :], flag[0:1, :], ALU.mult))
            step(dve.tensor_tensor(eqg[0:1], bc(incl[0:1, :], MAXO), tail(iotaT[0:1, 1:1 + MAXO], NFLAG), ALU.is_equal))
            step(dve.tensor_copy(fsum[0:1, 0, 0:NE], iotaT[0:1, 0:NE]))
            for row, values in ((0, ev), (1, ov)):
                step(dve.tensor_tensor(pick[0:1], eqg[0:1], bc(values[0:1, :], MAXO), ALU.mult))
                step(dve.tensor_reduce(fsum[0:1, row, NE:NE + MAXO], pick[0:1], AXX, ALU.add))
            dve.tensor_copy(tab[:], fsum[:]).then_inc(S.table_ready, 1)
            dve.wait_ge(S.table_ready, 1)

            def one_hot(k):
                e = dve.value_load(tab[0:1, 0, bass.ds(k, 1)], min_val=0, max_val=NE - 1)
                first = dve.value_load(tab[0:1, 1, bass.ds(k, 1)], min_val=0, max_val=wide - CAP)
                for i, (t0, n) in enumerate(TILES):
                    dve.tensor_scalar(oneh[0:n, i, :], iotaT[0:n, bass.ds(first, CAP)], posx[0:n, i, bass.ds(e, 1)],
                                      None, ALU.is_equal)
                dve.tensor_copy(gsel, gates[:, :, bass.ds(e, 1)]).then_inc(S.oneh_ready, 1)

            def gathered_low(i):
                for half in range(2):
                    dve.wait_ge(S.xm_hi_ready, 2 * i + (half + 1))
                    dve.tensor_tensor(xm_lo[:, 4 * half:4 * half + 4, :],
                                      ps[:, 4 + half, 0:4 * CAP].rearrange("p (c t) -> p c t", c=4),
                                      xm_hi[:, 4 * half:4 * half + 4, :], ALU.subtract).then_inc(S.xm_lo_ready, 1)

            def slot_gates(i):
                dve.wait_ge(S.gslot_mm, i + 1)
                dve.tensor_copy(gslot[0:CAP, :], ps[0:CAP, 7, 0:1]).then_inc(S.gslot_ready, 1)

            one_hot(0)
            for j in range(PARTS):
                item_low(0, j)
            gathered_low(0)
            slot_gates(0)
            n_items = dve.value_load(ntab[0:1, 0:1], min_val=NE, max_val=NE + MAXO)
            with dve.Fori(0, n_items) as i:
                one_hot(i + 1)
                for j in range(FFNN):
                    s = j // 2
                    if j + PARTS < FFNN:
                        item_low(i, j + PARTS)
                    elif j < FFNN - 1:
                        item_low(i + 1, j + PARTS - FFNN)
                    if j % 2 and s < FC // 2:
                        dve.wait_ge(S.msilu_ready, i * (FC // 2) + (s + 1))
                        dve.tensor_tensor(hmTok[0:CAP, s % 2, :], ps[0:CAP, 2 + s % 2, 0:PIECE], sgm[0:CAP, s % 2, :],
                                          ALU.mult).then_inc(S.mhid_prod, 1)
                    if j % 2 and 1 <= s <= FC // 2:
                        dve.wait_ge(S.hm_hi_ready, i * (FC // 2) + s)
                        dve.tensor_tensor(hm_lo[:, 2 * s - 2:2 * s, :],
                                          ps[:, 4 + (s - 1) % 2, 0:2 * CAP].rearrange("p (c t) -> p c t", c=2),
                                          hm_hi[:, 2 * s - 2:2 * s, :], ALU.subtract).then_inc(S.hm_lo_ready, 1)
                for z in range(2):
                    dve.wait_ge(S.y_hi_ready, 2 * i + (z + 1))
                    dve.scalar_tensor_tensor(out=y_lo[0:CAP, 512 * z:512 * z + 512], in0=ps[0:CAP, 6 + z, :],
                                             scalar=gslot[0:CAP, :], in1=y_hi[0:CAP, 512 * z:512 * z + 512],
                                             op0=ALU.mult, op1=ALU.subtract).then_inc(S.y_lo_ready, 1)
                item_low(i + 1, PARTS - 1)
                gathered_low(i + 1)
                for c in range(DC):
                    dve.wait_ge(S.scat_mm, DC * i + (c + 1))
                    dve.tensor_tensor(hT[:, c, :], ps[:, c % 4, 0:T], hT[:, c, :], ALU.add).then_inc(S.h_item, 1)
                slot_gates(i + 1)
            for i, (t0, n) in enumerate(TILES):
                dve.wait_ge(S.out_mm, 2 * i + 2)
                dve.tensor_copy(xTok[0:n, i, 512:1024], ps[0:n, 2 * (i % 2) + 1, :]).then_inc(S.out_dve, 1)

        @block.tensor
        def _(pe):
            mm = pe.matmul

            def group(out, pairs, start=True, stop=True, **kw):
                pairs = list(pairs)
                for k, (a, b) in enumerate(pairs):
                    ins = mm(out, a, b, start=start and k == 0, stop=stop and k == len(pairs) - 1, **kw)
                return ins

            def piece_view(k, n):
                return slot(slot_of[k])[:, 0:DC * n].rearrange("p (c n) -> p c n", c=DC)

            def norm_sum(idx):
                for c in range(DC):
                    if c % 4 == 0:
                        pe.wait_ge(S.sq_ready, 2 * idx + c // 4 + 1)
                    ins = mm(ps[:, 7, 0:T], C.ones, sqT[:, c, :], start=c == 0, stop=c == DC - 1)
                ins.then_inc(S.nsum_mm, 1)

            def project(l, n):
                k = (MIXN + FFNN) * l + n // 2
                width = min(PIECE, IN_COLS - PIECE * (n // 2))
                w = piece_view(k, width)
                if n % 2 == 0:
                    pe.wait_ge(loaded[slot_of[k]], 16 * load_value[k])
                    if n:
                        pe.wait_ge(S.proj_act, 13 * l + n // 2)
                elif n > 1:
                    pe.wait_ge(S.proj_dve, 12 * l + n // 2)
                for c in range(DC):
                    if n == 0:
                        pe.wait_ge(S.hn_ready, 2 * DC * l + c + 1)
                    ins = mm(ps[:, n % 2, 0:T], w[:, c, P * (n % 2):P * (n % 2) + P], hnT[:, c, :],
                             start=c == 0, stop=c == DC - 1)
                ins.then_inc(S.proj_mm, 1)

            def rwkv_lora(l):
                pe.wait_ge(S.lora_w_in, 48 * (l + 1))
                pe.wait_ge(S.lora_act, 3 * l + 3)
                pe.wait_ge(S.lora_sig, l + 1)
                for k, (a, b) in enumerate(((0, 32), (32, 64), (64, 128))):
                    for p in range(2):
                        ins = mm(ps[:, 2 + 2 * k + p, 0:T], lora_w[a:b, P * p:P * p + P], lora[a:b, :],
                                 start=True, stop=True)
                    ins.then_inc(S.lora_mm, 1)

            def head_sums(bank, x, signal):
                for p in range(x.shape[1]):
                    ins = mm(ps[:, bank + p, 0:T], C.blk, x[:, p, :], start=True, stop=True)
                ins.then_inc(signal, 1)

            def token_rows(l):
                V = hxT[:, 4:6, :]
                k = 0
                for i, (t0, n) in enumerate(TILES):
                    for bank, (x, y) in ((2, (AtT, V)), (3, (bT, KhT)))[:2 if i < 2 else 1]:
                        if k == 0:
                            pe.wait_ge(S.til_ready, 6 * l + 6)
                        if i:
                            pe.wait_ge(S.tok_ready, 5 * l + k - 1)
                        for j, z in enumerate((x, y)):
                            for p in range(2):
                                ins = pe.transpose(ps[0:n, bank, 256 * j + P * p:256 * j + P * p + P],
                                                   z[:, p, t0:t0 + n], C.ident)
                        ins.then_inc(S.tok_mm, 1)
                        k += 1

            def matrices(l, i):
                t0, n = TILES[i]
                g = 3 * l + i
                lm, la, ld = lvl(LVM, l, i), lvl(LVA, l, i), lvl(LVD, l, i)

                def products(bank, x, y):
                    for p in range(2):
                        for q in range(2):
                            ins = mm(ps[0:n, bank + q, P * p:P * p + n], x[64 * q:64 * q + 64, p, t0:t0 + n],
                                     y[64 * q:64 * q + 64, p, t0:t0 + n], start=True, stop=True)
                    ins.then_inc(S.mat_mm, 1)

                def quad(bank, x, y):
                    for h in range(4):
                        ins = mm(ps[0:n, bank, P * h:P * h + n], x[0:n, h, 0:n], y[0:n, h, 0:n], start=True, stop=True)
                    ins.then_inc(S.lvl_mm, 1)

                pe.wait_ge(S.tok_ready, 5 * l + 5)
                if i:
                    pe.wait_ge(S.wt_act, 2 * g)
                    pe.wait_ge(S.mat_ev, 6 * g)
                    pe.wait_ge(S.nv_ready, g)
                products(2, BtT, AtT)
                products(4, AtT, BtT)
                products(6, KtT, AtT)
                pe.wait_ge(S.mat_ev, 6 * g + 1)
                products(2, BtT, RtT)
                pe.wait_ge(S.mat_ev, 6 * g + 3)
                quad(4, m16, mt16)
                quad(5, mt16, m16)
                pe.wait_ge(S.mat_ev, 6 * g + 5)
                products(2, KtT, RtT)
                pe.wait_ge(S.q1_ready, g + 1)
                pe.wait_ge(S.lvl_act, la + 2)
                quad(6, m2, qm)
                quad(4, m2, mt2)
                quad(5, mt2, m2)
                pe.wait_ge(S.lvl_act, la + 4)
                pe.wait_ge(S.lvl_dve, ld + 1)
                quad(6, m16, qm)
                quad(5, mt16, m16)
                pe.wait_ge(S.lvl_act, la + 5)
                pe.wait_ge(S.lvl_dve, ld + 2)
                quad(6, m2, qm)
                if i < 2:
                    pe.wait_ge(S.lvl_dve, ld + 3)
                    for h in range(4):
                        ins = pe.transpose(ps[0:n, 4, P * h:P * h + n], qm[0:n, h, 0:n], C.ident[0:n, 0:n])
                    ins.then_inc(S.lvl_mm, 1)
                    quad(5, moff, qm)
                    pe.wait_ge(S.lvl_act, la + 6)
                    pe.wait_ge(S.lvl_dve, ld + 4)
                    quad(6, mt2, m16)
                    pe.wait_ge(S.lvl_dve, ld + 5)
                else:
                    pe.wait_ge(S.lvl_dve, ld + 3)
                for h in range(4):
                    p, q = h // 2, 64 * (h % 2)
                    ins = mm(ps[q:q + 64, 4, P * p:P * p + n], tokAV[0:n, i, 0, 64 * h:64 * h + 64], qm[0:n, h, 0:n],
                             start=True, stop=True)
                ins.then_inc(S.wt_mm, 1)
                for h in range(4):
                    ins = mm(ps[0:n, 5, 64 * h:64 * h + 64], ntm[0:n, h, 0:n], tokAV[0:n, i, 1, 64 * h:64 * h + 64],
                             start=True, stop=True)
                ins.then_inc(S.wt_mm, 1)
                pe.wait_ge(S.nv_ready, g + 1)
                for h in range(4):
                    ins = mm(ps[0:n, 6, 64 * h:64 * h + 64], qm[0:n, h, 0:n], nv[0:n, 64 * h:64 * h + 64],
                             start=True, stop=True)
                ins.then_inc(S.wt_mm, 1)

            def chain(l):
                for c in range(NCHUNK):
                    i, r, n = c // 4, CH * (c % 4), min(CH, T - CH * c)
                    if c:
                        pe.wait_ge(S.st_ready, 8 * l + c)
                        for h in range(4):
                            p, q = h // 2, 64 * (h % 2)
                            ins = mm(ps[r:r + n, 2 + h % 2, 64 * p:64 * p + 64], wT[q:q + 64, p, CH * c:CH * c + n],
                                     stT[q:q + 64, c, p, :], start=True, stop=True)
                        ins.then_inc(S.u_mm, 1)
                    if c == NCHUNK - 1:
                        break
                    for h in range(4):
                        p, q = h // 2, 64 * (h % 2)
                        mm(ps[q:q + 64, 0, 64 * p:64 * p + 64], tokBK[r:r + n, i, 1, 64 * h:64 * h + 64],
                           tokAV[r:r + n, i, 1, 64 * h:64 * h + 64], start=p == 0, stop=False, skip_group_check=True)
                    pe.wait_ge(S.u_ready, NCHUNK * l + c + 1)
                    for h in range(4):
                        p, q = h // 2, 64 * (h % 2)
                        ins = mm(ps[q:q + 64, 0, 64 * p:64 * p + 64], tokBK[r:r + n, i, 0, 64 * h:64 * h + 64],
                                 uTok[r:r + n, i, 64 * h:64 * h + 64], start=False, stop=True, skip_group_check=True)
                    ins.then_inc(S.st_mm, 1)

            def outputs(l):
                pe.wait_ge(S.u_ready, NCHUNK * (l + 1))
                for h in range(4):
                    p, q = h // 2, 64 * (h % 2)
                    for i, (t0, n) in enumerate(TILES):
                        mm(ps[q:q + 64, 4 + h, t0:t0 + n], tokAV[0:n, i, 1, 64 * h:64 * h + 64], rkm[i][0:n, h, 0:n],
                           start=i == 0, stop=False, skip_group_check=True)
                        mm(ps[q:q + 64, 4 + h, t0:t0 + n], uTok[0:n, i, 64 * h:64 * h + 64], rbm[i][0:n, h, 0:n],
                           start=False, stop=False, skip_group_check=True)
                    for c in range(1, NCHUNK):
                        t0, n = CH * c, min(CH, T - CH * c)
                        ins = mm(ps[q:q + 64, 4 + h, t0:t0 + n], stT[q:q + 64, c, p, :], RtT[q:q + 64, p, t0:t0 + n],
                                 start=False, stop=True, skip_group_check=True)
                ins.then_inc(S.y_mm, 1)
                pe.wait_ge(S.y_sb, 2 * l + 2)
                head_sums(0, eT, S.gn_mm)
                pe.wait_ge(S.gn_sq, l + 1)
                head_sums(2, cumT, S.gn_mm)

            def attention(l):
                for i, (t0, n) in enumerate(TILES):
                    if i:
                        pe.wait_ge(S.vt_ready, 3 * l + i)
                    else:
                        pe.wait_ge(S.oa_ready, l + 1)
                    for h in range(4):
                        ins = pe.transpose(ps[0:n, 6, P * h:P * h + P], cur(V_CH + h)[:, 0, t0:t0 + n], C.ident)
                    ins.then_inc(S.vt_mm, 1)
                for k in range(2):
                    pe.wait_ge(S.qk_sq, 2 * l + k + 1)
                    if k:
                        pe.wait_ge(S.vt_ready, 3 * l + 3)
                    head_sums(4 * k, sqT[:, 4 * k:4 * k + 4, :], S.qk_mm)
                for k in range(2):
                    pe.wait_ge(S.qg_ready, 8 * l + 4 * k + 4)
                    pe.wait_ge(S.root_ready, NORMS * l + 4 + k)
                    for c in range(4):
                        ins = mm(ps[:, 4 * k + c, 0:T], C.rope, hnT[:, 4 * k + c, :], start=True, stop=True)
                    ins.then_inc(S.rot_mm, 1)

                def scores(u):
                    h, i = u // 3, u % 3
                    t0, n = TILES[i]
                    b, m = u % 2, t0 + n
                    if u >= 2:
                        pe.wait_ge(S.p_ready, 24 * l + 2 * u - 2)
                    for c in range(2):
                        q = 64 * c
                        mm(ps[0:n, 2 * b + c, 0:m], projT[q:q + 64, Q_CH + h, 2 + t0:2 + t0 + n],
                           projT[q:q + 64, K_CH + h, 2:2 + m], start=True, stop=False, skip_group_check=True)
                        ins = mm(ps[0:n, 2 * b + c, t0:m], C.ident[0:n, 0:n], C.causal[0:n, 0:n],
                                 start=False, stop=True, skip_group_check=True)
                    ins.then_inc(S.sc_mm, 1)

                def turn(u):
                    h, i = u // 3, u % 3
                    t0, n = TILES[i]
                    pe.wait_ge(S.pd_ready, 12 * l + u + 1)
                    if u:
                        pe.wait_ge(S.pt_ready, 12 * l + u)
                    for k in range(i + 1):
                        k0, kn = TILES[k]
                        ins = pe.transpose(ps[0:kn, 6, P * k:P * k + n], pd[0:n, u % 2, k0:k0 + kn], C.ident[0:n, 0:n])
                    ins.then_inc(S.pt_mm, 1)

                def values(h):
                    pe.wait_ge(S.pt_ready, 12 * l + 3 * h + 3)
                    if h:
                        pe.wait_ge(S.o_sb, 4 * l + h)
                    for k, (k0, kn) in enumerate(TILES):
                        ins = mm(ps[:, 7, k0:T], vTok[0:kn, k, P * h:P * h + P], pT[0:kn, h % 2, k, k0:T],
                                 start=k == 0, stop=k == 2, skip_group_check=True)
                    ins.then_inc(S.o_mm, 1)

                pe.wait_ge(S.qk_ready, 2 * l + 2)
                for u in range(14):
                    if u < 12:
                        scores(u)
                    if 1 <= u < 13:
                        turn(u - 1)
                    if u >= 3 and u % 3 == 1:
                        values(u // 3 - 1)
                pe.wait_ge(S.osq_ready, 4 * l + 4)
                for h in range(4):
                    ins = mm(ps[:, h, 0:T], C.ones, sqT[:, h, :], start=True, stop=True)
                ins.then_inc(S.ob_mm, 1)

            def project_out(l):
                pe.wait_ge(S.oa_ready, l + 1)
                pe.wait_ge(S.oc_ready, l + 1)
                pe.wait_ge(S.ob_ready, l + 1)
                for d in range(DC):
                    k = (MIXN + FFNN) * l + -(-IN_COLS // PIECE) + d // 2
                    w = piece_view(k, PIECE)
                    if d % 2 == 0:
                        pe.wait_ge(loaded[slot_of[k]], 16 * load_value[k])
                    if d >= 2:
                        pe.wait_ge(S.h_ready, DC * (2 * l + 1) + d - 1)
                    ins = group(ps[:, d % 2, 0:T], ((w[:, c, P * (d % 2):P * (d % 2) + P], oT[:, c, :])
                                                    for c in range(DC)))
                    ins.then_inc(S.wout_mm, 1)

            def split_products(out, lhs, rhs, first, last, swap=False):
                pairs = ((0, 0), (0, 1), (1, 0))
                for k, (a, b) in enumerate(pairs):
                    ins = mm(out, lhs[a], rhs[b], start=first and k == 0, stop=last and k == 2)
                return ins

            def weights(j, width):
                return [w[:, j % PARTS, :].rearrange("p (c n) -> p c n", n=width) for w in (w_hi, w_lo)]

            pe.wait_ge(S.consts_in, 16)
            pe.wait_ge(S.x_in, 64)
            for c in range(DC):
                if c >= 2:
                    pe.wait_ge(S.h_ready, c - 1)
                for i, (t0, n) in enumerate(TILES):
                    ins = pe.transpose(ps[:, c % 2, t0:t0 + n], xTok[0:n, i, P * c:P * c + P], C.ident[0:n, 0:n])
                ins.then_inc(S.x_mm, 1)
            norm_sum(0)
            pe.wait_ge(S.params_in, 16 * N_PARAMS)
            nr = DEPTH * ROWS
            pe.transpose(ps[:, 2, 0:nr], vrow[0:nr, :], C.ident[0:nr, 0:nr]).then_inc(S.vcol_mm, 1)
            pe.wait_ge(S.lam_prod, DEPTH)
            mm(ps[:, 3, 0:DEPTH], C.ones[0:64, :], small[0:64, 0:DEPTH], start=True, stop=True).then_inc(S.lam_mm, 1)
            mm(ps[:, 4, 0:DEPTH], C.ones[64:P, :], small[64:P, 0:DEPTH], start=True, stop=True).then_inc(S.lam_mm, 1)

            for l in range(DEPTH):
                if l:
                    norm_sum(2 * l)
                for n in range(NCH):
                    project(l, n)
                    if n == 9:
                        if l == 0:
                            pe.wait_ge(S.lam_exp, 2)
                        rwkv_lora(l)
                    if n == 15:
                        pe.wait_ge(S.kk_sq, l + 1)
                        pe.wait_ge(S.lora_out, 5 * l + 5)
                        head_sums(2, kks, S.kk_mm)
                    if n == 19:
                        pe.wait_ge(S.bonus_pre, l + 1)
                        head_sums(4, bonusT, S.bonus_mm)
                token_rows(l)
                for i in range(3):
                    matrices(l, i)
                chain(l)
                outputs(l)
                attention(l)
                project_out(l)
                norm_sum(2 * l + 1)
                if l == 0:
                    for j in range(2 * (FC // 2)):
                        s, z = j // 2, j % 2
                        pe.wait_ge(S.lo_ready, j + 1)
                        w = weights(j, PIECE)
                        if z == 0 and s >= 2:
                            pe.wait_ge(S.hid_prod, s - 1)
                        for half in range(2):
                            for c in range(DC):
                                if j == 0 and half == 0:
                                    pe.wait_ge(S.xd_lo_ready, c + 1)
                                ins = split_products(ps[:, 4 * (s % 2) + 2 * z + half, 0:T],
                                                     [x[:, c, P * half:P * half + P] for x in w],
                                                     [x[:, c, :] for x in (xd_hi, xd_lo)], c == 0, c == DC - 1)
                        ins.then_inc(S.parts_used, 1)
                    for f in range(FC):
                        j = FC + f // 2
                        if f % 2 == 0:
                            pe.wait_ge(S.lo_ready, j + 1)
                            w = weights(j, D)
                        if f == 0:
                            pe.wait_ge(S.hid_prod, FC // 2)
                        if f == FC - 4:
                            pe.wait_ge(S.hd_lo_ready, FC // 2 - 1)
                        if f == FC - 2:
                            pe.wait_ge(S.hd_lo_ready, FC // 2)
                        elif f == 0:
                            pe.wait_ge(S.hd_lo_ready, FC // 2 - 2)
                        for d in range(DC):
                            ins = split_products(ps[:, d, 0:T], [x[:, f % 2, P * d:P * d + P] for x in w],
                                                 [x[:, f, :] for x in (hd_hi, hd_lo)], f == 0, f == FC - 1)
                            if f == FC - 1 and d < DC - 1:
                                ins.then_inc(S.down_mm, 1)
                        if f % 2:
                            ins.then_inc(S.parts_used, 1)

            pe.wait_ge(S.hn_ready, 4 * DC)
            pe.wait_ge(S.router_in, 16)
            for i, (t0, n) in enumerate(TILES):
                ins = group(ps[0:n, 0, NE * i:NE * i + NE], ((hnT[:, c, t0:t0 + n], router[:, c, :])
                                                             for c in range(DC)))
            ins.then_inc(S.lg_mm, 1)
            for k in range(6):
                i, half = k // 2, k % 2
                t0, n = TILES[i]
                if k >= 2:
                    pe.wait_ge(S.hntok_ready, k - 1)
                for c in range(4):
                    ins = pe.transpose(ps[0:n, 2 + half, P * c:P * c + P], hnT[:, 4 * half + c, t0:t0 + n], C.ident)
                ins.then_inc(S.hntok_mm, 1)
            pe.wait_ge(S.sel_ready, 1)
            for i, (t0, n) in enumerate(TILES):
                group(ps[0:n, 1, NE * i:NE * i + NE],
                      [(C.ones[:, 0:n], sel[:, j, :]) for j in range(i)] + [(C.tri[0:n, 0:n], sel[0:n, i, :])])
            group(ps[0:1, 1, 3 * NE:4 * NE], [(C.ones[0:n, 0:1], sel[0:n, i, :]) for i, (t0, n) in enumerate(TILES)]
                  ).then_inc(S.pos_mm, 1)

            pe.wait_ge(S.hntok_ready, 6)
            pe.wait_ge(S.table_ready, 1)

            def gather(i):
                pe.wait_ge(S.oneh_ready, i + 1)
                for c in range(DC):
                    ins = group(ps[:, 4 + c // 4, CAP * (c % 4):CAP * (c % 4) + CAP],
                                ((hnTok[0:n, i, P * c:P * c + P], oneh[0:n, i, :])
                                 for i, (t0, n) in enumerate(TILES)))
                    if c % 4 == 3:
                        ins.then_inc(S.gather_mm, 1)

            def turn_slots():
                for i, (t0, n) in enumerate(TILES):
                    ins = pe.transpose(ps[0:CAP, 6, t0:t0 + n], oneh[0:n, i, :], C.ident[0:n, 0:n])
                ins.then_inc(S.oht_mm, 1)
                group(ps[0:CAP, 7, 0:1], ((oneh[0:n, i, :], gsel[0:n, i, :]) for i, (t0, n) in enumerate(TILES))
                      ).then_inc(S.gslot_mm, 1)

            gather(0)
            turn_slots()
            n_items = pe.value_load(ntab[0:1, 0:1], min_val=NE, max_val=NE + MAXO)
            with pe.Fori(0, n_items) as it:
                pairs = FC // 2
                for j in range(FFNN):
                    pe.wait_ge(S.lo_ready, it * FFNN + (FFNN + j + 1))
                    s, z = j // 2, j % 2
                    if j < 2 * pairs:
                        w = weights(j, PIECE)
                        if z == 0 and s >= 2:
                            pe.wait_ge(S.mhid_prod, it * pairs + (s - 1))
                        for c in range(DC):
                            if j == 0 and c % 4 == 0:
                                pe.wait_ge(S.xm_lo_ready, 2 * it + (c // 4 + 1))
                            ins = split_products(ps[0:CAP, 2 * z + s % 2, 0:PIECE], [x[:, c, :] for x in (xm_hi, xm_lo)],
                                                 [x[:, c, :] for x in w], c == 0, c == DC - 1)
                    else:
                        w = weights(j, D)
                        if j == 2 * pairs:
                            pe.wait_ge(S.oht_ready, it + 1)
                            pe.wait_ge(S.gslot_ready, it + 1)
                        q = j - 2 * pairs
                        pe.wait_ge(S.hm_lo_ready, it * pairs + (q + 1))
                        for f in (2 * q, 2 * q + 1):
                            for y in range(2):
                                ins = split_products(ps[0:CAP, 6 + y, :], [x[:, f, :] for x in (hm_hi, hm_lo)],
                                                     [x[:, f % 2, 512 * y:512 * y + 512] for x in w],
                                                     f == 0, f == FC - 1)
                    ins.then_inc(S.parts_used, 1)
                    if z == 1 and 1 <= s <= pairs:
                        pe.wait_ge(S.mhid_prod, it * pairs + s)
                        if s >= 3:
                            pe.wait_ge(S.hm_lo_ready, it * pairs + (s - 2))
                        for half in range(2):
                            ins = pe.transpose(ps[:, 4 + (s - 1) % 2, CAP * half:CAP * half + CAP],
                                               hmTok[0:CAP, (s - 1) % 2, P * half:P * half + P], C.ident[0:CAP, 0:CAP])
                        ins.then_inc(S.ht_mm, 1)
                gather(it + 1)
                for c in range(DC):
                    if c % 4 == 0:
                        pe.wait_ge(S.y_lo_ready, 2 * it + (c // 4 + 1))
                    if c >= 4:
                        pe.wait_ge(S.h_item, DC * it + (c - 3))
                    for part, y in enumerate((y_hi, y_lo)):
                        ins = mm(ps[:, c % 4, 0:T], y[0:CAP, P * c:P * c + P], ohT[0:CAP, :],
                                 start=part == 0, stop=part == 1)
                    ins.then_inc(S.scat_mm, 1)
                turn_slots()
                pe.wait_ge(S.h_item, DC * it + DC)

            for i, (t0, n) in enumerate(TILES):
                if i == 2:
                    pe.wait_ge(S.out_act, 1)
                    pe.wait_ge(S.out_dve, 1)
                for half in range(2):
                    for c in range(4):
                        ins = pe.transpose(ps[0:n, 2 * (i % 2) + half, P * c:P * c + P], hT[:, 4 * half + c, t0:t0 + n],
                                           C.ident)
                    ins.then_inc(S.out_mm, 1)


N_PARAMS = DEPTH * 20

_OUT = (1, SEQ, D)


def kernel(**inputs):
    import concourse.bacc as _bacc
    from concourse.bass_utils import run_bass_kernel_spmd as _run

    nc = _bacc.Bacc("TRN2", target_bir_lowering=False, num_devices=1)
    arrays, A = {}, {}
    for name, value in list(inputs.items()) + [("consts", constants())]:
        a = np.ascontiguousarray(value)
        arrays[f"in_{name}"] = a
        A[name] = nc.dram_tensor(f"in_{name}", a.shape, mybir.dt.from_np(a.dtype), kind="ExternalInput").ap()
    out = nc.dram_tensor("out_0", _OUT, F32, kind="ExternalOutput").ap()
    build(nc, A, out)
    r = _run(nc, [arrays], core_ids=[0])
    return r.results[0]["out_0"]
```

```python
import math
from collections import namedtuple
from contextlib import ExitStack

import numpy as np

import concourse.bass as bass
from concourse import mybir

F32 = mybir.dt.float32
F32R = mybir.dt.float32r
I32 = mybir.dt.int32
U32 = mybir.dt.uint32
ALU = mybir.AluOpType
ACT = mybir.ActivationFunctionType
AXX = mybir.AxisListType.X

P = 128
D = 1024
DC = D // P
SEQ = 256
META = 16
T = SEQ + META
TILES = [(0, 128), (128, 128), (256, 16)]
OUT_TILES = [(META, 128), (META + 128, 128)]
NT = len(OUT_TILES)
DEPTH = 2
HR, NR = 4, 64
RW = HR * NR
HD, DK = 4, 64
FF = 2816
FC = FF // P
NE = 8
TOPK = 2
IN_COLS = 3200
NCH = IN_COLS // P
RWKV_CH, Q_CH, K_CH, V_CH, BG_CH, CG_CH, U_CH = 0, 7, 11, 15, 19, 21, 23
LAM_INIT = [0.8 - 0.6 * math.exp(-0.3 * i) for i in range(DEPTH)]
NORM_EPS, GN_EPS, SUB_EPS = 1e-6, 64e-5, 1e-5
CH = 32
NCHUNK = -(-T // CH)
E_HALF = math.exp(-0.5)

CAP = 96
MAXO = (SEQ * TOPK) // CAP
NIT = NE + MAXO + 1
NFLAG = NE * (-(-SEQ // CAP) - 1)

SMALL_RING = 5
BIG_RING = 6
ITEM_RING = 9
PARTS = 3
IN_PARTS = 2
SLOT = 2048
PIECE = 2 * P

ROWS = 48
(MIXG, FFNG, MU, W0, A0, KK, KA, RK, GNG, GNB, QG, KG, SUBG, CONV, LAMQ, LAMK) = (
    0, 8, 16, 23, 25, 27, 29, 31, 33, 35, 37, 38, 39, 40, 46, 47)
FIRSTS = (MIXG, FFNG, MU, W0, A0, KK, KA, RK, GNG, GNB, QG, KG, SUBG, CONV, LAMQ, LAMK, ROWS)


def column(l, k):
    g = max(i for i, first in enumerate(FIRSTS) if first <= k)
    return DEPTH * FIRSTS[g] + (FIRSTS[g + 1] - FIRSTS[g]) * l + k - FIRSTS[g]


CONSTS = ["ident", "ones", "blk", "rope", "m16t", "m16", "moff", "m32s", "m32i", "causal", "tri"]
WIDE = ["cos", "sin", "reset", "iota"]


def constants():
    r = np.arange(P)
    a, b = r[:, None], r[None, :]
    c = {
        "ident": a == b,
        "ones": np.ones((P, P)),
        "blk": a // 64 == b // 64,
        "m16t": (a < b) & (a // 16 == b // 16),
        "m16": (b < a) & (a // 16 == b // 16),
        "moff": (b < a) & (a // 32 == b // 32) & (a // 16 != b // 16),
        "m32s": (a < b) & (a // 32 == b // 32),
        "m32i": (a <= b) & (a // 32 == b // 32),
        "causal": np.where(b > a, -1e30, 0.0),
        "tri": a < b,
    }
    rope = np.zeros((P, P))
    for h in (0, 64):
        for d in range(8):
            rope[h + d + 8, h + d] = -1.0
            rope[h + d, h + d + 8] = 1.0
    c["rope"] = rope
    inv = (np.float32(500000.0) ** (-np.arange(0, 16, 2, dtype=np.float32) / np.float32(16))).astype(np.float32)
    ang = np.arange(T, dtype=np.float32)[:, None] * inv[None, :]
    cos, sin = np.ones((P, T), np.float32), np.zeros((P, T), np.float32)
    for h in (0, 8, 64, 72):
        cos[h:h + 8] = np.cos(ang).T
        sin[h:h + 8] = np.sin(ang).T
    reset = np.broadcast_to((np.arange(T) % CH != 0), (P, T))
    iota = np.broadcast_to(np.arange(CAP * -(-SEQ // CAP)), (P, CAP * -(-SEQ // CAP)))
    parts = [np.asarray(c[n], np.float32) for n in CONSTS] + [cos, sin, reset, iota]
    return np.ascontiguousarray(np.concatenate([np.asarray(x, np.float32) for x in parts], axis=1))


def build(nc, A, out):
    ctx = ExitStack()
    with ctx:
        def sb(name, shape, dt=F32):
            return ctx.enter_context(nc.sbuf_tensor(name, shape, dt))

        def sems(*names):
            return namedtuple("Semaphores", names)(*(ctx.enter_context(nc.semaphore(n)) for n in names))

        ps = ctx.enter_context(nc.psum_tensor("ps", [P, 8, 512], F32))
        hT = sb("hT", [P, DC, T])
        hnT = sb("hnT", [P, DC, T])
        ring_small = sb("ring_small", [P, SMALL_RING, SLOT])
        vrow = sb("vrow", [DEPTH * ROWS, P])
        vcol = sb("vcol", [P, DEPTH * ROWS])
        vhalf = sb("vhalf", [P, DEPTH, 4])
        wide = CAP * -(-SEQ // CAP)
        cst = sb("cst", [P, P * len(CONSTS) + 3 * T + wide])
        C = namedtuple("Tables", CONSTS)(*(cst[:, P * k:P * k + P] for k in range(len(CONSTS))))
        o = P * len(CONSTS)
        cosT, sinT, resetT = (cst[:, o + k * T:o + (k + 1) * T] for k in range(3))
        iotaT = cst[:, o + 3 * T:o + 3 * T + wide]
        epsT = sb("epsT", [P, 3])
        msT = sb("msT", [P, 4 * T])
        rsT = sb("rsT", [P, 4 * T])
        small = sb("small", [P, 64])
        router = sb("router", [P, DC, NE])
        ARENA = 33216
        arena_at = nc.sbuf_base
        arena = sb("arena", [P, ARENA])
        used = [0]

        def carve(*shape):
            n = int(np.prod(shape))
            v = arena[:, used[0]:used[0] + n]
            used[0] += n
            assert used[0] <= ARENA, used[0]
            if len(shape) == 1:
                return v
            names = "abcd"[:len(shape)]
            return v.rearrange(f"p ({' '.join(names)}) -> p {' '.join(names)}",
                               **{n: s for n, s in zip(names, shape)})

        def carve_parts(name, *shape):
            o = -(-used[0] // 8) * 8
            used[0] = o
            carve(int(np.prod(shape)))
            return nc.alloc_sbuf_tensor_at(name, [P, *shape], F32R, offset=arena_at + 4 * o)

        projT = carve(NCH, T + 2)
        sqT = carve(DC, T)
        used[0] = o_at = -(-used[0] // 8) * 8
        oT = carve(DC, T)
        hxT = carve(7, T)
        lora = carve(T)
        lora_w = carve(RW)
        eT, cumT, PtT, AtT, KtT, KhT, aT, gT, kkT, bT, BtT, RtT, bonusT, kks = (carve(2, T) for _ in range(14))
        cvT = kks
        tok_at = used[0]
        tokAV = carve(3, 2, 256)
        tokBK = carve(2, 2, 256)
        mark = used[0]
        m16, mt16, moff, m2, mt2, ntm, qm = (carve(4, P) for _ in range(7))
        rbm, rkm = ([carve(4, P), carve(4, P), carve(4, TILES[2][1])] for _ in range(2))
        wT = carve(2, T)
        nv = carve(256)
        zTok = carve(3, 256)
        uTok = carve(3, 256)
        stT = carve(NCHUNK, 2, NR)
        pst = carve(2, NR)
        vTok = arena[:, 0:3 * 512].rearrange("p (i n) -> p i n", i=3)
        assert 3 * 512 <= 7 * (T + 2)
        prob = sqT[:, 4:8, :].rearrange("p (b c) t -> p b c t", b=2)
        pd = arena[:, V_CH * (T + 2):V_CH * (T + 2) + 2 * T].rearrange("p (b t) -> p b t", b=2)
        oat = hnT[:, 0:4, :]
        pT = hnT[:, 4:7, :]
        scaled = hnT[:, 7, :]
        used[0] = mark
        xTok = carve(3, D)
        used[0] = o_at
        xp_hi = carve_parts("xp_hi", DC, T)
        used[0] = tok_at
        xp_lo = carve_parts("xp_lo", DC, T)
        assert used[0] <= mark
        used[0] = mark
        wp_hi, wp_lo = carve_parts("wp_hi", IN_PARTS, SLOT), carve_parts("wp_lo", IN_PARTS, SLOT)
        used[0] = 0
        big = carve(BIG_RING - SMALL_RING, SLOT)
        w_hi = carve_parts("w_hi", PARTS, SLOT)
        mark = used[0]
        low_at = used[0] = ARENA - PARTS * SLOT
        w_lo = carve_parts("w_lo", PARTS, SLOT)
        used[0] = mark
        xd_hi, xd_lo = carve_parts("xd_hi", DC, T), carve_parts("xd_lo", DC, T)
        hd_hi, hd_lo = carve_parts("hd_hi", FC, T), carve_parts("hd_lo", FC, T)
        sgd = carve(2, 2, T)
        assert used[0] <= low_at
        hmd = sgd
        used[0] = mark
        xm_hi, xm_lo = carve_parts("xm_hi", DC, CAP), carve_parts("xm_lo", DC, CAP)
        hm_hi, hm_lo = carve_parts("hm_hi", FC, CAP), carve_parts("hm_lo", FC, CAP)
        y_hi, y_lo = carve_parts("y_hi", D), carve_parts("y_lo", D)
        ohT = carve_parts("ohT", SEQ)
        sgm = carve(2, PIECE)
        hmTok = carve(2, PIECE)
        hnTok = carve(NT, D)
        oneh = carve(NT, CAP)
        gsel = carve(NT, 1)
        gslot = carve(1)
        lgS, sel, posx, gates, oh1, oh2, top8 = (carve(NT, NE) for _ in range(7))
        fidx, gw = carve(NT, 2), carve(NT, 2)
        cnt, flag, incl, ev, ov = (carve(NFLAG) for _ in range(5))
        eqg, pick = carve(MAXO, NFLAG), carve(MAXO, NFLAG)
        used[0] = -(-used[0] // 8) * 8
        more = carve(ITEM_RING - BIG_RING, SLOT)
        assert used[0] <= low_at
        tab = sb("tab", [1, 2, NIT], I32)
        ntab = sb("ntab", [1, 1], I32)
        fsum = sb("fsum", [1, 2, NIT])
        stat = sb("stat", [P, 2, 6])
        idx8 = sb("idx8", [P, NT, 8], U32)

        def slot(s):
            if s < SMALL_RING:
                return ring_small[:, s, :]
            return big[:, s - SMALL_RING, :] if s < BIG_RING else more[:, s - BIG_RING, :]

        w_in, w_out = A["w_in"], A["w_out"]

        def cols_piece(w, n0, n):
            return w[:, n0:n0 + n].rearrange("(c p) n -> p c n", p=P)

        def rows_piece(w, r0):
            return w[r0:r0 + PIECE, :].rearrange("(c p) n -> p c n", p=P)

        def mixer_loads(l):
            for n0 in range(0, IN_COLS, PIECE):
                n = min(PIECE, IN_COLS - n0)
                yield cols_piece(w_in[l], n0, n), DC * n
            for n0 in range(0, D, PIECE):
                yield cols_piece(w_out[l], n0, PIECE), SLOT

        def ffn_loads(g, u, d):
            for s in range(FF // PIECE):
                yield cols_piece(g, s * PIECE, PIECE), SLOT
                yield cols_piece(u, s * PIECE, PIECE), SLOT
            for s in range(FF // PIECE):
                yield rows_piece(d, s * PIECE), SLOT

        MIXN, FFNN = -(-IN_COLS // PIECE) + D // PIECE, 3 * FF // PIECE
        STATIC = 2 * MIXN + FFNN
        slot_of, prior, filled = [], [], [0] * ITEM_RING
        last = [None] * BIG_RING
        load_value = []
        for k in range(STATIC):
            if k < MIXN:
                s = k % SMALL_RING
            elif k < MIXN + FFNN:
                s = (k - MIXN + MIXN % SMALL_RING) % BIG_RING
            else:
                s = (k - STATIC + SMALL_RING) % SMALL_RING
            slot_of.append(s)
            prior.append(last[s])
            last[s] = k
            filled[s] += 1
            load_value.append(filled[s])
        item_prior = [max(k for k in range(-FFNN, j) if (k % FFNN) % ITEM_RING == j % ITEM_RING) for j in range(FFNN)]
        per_item = [len(range(s, FFNN, ITEM_RING)) for s in range(ITEM_RING)]

        assert FFNN % PARTS == 0

        loaded = [ctx.enter_context(nc.semaphore(f"piece_in_slot{s}")) for s in range(ITEM_RING)]

        S = sems(
            "consts_in", "params_act", "params_pool", "x_in", "lora_w_in", "out_stored", "router_in",
            "eps_set", "pads_zero", "vcol_mm", "vcol_ready", "vhalf_ready", "dve_chain", "pool_chain",
            "x_mm", "h_ready", "sq_ready", "nsum_mm", "root_ready", "kk_max", "rs_ready", "hn_ready",
            "proj_mm", "proj_act", "proj_dve",
            "shift_d", "hx_ready", "lora_act", "lora_sig", "lora_mm", "lora_out",
            "decay_ready", "exp_ready", "kk_sq", "kk_mm", "bonus_pre", "bonus_mm", "til_ready",
            "tok_mm", "tok_ready", "mat_mm", "mat_ev", "lvl_mm", "lvl_act", "lvl_dve", "q1_ready",
            "wt_mm", "wt_act", "nv_ready",
            "u_mm", "u_ready", "st_mm", "st_ready", "y_mm", "y_sb",
            "gn_mm", "gn_cent", "gn_sq", "gn_root", "gn_inv", "oa_ready", "oc_ready",
            "qk_sq", "qk_mm", "qg_ready", "qcos_ready", "rot_mm", "rot_read", "qk_ready",
            "vt_mm", "vt_ready", "lam_prod", "lam_mm", "lam_exp",
            "sc_mm", "mx_ready", "p_ready", "pd_ready", "pt_mm", "pt_ready", "o_mm", "o_sb", "osq_ready",
            "ob_mm", "ob_root", "ob_inv", "ob_ready", "wout_mm",
            "xp_hi_ready", "xp_lo_ready", "wp_hi_ready", "wp_lo_ready",
            "hi_ready", "lo_ready", "parts_used", "xd_hi_ready", "xd_lo_ready",
            "silu_ready", "hid_prod", "hd_hi_ready", "hd_lo_ready", "down_mm",
            "msilu_ready", "mhid_prod", "ht_mm", "hm_hi_ready", "hm_lo_ready",
            "hntok_mm", "hntok_ready", "lg_mm", "gap_ready", "gap_exp", "sel_ready", "pos_mm", "table_ready",
            "oneh_ready", "gather_mm", "xm_hi_ready", "xm_lo_ready", "oht_mm", "oht_ready", "gslot_mm", "gslot_ready",
            "y_hi_ready", "y_lo_ready", "scat_mm",
            "h_item", "out_mm", "out_act", "out_dve",
        )

        def freed(k):
            if MIXN <= k < MIXN + FFNN:
                return S.lo_ready, k - MIXN + 1
            l, q = (0, k) if k < MIXN else (1, k - MIXN - FFNN)
            n_in = -(-IN_COLS // PIECE)
            if q < n_in:
                return S.wp_lo_ready, n_in * l + q + 1
            return S.wout_mm, DC * l + 2 * (q - n_in) + 2
        block = ctx.enter_context(nc.Block())

        def vc(l, k, n=1):
            return vcol[:, column(l, k):column(l, k) + n]

        def bc(ap, n):
            return ap.unsqueeze(1).broadcast_to([ap.shape[0], n, ap.shape[1]])

        def tail(ap, n):
            return ap.unsqueeze(len(ap.shape)).broadcast_to(list(ap.shape) + [n])

        def cur(c0, n=1):
            return projT[:, c0:c0 + n, 2:T + 2]

        def prev(c0, k, n=1):
            return projT[:, c0:c0 + n, 2 - k:T + 2 - k]

        def lvl(per_tile, l, i):
            return (2 * per_tile[0] + per_tile[1]) * l + per_tile[0] * i

        def together(one, other):
            going = [one, other]
            while going:
                going = [g for g in going if next(g, "end") != "end"]

        LVM, LVA, LVD = (11, 8), (6, 5), (5, 3)
        HALVES = 6
        NORMS = 5
        SQUARED = ((0, 4), (4, 6), (6, DC))
        NORM_BANK = (7, 4, 0, 4)

        tall = [(MIXG, A["mix_norm_g"].rearrange("l (c p) -> (l c) p", p=P)),
                (MU, A["tm_mu"].rearrange("l (c p) -> (l c) p", p=P)),
                (W0, A["tm_w0"].rearrange("l (c p) -> (l c) p", p=P)),
                (A0, A["tm_a0"].rearrange("l (c p) -> (l c) p", p=P)),
                (KK, A["tm_k_k"].rearrange("l (c p) -> (l c) p", p=P)),
                (KA, A["tm_k_a"].rearrange("l (c p) -> (l c) p", p=P)),
                (RK, A["tm_r_k"].rearrange("l (c a) n -> (l c) (a n)", a=2)),
                (GNG, A["tm_gn_g"].rearrange("l (c p) -> (l c) p", p=P)),
                (GNB, A["tm_gn_b"].rearrange("l (c p) -> (l c) p", p=P)),
                (SUBG, A["da_subln_g"]),
                (CONV, A["sc_conv_w"].rearrange("l j (c p) -> (l j c) p", p=P)),
                (FFNG, A["ffn_norm_g"].rearrange("l (c p) -> (l c) p", p=P))]
        halves = [(QG, 0, A["da_q_norm_g"]), (QG, 1, A["da_q_norm_g"]), (KG, 0, A["da_k_norm_g"]),
                  (KG, 1, A["da_k_norm_g"]), (LAMQ, 0, A["da_lambda_q1"]), (LAMQ, 1, A["da_lambda_q2"]),
                  (LAMK, 0, A["da_lambda_k1"]), (LAMK, 1, A["da_lambda_k2"])]

        @block.sync
        def _(sp):
            sp.dma_start(cst[:], A["consts"]).then_inc(S.consts_in, 16)
            sp.dma_start(xTok[0:META, 0, :], A["meta_tokens"]).then_inc(S.x_in, 16)
            sp.dma_start(xTok[META:P, 0, :], A["x"][0, 0:P - META, :]).then_inc(S.x_in, 16)
            sp.dma_start(xTok[:, 1, :], A["x"][0, P - META:2 * P - META, :]).then_inc(S.x_in, 16)
            sp.dma_start(xTok[0:META, 2, :], A["x"][0, 2 * P - META:SEQ, :]).then_inc(S.x_in, 16)

            sp.wait_ge(S.params_act, 16 * len(tall))
            sp.wait_ge(S.params_pool, 16 * len(halves))
            k = 0
            for stage in (mixer_loads(0),
                          ffn_loads(A["ffn_w_gate"][0], A["ffn_w_up"][0], A["ffn_w_down"][0]),
                          mixer_loads(1)):
                for src, width in stage:
                    s = slot_of[k]
                    if prior[k] is not None:
                        sp.wait_ge(*freed(prior[k]))
                    if MIXN <= k < MIXN + FFNN and SMALL_RING <= s:
                        sp.wait_ge(S.h_ready, 2 * DC)
                    dst = slot(s)[:, 0:width].rearrange("p (c n) -> p c n", c=src.shape[1])
                    sp.dma_start(dst, src).then_inc(loaded[s], 16)
                    k += 1

            def item_loads(i, expert, first, end):
                pieces = list(ffn_loads(*(A[n][0, expert] for n in ("moe_w_gate", "moe_w_up", "moe_w_down"))))
                for j in range(first, end):
                    src = pieces[j][0]
                    if j != 2 * FFNN // 3:
                        after = item_prior[j + 1 if j + 1 == 2 * FFNN // 3 else j]
                        sp.wait_ge(S.lo_ready, i * FFNN + (FFNN + after + 1))
                    dst = slot(j % ITEM_RING).rearrange("p (c n) -> p c n", c=src.shape[1])
                    sp.dma_start(dst, src).then_inc(loaded[j % ITEM_RING], 16)

            for j in range(SMALL_RING):
                sp.wait_ge(*freed(last[j]))
                if j < PARTS:
                    item_loads(0, 0, j, j + 1)
            with sp.Fori(0, NE - 1) as i:
                item_loads(i, i, PARTS, SMALL_RING)
                sp.wait_ge(S.h_ready, 4 * DC)
                item_loads(i, i, SMALL_RING, FFNN)
                item_loads(i + 1, i + 1, 0, PARTS)
            sp.wait_ge(S.table_ready, 1)
            n_items = sp.value_load(ntab[0:1, 0:1], min_val=NE, max_val=NE + MAXO)
            with sp.Fori(NE - 1, n_items) as i:
                expert = sp.value_load(tab[0:1, 0, bass.ds(i, 1)], min_val=0, max_val=NE - 1)
                item_loads(i, expert, PARTS, FFNN)
                expert = sp.value_load(tab[0:1, 0, bass.ds(i + 1, 1)], min_val=0, max_val=NE - 1)
                item_loads(i + 1, expert, 0, PARTS)
            for i, (t0, n) in enumerate(OUT_TILES):
                sp.wait_ge(S.out_act, i + 1)
                sp.wait_ge(S.out_dve, i + 1)
                sp.dma_start(out[0, t0 - META:t0 - META + n, :], hnTok[0:n, i, :]).then_inc(S.out_stored, 16)
            sp.wait_ge(S.out_stored, 16 * NT)

        @block.gpsimd
        def _(pool):
            done = [0]

            def step(ins):
                done[0] += 1
                ins.then_inc(S.pool_chain, 1)
                pool.wait_ge(S.pool_chain, done[0])

            def qk_cosine(l, k):
                pool.wait_ge(S.qg_ready, 8 * l + 4 * k + 4)
                pool.tensor_tensor(cur(Q_CH + 4 * k, 4), hnT[:, 4 * k:4 * k + 4, :], bc(cosT, 4),
                                   ALU.mult).then_inc(S.qcos_ready, 1)

            for first, half, src in halves:
                row = DEPTH * first
                pool.dma_start(vrow[row:row + DEPTH, 64 * half:64 * half + 64], src).then_inc(S.params_pool, 16)
            for k, eps in enumerate((NORM_EPS, GN_EPS, SUB_EPS)):
                pool.memset(epsT[:, k:k + 1], eps).then_inc(S.eps_set, 1)

            for l in range(DEPTH):
                pool.wait_ge(S.h_ready, DC * (2 * l + 1))
                pool.memset(projT[:, :, 0:2], 0.0).then_inc(S.pads_zero, 1)
                pool.wait_ge(S.pads_zero, l + 1)
                pool.wait_ge(S.proj_act, 13 * l + 4)
                pool.wait_ge(S.proj_dve, 12 * l + 3)
                pool.tensor_tensor(sqT[:, 0:7, :], prev(RWKV_CH, 1, 7), cur(RWKV_CH, 7),
                                   ALU.subtract).then_inc(S.shift_d, 1)
                qk_cosine(l, 0)
                pool.wait_ge(S.proj_act, 13 * l + 13)
                pool.wait_ge(S.proj_dve, 12 * l + 12)
                step(pool.tensor_tensor(cur(CG_CH, 2), cur(CG_CH, 2), cur(U_CH, 2), ALU.mult))
                for j in range(3):
                    for c in range(2):
                        ins = pool.tensor_scalar((cvT if j else oT[:, 6:8, :])[:, c, :], prev(CG_CH + c, 2 - j)[:, 0, :],
                                                 vc(l, CONV + 2 * j + c), None, ALU.mult)
                        if c == 1:
                            step(ins)
                    if j:
                        step(pool.tensor_tensor(oT[:, 6:8, :], oT[:, 6:8, :], cvT, ALU.add))
                pool.tensor_tensor(oT[:, 6:8, :], oT[:, 6:8, :], cur(BG_CH, 2), ALU.mult).then_inc(S.oc_ready, 1)
                qk_cosine(l, 1)

        @block.scalar
        def _(act):
            for first, src in tall:
                row = DEPTH * first
                act.dma_start(vrow[row:row + src.shape[0], :], src).then_inc(S.params_act, 16)
            act.wait_ge(S.eps_set, 3)

            def log_exp_table():
                act.preload_act_table_set("natural_log_exp_and_others")


            def lambdas():
                act.wait_ge(S.lam_mm, 2)
                act.activation(small[:, 2:4], ps[:, 3, 0:2], ACT.Exp).then_inc(S.lam_exp, 1)
                act.activation(small[:, 4:6], ps[:, 4, 0:2], ACT.Exp).then_inc(S.lam_exp, 1)

            def squares(idx):
                for a, b in SQUARED:
                    act.wait_ge(S.h_ready, DC * idx + b)
                    act.activation(sqT[:, a:b, :], hT[:, a:b, :], ACT.Square).then_inc(S.sq_ready, 1)

            def inverse_root(dst, tmp, src, scale, eps, logged, done, k):
                bias = {} if eps is None else {"bias": epsT[:, eps:eps + 1]}
                act.activation(tmp, src, ACT.Ln, scale=scale, **bias).then_inc(logged, 1)
                act.wait_ge(logged, k)
                act.activation(dst, tmp, ACT.Exp, scale=-0.5).then_inc(done, 1)

            def chunked(x, n):
                return x[:, 0:n * T].rearrange("p (c t) -> p c t", c=n)

            def norm_root(idx):
                act.wait_ge(S.nsum_mm, idx + 1)
                inverse_root(rsT[:, 0:T], msT[:, 0:T], ps[:, NORM_BANK[idx], 0:T], 1.0 / D, 0, S.root_ready, S.rs_ready,
                             NORMS * (idx // 2) + (1 if idx % 2 == 0 else NORMS))

            def in_high(l, q):
                k, n = (MIXN + FFNN) * l + q, min(PIECE, IN_COLS - PIECE * q)
                act.wait_ge(loaded[slot_of[k]], 16 * load_value[k])
                if q >= IN_PARTS:
                    act.wait_ge(S.proj_mm, NCH * l + 2 * (q - IN_PARTS) + 2)
                act.activation(wp_hi[:, q % IN_PARTS, 0:DC * n], slot(slot_of[k])[:, 0:DC * n],
                               ACT.Copy).then_inc(S.wp_hi_ready, 1)

            def rwkv_lora(l):
                act.wait_ge(S.hx_ready, 7 * l + 1)
                act.activation(lora[0:32, :], hxT[0:32, 6, :], ACT.Tanh).then_inc(S.lora_act, 1)
                act.activation(lora[64:128, :], hxT[64:128, 6, :], ACT.Tanh, scale=0.5).then_inc(S.lora_act, 1)
                act.activation(lora[32:64, :], hxT[32:64, 6, :], ACT.Copy).then_inc(S.lora_act, 1)

            def rwkv_lora_out(l):
                act.wait_ge(S.vhalf_ready, DEPTH)
                for k, dst in ((0, eT), (1, aT)):
                    act.wait_ge(S.lora_mm, 3 * l + k + 1)
                    for p in range(2):
                        act.activation(dst[:, p, :], ps[:, 2 + 2 * k + p, 0:T], ACT.Tanh, scale=0.5,
                                       bias=vhalf[:, l, 2 * k + p:2 * k + p + 1]).then_inc(S.lora_out, 1)
                act.wait_ge(S.lora_mm, 3 * l + 3)
                act.activation(gT, ps[:, 6:8, 0:T], ACT.Copy).then_inc(S.lora_out, 1)

            def rwkv_exp(l):
                act.wait_ge(S.decay_ready, l + 1)
                act.activation(PtT, cumT, ACT.Exp, scale=-1.0).then_inc(S.exp_ready, 1)
                act.activation(AtT, AtT, ACT.Exp, scale=-1.0).then_inc(S.exp_ready, 1)
                act.activation(KtT, cumT, ACT.Exp).then_inc(S.exp_ready, 1)
                act.activation(KhT[:, :, 0:256], KhT[:, :, 0:256], ACT.Exp).then_inc(S.exp_ready, 1)

            def rwkv_tok(l):
                k = 0
                for i, (t0, n) in enumerate(TILES):
                    for bank, dst in ((4, tokAV), (5, tokBK))[:2 if i < 2 else 1]:
                        k += 1
                        act.wait_ge(S.tok_mm, 5 * l + k)
                        act.activation(dst[0:n, i], ps[0:n, bank, :].rearrange("p (a b) -> p a b", a=2),
                                       ACT.Copy).then_inc(S.tok_ready, 1)

            def rwkv_levels(l, i):
                t0, n = TILES[i]
                g = 3 * l + i
                at = lvl(LVM, l, i)

                def copy(dst, bank, need):
                    act.wait_ge(S.lvl_mm, at + need)
                    act.activation(dst[0:n, :, 0:n], ps[0:n, bank, :].rearrange("p (h t) -> p h t", h=4)[:, :, 0:n],
                                   ACT.Copy).then_inc(S.lvl_act, 1)

                yield
                copy(mt2, 4, 1)
                copy(m2, 5, 2)
                yield
                act.wait_ge(S.q1_ready, g + 1)
                copy(mt16, 4, 4)
                copy(m16, 5, 5)
                yield
                copy(m2, 5, 7)
                yield
                yield
                if i < 2:
                    copy(mt2, 4, 9)
                yield
                yield
                act.wait_ge(S.wt_mm, 3 * g + 1)
                act.activation(wT[:, :, t0:t0 + n], ps[:, 4, 0:256].rearrange("p (a t) -> p a t", a=2)[:, :, 0:n],
                               ACT.Copy).then_inc(S.wt_act, 1)
                yield
                act.wait_ge(S.wt_mm, 3 * g + 3)
                act.activation(zTok[0:n, i], ps[0:n, 6, 0:256], ACT.Copy).then_inc(S.wt_act, 1)
                yield

            def rwkv(l):
                rwkv_tok(l)
                yield
                for i in range(3):
                    yield from rwkv_levels(l, i)
                for c in range(2 * NCHUNK - 1 + 4):
                    yield
                yield from group_norm(l)

            def group_norm(l):
                act.wait_ge(S.y_mm, l + 1)
                act.activation(eT[0:64], ps[0:64, 0:4:2, 0:T], ACT.Copy).then_inc(S.y_sb, 1)
                act.activation(eT[64:128], ps[64:128, 1:4:2, 0:T], ACT.Copy).then_inc(S.y_sb, 1)
                yield
                act.wait_ge(S.gn_cent, l + 1)
                act.activation(cumT, eT, ACT.Square).then_inc(S.gn_sq, 1)
                yield
                act.wait_ge(S.gn_mm, 2 * l + 2)
                inverse_root(cumT, cumT, ps[:, 2:4, 0:T], 1.0 / NR, 1, S.gn_root, S.gn_inv, l + 1)
                yield

            def attention(l):
                def squares_gains(k):
                    act.activation(sqT[:, 4 * k:4 * k + 4, :], cur(Q_CH + 4 * k, 4), ACT.Square).then_inc(S.qk_sq, 1)
                    for c in range(4):
                        act.activation(hnT[:, 4 * k + c, :], cur(Q_CH + 4 * k + c)[:, 0, :], ACT.Copy,
                                       scale=vc(l, (QG, KG)[k])).then_inc(S.qg_ready, 1)

                squares_gains(0)
                yield
                for i, (t0, n) in enumerate(TILES):
                    act.wait_ge(S.vt_mm, 3 * l + i + 1)
                    act.activation(vTok[0:n, i], ps[0:n, i, :], ACT.Copy).then_inc(S.vt_ready, 1)
                yield
                for k in range(2):
                    act.wait_ge(S.qk_mm, 2 * l + k + 1)
                    if k:
                        act.wait_ge(S.qk_ready, 2 * l + 1)
                    else:
                        act.wait_ge(S.til_ready, 6 * l + 1)
                    inverse_root(chunked(rsT, 4), chunked(msT, 4), ps[:, 0:4, 0:T], 1.0 / DK, 0, S.root_ready, S.rs_ready,
                                 NORMS * l + 3 + k)
                    yield
                    if k == 0:
                        squares_gains(1)
                    yield
                    yield
                for u in range(14):
                    i = u % 3
                    t0, n = TILES[i]
                    b, m = u % 2, t0 + n
                    if u < 12:
                        act.wait_ge(S.mx_ready, 12 * l + u + 1)
                        for c in range(2):
                            act.activation(prob[0:n, b, c, 0:m], ps[0:n, c, 0:m], ACT.Exp, scale=DK ** -0.5,
                                           bias=stat[0:n, b, c:c + 1],
                                           accum_out=stat[0:n, b, 2 + c:3 + c]).then_inc(S.p_ready, 1)
                    if u >= 4 and u % 3 == 1:
                        output(l, u // 3 - 1)
                    yield
                    if u >= 4 and u % 3 == 1:
                        h = u // 3 - 1
                        act.wait_ge(S.ob_mm, 4 * l + h + 1)
                        inverse_root(rsT[:, h * T:h * T + T], msT[:, h * T:h * T + T], ps[:, 3, 0:T], 1.0 / P, 2,
                                     S.ob_root, S.ob_inv, 4 * l + h + 1)
                    yield

            def output(l, h):
                act.wait_ge(S.o_mm, 4 * l + h + 1)
                act.activation(oat[:, h, :], ps[:, 3, 0:T], ACT.Copy).then_inc(S.o_sb, 1)
                act.wait_ge(S.o_sb, 4 * l + h + 1)
                act.activation(sqT[:, h, :], oat[:, h, :], ACT.Square).then_inc(S.osq_ready, 1)

            def high(g, slot_no, value, parts):
                act.wait_ge(loaded[slot_no], value)
                if parts is not None:
                    act.wait_ge(S.parts_used, parts)
                act.activation(w_hi[:, g % PARTS, :], slot(slot_no), ACT.Copy).then_inc(S.hi_ready, 1)

            def dense_high(j):
                k = MIXN + j
                high(j, slot_of[k], 16 * load_value[k], j - PARTS + 1 if j >= PARTS else None)

            def item_high(i, j):
                q = j % ITEM_RING
                high(j, q, i * (16 * per_item[q]) + 16 * (filled[q] + j // ITEM_RING + 1),
                     i * FFNN + (FFNN + j - PARTS + 1))

            for l in range(DEPTH):
                log_exp_table()
                if l:
                    act.wait_ge(S.h_ready, DC * (2 * l + 1))
                squares(2 * l)
                in_high(l, 0)
                norm_root(2 * l)
                act.dma_start(lora_w[0:32, :], A["tm_w_decay_up"][l]).then_inc(S.lora_w_in, 16)
                act.dma_start(lora_w[32:64, :], A["tm_w_a_up"][l]).then_inc(S.lora_w_in, 16)
                act.dma_start(lora_w[64:128, :], A["tm_w_g_up"][l]).then_inc(S.lora_w_in, 16)
                for c in range(DC):
                    act.wait_ge(S.hn_ready, 2 * DC * l + c + 1)
                    act.activation(xp_hi[:, c, :], hnT[:, c, :], ACT.Copy).then_inc(S.xp_hi_ready, 1)
                in_high(l, 1)
                if l == 0:
                    lambdas()
                    act.dma_start(router[:], A["router_w"][0].rearrange("(c p) e -> p c e", p=P)
                                  ).then_inc(S.router_in, 16)
                for n in range(0, NCH, 2):
                    act.wait_ge(S.proj_mm, NCH * l + n + 1)
                    act.activation(projT[:, n, 2:T + 2], ps[:, 0, 0:T], ACT.Copy).then_inc(S.proj_act, 1)
                    if n // 2 + IN_PARTS <= NCH // 2:
                        in_high(l, n // 2 + IN_PARTS)
                    if n == 6:
                        rwkv_lora(l)
                    if n == 10:
                        rwkv_lora_out(l)
                    if n == 16:
                        log_exp_table()
                        rwkv_exp(l)
                        act.wait_ge(S.kk_max, l + 1)
                        inverse_root(rsT[:, 0:2 * T], msT[:, 0:2 * T], msT[:, 0:2 * T], 1.0, None, S.root_ready,
                                     S.rs_ready, NORMS * l + 2)
                together(rwkv(l), attention(l))
                squares(2 * l + 1)
                if l == 0:
                    dense_high(0)
                    norm_root(1)
                    dense_high(1)
                    dense_high(2)
                    for c in range(DC):
                        act.wait_ge(S.hn_ready, DC + c + 1)
                        act.activation(xd_hi[:, c, :], hnT[:, c, :], ACT.Copy).then_inc(S.xd_hi_ready, 1)
                    for j in range(FFNN):
                        s = j // 2
                        if j % 2 and s < FC // 2:
                            act.wait_ge(S.parts_used, j + 1)
                            if s >= 2:
                                act.wait_ge(S.hd_lo_ready, s - 1)
                            b = 4 * (s % 2)
                            act.activation(sgd[:, s % 2], ps[:, b:b + 2, 0:T], ACT.Silu).then_inc(S.silu_ready, 1)
                        if j + PARTS < FFNN:
                            dense_high(j + PARTS)
                        if j % 2 and s < FC // 2:
                            act.wait_ge(S.hid_prod, s + 1)
                            act.activation(hd_hi[:, 2 * s:2 * s + 2, :], hmd[:, s % 2],
                                           ACT.Copy).then_inc(S.hd_hi_ready, 1)
                else:
                    norm_root(3)
                    item_high(0, 0)

            for k in range(0, 2 * NT, 2):
                act.wait_ge(S.hntok_mm, k + 1)
                i = k // 2
                n = OUT_TILES[i][1]
                act.activation(hnTok[0:n, i, 0:512], ps[0:n, 2, :], ACT.Copy).then_inc(S.hntok_ready, 1)
                act.wait_ge(S.hntok_mm, k + 2)
                act.activation(hnTok[0:n, i, 512:1024], ps[0:n, 3, :], ACT.Copy).then_inc(S.hntok_ready, 1)
            act.wait_ge(S.gap_ready, 1)
            act.activation(gw[:, :, 1], gw[:, :, 1], ACT.Exp).then_inc(S.gap_exp, 1)
            for j in range(1, PARTS):
                item_high(0, j)

            def gathered_high(i):
                for half in range(2):
                    act.wait_ge(S.gather_mm, 2 * i + (half + 1))
                    act.activation(xm_hi[:, 4 * half:4 * half + 4, :],
                                   ps[:, 4 + half, 0:4 * CAP].rearrange("p (c t) -> p c t", c=4),
                                   ACT.Copy).then_inc(S.xm_hi_ready, 1)

            def slots_turned(i):
                act.wait_ge(S.oht_mm, i + 1)
                act.activation(ohT[0:CAP, :], ps[0:CAP, 6, 0:SEQ], ACT.Copy).then_inc(S.oht_ready, 1)

            gathered_high(0)
            slots_turned(0)
            act.preload_act_table(ACT.Silu)
            act.wait_ge(S.table_ready, 1)
            n_items = act.value_load(ntab[0:1, 0:1], min_val=NE, max_val=NE + MAXO)
            with act.Fori(0, n_items) as i:
                for j in range(FFNN):
                    s = j // 2
                    if j + PARTS < FFNN:
                        item_high(i, j + PARTS)
                    elif j < FFNN - 1:
                        item_high(i + 1, j + PARTS - FFNN)
                    if j % 2 and s < FC // 2:
                        act.wait_ge(S.parts_used, i * FFNN + (FFNN + j + 1))
                        if s >= 2:
                            act.wait_ge(S.mhid_prod, i * (FC // 2) + (s - 1))
                        act.activation(sgm[0:CAP, s % 2, :], ps[0:CAP, s % 2, 0:PIECE],
                                       ACT.Silu).then_inc(S.msilu_ready, 1)
                    if j % 2 and 1 <= s <= FC // 2:
                        act.wait_ge(S.ht_mm, i * (FC // 2) + s)
                        act.activation(hm_hi[:, 2 * s - 2:2 * s, :],
                                       ps[:, 4 + (s - 1) % 2, 0:2 * CAP].rearrange("p (c t) -> p c t", c=2),
                                       ACT.Copy).then_inc(S.hm_hi_ready, 1)
                act.wait_ge(S.parts_used, i * FFNN + 2 * FFNN)
                for z in range(2):
                    act.activation(y_hi[0:CAP, 512 * z:512 * z + 512], ps[0:CAP, 6 + z, :], ACT.Copy,
                                   scale=gslot[0:CAP, :]).then_inc(S.y_hi_ready, 1)
                item_high(i + 1, PARTS - 1)
                gathered_high(i + 1)
                act.wait_ge(S.scat_mm, i * DC + DC)
                slots_turned(i + 1)
            for i, (t0, n) in enumerate(OUT_TILES):
                act.wait_ge(S.out_mm, 2 * i + 1)
                act.activation(hnTok[0:n, i, 0:512], ps[0:n, 2 * (i % 2), :], ACT.Copy).then_inc(S.out_act, 1)

        @block.vector
        def _(dve):
            done = [0]

            def step(ins):
                done[0] += 1
                ins.then_inc(S.dve_chain, 1)
                dve.wait_ge(S.dve_chain, done[0])

            def rs(n):
                return rsT[:, 0:n * T].rearrange("p (c t) -> p c t", c=n)

            def norm(idx, g):
                l = idx // 2
                dve.wait_ge(S.rs_ready, NORMS * l + (1 if idx % 2 == 0 else NORMS))
                for c in range(DC):
                    dve.scalar_tensor_tensor(out=hnT[:, c, :], in0=hT[:, c, :], scalar=vc(l, g + c), in1=rsT[:, 0:T],
                                             op0=ALU.mult, op1=ALU.mult).then_inc(S.hn_ready, 1)

            def in_low(l, q):
                k, n = (MIXN + FFNN) * l + q, min(PIECE, IN_COLS - PIECE * q)
                dve.wait_ge(S.wp_hi_ready, (NCH // 2 + 1) * l + q + 1)
                dve.tensor_tensor(wp_lo[:, q % IN_PARTS, 0:DC * n], slot(slot_of[k])[:, 0:DC * n],
                                  wp_hi[:, q % IN_PARTS, 0:DC * n], ALU.subtract).then_inc(S.wp_lo_ready, 1)

            def hx(l, c):
                dve.scalar_tensor_tensor(out=hxT[:, c, :], in0=sqT[:, c, :], scalar=vc(l, MU + c),
                                         in1=cur(c)[:, 0, :], op0=ALU.mult, op1=ALU.add).then_inc(S.hx_ready, 1)

            R, K, V = hxT[:, 0:2, :], hxT[:, 2:4, :], hxT[:, 4:6, :]

            def prep(l, n):
                if n == 5:
                    dve.wait_ge(S.shift_d, l + 1)
                    hx(l, 6)
                if n == 7:
                    hx(l, 2)
                    hx(l, 3)
                    dve.wait_ge(S.lora_act, 3 * l + 2)
                    dve.tensor_scalar(lora[64:128, :], lora[64:128, :], 0.5, 0.5, ALU.mult,
                                      ALU.add).then_inc(S.lora_sig, 1)
                if n == 9:
                    for c in (0, 1, 4, 5):
                        hx(l, c)
                if n == 11:
                    dve.wait_ge(S.lora_out, 5 * l + 4)
                    step(dve.tensor_scalar(eT, eT, 0.5 * E_HALF, 0.5 * E_HALF, ALU.mult, ALU.add))
                    step(dve.tensor_scalar(aT, aT, 0.5, 0.5, ALU.mult, ALU.add))
                    for p in range(2):
                        step(dve.tensor_tensor_scan(cumT[:, p, :], resetT, eT[:, p, :], 0.0, ALU.mult, ALU.add))
                if n == 13:
                    dve.tensor_tensor(AtT, cumT, eT, ALU.subtract)
                    for p in range(2):
                        c32 = cumT[:, p, 0:256].rearrange("p (c t) -> p c t", t=CH)
                        ins = dve.tensor_tensor(KhT[:, p, 0:256].rearrange("p (c t) -> p c t", t=CH), c32,
                                                c32[:, :, CH - 1:CH].broadcast_to([P, 8, CH]), ALU.subtract)
                    ins.then_inc(S.decay_ready, 1)
                    dve.wait_ge(S.hx_ready, 7 * l + 7)
                    for p in range(2):
                        step(dve.tensor_scalar(kkT[:, p, :], K[:, p, :], vc(l, KK + p), None, ALU.mult))
                    dve.tensor_tensor(kks, kkT, kkT, ALU.mult).then_inc(S.kk_sq, 1)
                if n == 15:
                    for p in range(2):
                        step(dve.tensor_scalar(bT[:, p, :], aT[:, p, :], -1.0, vc(l, KA + p), ALU.add, ALU.mult))
                    step(dve.scalar_tensor_tensor(out=K, in0=bT, scalar=1.0, in1=K, op0=ALU.add, op1=ALU.mult))
                    dve.wait_ge(S.kk_mm, l + 1)
                    dve.tensor_scalar(msT[:, 0:2 * T].rearrange("p (c t) -> p c t", c=2), ps[:, 2:4, 0:T], 1e-24, None,
                                      ALU.max).then_inc(S.kk_max, 1)
                if n == 17:
                    for p in range(2):
                        ins = dve.scalar_tensor_tensor(out=bonusT[:, p, :], in0=R[:, p, :], scalar=vc(l, RK + p),
                                                       in1=K[:, p, :], op0=ALU.mult, op1=ALU.mult)
                    ins.then_inc(S.bonus_pre, 1)
                    dve.wait_ge(S.rs_ready, NORMS * l + 2)
                    step(dve.tensor_tensor(kkT, kkT, rs(2), ALU.mult))
                    step(dve.tensor_tensor(bT, kkT, aT, ALU.mult))
                if n == 19:
                    dve.wait_ge(S.exp_ready, 4 * l + 4)
                    dve.scalar_tensor_tensor(out=AtT, in0=kkT, scalar=-1.0, in1=AtT, op0=ALU.mult,
                                             op1=ALU.mult).then_inc(S.til_ready, 1)
                    dve.tensor_tensor(BtT, bT, KtT, ALU.mult).then_inc(S.til_ready, 1)
                    dve.tensor_tensor(RtT, R, PtT, ALU.mult).then_inc(S.til_ready, 1)
                if n == 21:
                    dve.wait_ge(S.til_ready, 6 * l + 2)
                    dve.tensor_tensor(KtT, K, KtT, ALU.mult).then_inc(S.til_ready, 1)
                    dve.wait_ge(S.bonus_mm, l + 1)
                    dve.tensor_tensor(bonusT, ps[:, 4:6, 0:T], V, ALU.mult)
                if n == 23:
                    dve.tensor_tensor(bT[:, :, 0:256], bT[:, :, 0:256], KhT[:, :, 0:256],
                                      ALU.mult).then_inc(S.til_ready, 1)
                    dve.tensor_tensor(KhT[:, :, 0:256], K[:, :, 0:256], KhT[:, :, 0:256],
                                      ALU.mult).then_inc(S.til_ready, 1)

            def quad(bank, n):
                return ps[0:n, bank, :].rearrange("p (h t) -> p h t", h=4)[:, :, 0:n]

            def masked(dst, bank, mask, n):
                for q in range(2):
                    ins = dve.tensor_tensor(dst[0:n, q::2, 0:n],
                                            ps[0:n, bank + q, 0:256].rearrange("p (a t) -> p a t", a=2)[:, :, 0:n],
                                            bc(mask[0:n, 0:n], 2), ALU.mult)
                ins.then_inc(S.mat_ev, 1)

            def matrices(l, i):
                n = TILES[i][1]
                g = 3 * l + i
                at = (2 + HALVES) * g

                def half(k):
                    dst, mask = ((ntm, C.m32s), (rbm[i], C.m32i), (rkm[i], C.m32i))[k // 2]
                    dve.wait_ge(S.mat_mm, at + 3 + k)
                    dve.tensor_tensor(dst[0:n, k % 2::2, 0:n],
                                      ps[0:n, 7, 0:256].rearrange("p (a t) -> p a t", a=2)[:, :, 0:n],
                                      bc(mask[0:n, 0:n], 2), ALU.mult).then_inc(S.mat_ev, 1)

                dve.wait_ge(S.mat_mm, at + 1)
                masked(mt16, 4, C.m16t, n)
                dve.wait_ge(S.mat_mm, at + 2)
                masked(m16, 6, C.m16, n)
                masked(moff, 6, C.moff, n)
                yield
                dve.wait_ge(S.mat_ev, (3 + HALVES) * g + 1)
                dve.tensor_tensor(qm[0:n, :, 0:n], mt16[0:n, :, 0:n], bc(C.ident[0:n, 0:n], 4),
                                  ALU.add).then_inc(S.q1_ready, 1)
                half(0)
                yield
                lm, ld = lvl(LVM, l, i), lvl(LVD, l, i)

                def add_to_q(need, have):
                    dve.wait_ge(S.lvl_mm, lm + need)
                    if have:
                        dve.wait_ge(S.lvl_dve, ld + have)
                    dve.tensor_tensor(qm[0:n, :, 0:n], quad(6, n), qm[0:n, :, 0:n], ALU.add).then_inc(S.lvl_dve, 1)

                add_to_q(3, 0)
                half(1)
                yield
                add_to_q(6, 1)
                half(2)
                yield
                add_to_q(8, 2)
                half(3)
                yield
                if i < 2:
                    dve.wait_ge(S.lvl_mm, lm + 10)
                    dve.tensor_copy(m16[0:n, :, 0:n], quad(5, n)).then_inc(S.lvl_dve, 1)
                half(4)
                yield
                if i < 2:
                    add_to_q(11, 3)
                half(5)
                yield
                dve.wait_ge(S.wt_mm, 3 * g + 2)
                dve.tensor_copy(nv[0:n, :], ps[0:n, 5, 0:256]).then_inc(S.nv_ready, 1)
                yield
                yield

            def rwkv(l):
                yield
                for i in range(3):
                    yield from matrices(l, i)
                yield from chain(l)
                for h in range(4):
                    yield
                yield from group_norm(l)

            def chain(l):
                dve.wait_ge(S.wt_act, 6 * l + 6)
                for c in range(NCHUNK):
                    i, r, n = c // 4, CH * (c % 4), min(CH, T - CH * c)
                    if c == 0:
                        dve.tensor_copy(uTok[0:n, 0, :], zTok[0:n, 0, :]).then_inc(S.u_ready, 1)
                    else:
                        dve.wait_ge(S.u_mm, 8 * l + c)
                        for q in range(2):
                            u, z = (x[r:r + n, i, :].rearrange("p (a q v) -> p q a v", q=2, v=NR)[:, q]
                                    for x in (uTok, zTok))
                            ins = dve.tensor_tensor(u, ps[r:r + n, 4 + q, 0:128].rearrange("p (a v) -> p a v", a=2), z,
                                                    ALU.add)
                        ins.then_inc(S.u_ready, 1)
                    yield
                    if c == NCHUNK - 1:
                        break
                    new = ps[:, 6, 0:2 * NR].rearrange("p (a v) -> p a v", a=2)
                    if c == 0:
                        dve.wait_ge(S.st_mm, 8 * l + 1)
                        dve.tensor_copy(stT[:, 1], new).then_inc(S.st_ready, 1)
                    else:
                        step(dve.tensor_tensor(pst, stT[:, c], tail(PtT[:, :, CH * c + CH - 1], NR), ALU.mult))
                        dve.wait_ge(S.st_mm, 8 * l + c + 1)
                        dve.tensor_tensor(stT[:, c + 1], new, pst, ALU.add).then_inc(S.st_ready, 1)
                    dve.wait_ge(S.st_ready, 8 * l + c + 1)
                    yield

            def group_norm(l):
                dve.wait_ge(S.gn_mm, 2 * l + 1)
                dve.scalar_tensor_tensor(out=eT, in0=ps[:, 0:2, 0:T], scalar=-1.0 / NR, in1=eT, op0=ALU.mult,
                                         op1=ALU.add).then_inc(S.gn_cent, 1)
                yield
                yield
                dve.wait_ge(S.gn_inv, l + 1)
                step(dve.tensor_tensor(eT, eT, cumT, ALU.mult))
                for p in range(2):
                    step(dve.tensor_scalar(eT[:, p, :], eT[:, p, :], vc(l, GNG + p), vc(l, GNB + p), ALU.mult, ALU.add))
                step(dve.tensor_tensor(eT, eT, bonusT, ALU.add))
                dve.tensor_tensor(oT[:, 0:2, :], eT, gT, ALU.mult).then_inc(S.oa_ready, 1)
                yield

            def qk_norm_rope(l, k):
                x = cur(Q_CH + 4 * k, 4)
                y = hnT[:, 4 * k:4 * k + 4, :]
                dve.wait_ge(S.rot_mm, 2 * l + k + 1)
                dve.wait_ge(S.qcos_ready, 2 * l + k + 1)
                dve.tensor_tensor(y, ps[:, 0:4, 0:T], bc(sinT, 4), ALU.mult).then_inc(S.rot_read, 1)
                dve.wait_ge(S.rot_read, 2 * l + k + 1)
                step(dve.tensor_tensor(x, x, y, ALU.add))
                yield
                dve.wait_ge(S.rs_ready, NORMS * l + 3 + k)
                dve.tensor_tensor(x, x, rs(4), ALU.mult).then_inc(S.qk_ready, 1)
                yield

            def attention(l):
                yield
                yield
                for k in range(2):
                    yield
                    yield from qk_norm_rope(l, k)
                yield from softmax(l)

            def softmax(l):
                def normalised(h):
                    at = slice(h * T, h * T + T)
                    dve.wait_ge(S.ob_inv, 4 * l + h + 1)
                    dve.scalar_tensor_tensor(out=oT[:, 2 + h, :], in0=oat[:, h, :], scalar=small[:, 8 + l:9 + l],
                                             in1=rsT[:, at], op0=ALU.mult, op1=ALU.mult).then_inc(S.ob_ready, 1)

                def maxima(u):
                    i = u % 3
                    t0, n = TILES[i]
                    b, m = u % 2, t0 + n
                    dve.wait_ge(S.sc_mm, 12 * l + u + 1)
                    step(dve.tensor_reduce(stat[0:n, b, 4:6], ps[0:n, 0:2, 0:m], AXX, ALU.max))
                    dve.tensor_scalar(stat[0:n, b, 0:2], stat[0:n, b, 4:6], -DK ** -0.5, None,
                                      ALU.mult).then_inc(S.mx_ready, 1)

                def difference(u):
                    i = u % 3
                    t0, n = TILES[i]
                    b, m = u % 2, t0 + n
                    dve.wait_ge(S.p_ready, 24 * l + 2 * u + 2)
                    step(dve.reciprocal(stat[0:n, b, 2:4], stat[0:n, b, 2:4]))
                    step(dve.tensor_scalar(stat[0:n, b, 3:4], stat[0:n, b, 3:4], small[0:n, 6 + l:7 + l], None, ALU.mult))
                    step(dve.tensor_scalar(scaled[0:n, 0:m], prob[0:n, b, 1, 0:m], stat[0:n, b, 3:4], None, ALU.mult))
                    if u >= 2:
                        dve.wait_ge(S.pt_mm, 12 * l + u - 1)
                    dve.scalar_tensor_tensor(out=pd[0:n, b, 0:m], in0=prob[0:n, b, 0, 0:m], scalar=stat[0:n, b, 2:3],
                                             in1=scaled[0:n, 0:m], op0=ALU.mult,
                                             op1=ALU.subtract).then_inc(S.pd_ready, 1)

                def turned(u):
                    h, i = u // 3, u % 3
                    t0, n = TILES[i]
                    dve.wait_ge(S.pt_mm, 12 * l + u + 1)
                    if i == 0 and h >= 1:
                        dve.wait_ge(S.o_mm, 4 * l + h)
                    w = min(i + 1, 2)
                    ins = dve.tensor_copy(pT[:, 0:w, t0:t0 + n],
                                          ps[:, 2, :].rearrange("p (k t) -> p k t", t=P)[:, 0:w, 0:n])
                    if i == 2:
                        ins = dve.tensor_copy(pT[0:n, 2, t0:t0 + n], ps[0:n, 2, 2 * P:2 * P + n])
                    ins.then_inc(S.pt_ready, 1)

                for u in range(14):
                    if u >= 2:
                        turned(u - 2)
                    if u < 12:
                        maxima(u)
                    if u >= 5 and u % 3 == 2:
                        normalised(u // 3 - 1)
                    yield
                    if 1 <= u < 13:
                        difference(u - 1)
                    if u == 13:
                        normalised(3)
                    yield

            def low(g, slot_no):
                dve.tensor_tensor(w_lo[:, g % PARTS, :], slot(slot_no), w_hi[:, g % PARTS, :],
                                  ALU.subtract).then_inc(S.lo_ready, 1)

            def dense_low(j):
                dve.wait_ge(S.hi_ready, j + 1)
                low(j, slot_of[MIXN + j])

            def item_low(i, j):
                dve.wait_ge(S.hi_ready, i * FFNN + (FFNN + j + 1))
                low(j, j % ITEM_RING)

            for c in range(DC):
                dve.wait_ge(S.x_mm, c + 1)
                dve.tensor_copy(hT[:, c, :], ps[:, c % 2, 0:T]).then_inc(S.h_ready, 1)
            in_low(0, 0)
            dve.wait_ge(S.vcol_mm, 1)
            dve.tensor_copy(vcol[:], ps[:, 2, 0:DEPTH * ROWS]).then_inc(S.vcol_ready, 1)
            dve.wait_ge(S.vcol_ready, 1)
            for l in range(DEPTH):
                dve.tensor_scalar(vhalf[:, l, 0:2], vc(l, W0, 2), 0.5, None, ALU.mult)
                dve.tensor_scalar(vhalf[:, l, 2:4], vc(l, A0, 2), 0.5, None, ALU.mult).then_inc(S.vhalf_ready, 1)
                dve.tensor_scalar(small[:, 8 + l:9 + l], vc(l, SUBG), 1.0 - LAM_INIT[l], None, ALU.mult)
                dve.tensor_tensor(small[:, l:l + 1], vc(l, LAMQ), vc(l, LAMK), ALU.mult).then_inc(S.lam_prod, 1)
            def lambdas():
                dve.wait_ge(S.lam_exp, 2)
                step(dve.tensor_tensor(small[:, 6:8], small[:, 2:4], small[:, 4:6], ALU.subtract))
                for l in range(DEPTH):
                    step(dve.tensor_scalar(small[:, 6 + l:7 + l], small[:, 6 + l:7 + l], LAM_INIT[l], None, ALU.add))

            for l in range(DEPTH):
                if l:
                    in_low(l, 0)
                norm(2 * l, MIXG)
                for c in range(DC):
                    dve.wait_ge(S.xp_hi_ready, DC * l + c + 1)
                    dve.tensor_tensor(xp_lo[:, c, :], hnT[:, c, :], xp_hi[:, c, :],
                                      ALU.subtract).then_inc(S.xp_lo_ready, 1)
                in_low(l, 1)
                if l == 0:
                    lambdas()
                for n in range(1, NCH, 2):
                    dve.wait_ge(S.proj_mm, NCH * l + n + 1)
                    dve.tensor_copy(projT[:, n, 2:T + 2], ps[:, 1, 0:T]).then_inc(S.proj_dve, 1)
                    if n // 2 + IN_PARTS <= NCH // 2:
                        in_low(l, n // 2 + IN_PARTS)
                    prep(l, n)
                together(rwkv(l), attention(l))
                for c in range(DC):
                    dve.wait_ge(S.wout_mm, DC * l + c + 1)
                    dve.tensor_tensor(hT[:, c, :], ps[:, (4 + c) % 8, 0:T], hT[:, c, :], ALU.add).then_inc(S.h_ready, 1)
                if l == 0:
                    dense_low(0)
                norm(2 * l + 1, FFNG)
                if l == 0:
                    for c in range(DC):
                        dve.wait_ge(S.xd_hi_ready, c + 1)
                        dve.tensor_tensor(xd_lo[:, c, :], hnT[:, c, :], xd_hi[:, c, :],
                                          ALU.subtract).then_inc(S.xd_lo_ready, 1)
                    dense_low(1)
                    dense_low(2)
                    for j in range(FFNN):
                        s = j // 2
                        if j % 2 and s < FC // 2:
                            b = 4 * (s % 2) + 2
                            dve.wait_ge(S.silu_ready, s + 1)
                            dve.tensor_tensor(hmd[:, s % 2], ps[:, b:b + 2, 0:T], sgd[:, s % 2],
                                              ALU.mult).then_inc(S.hid_prod, 1)
                        if j + PARTS < FFNN:
                            dense_low(j + PARTS)
                        if j % 2 and s < FC // 2:
                            dve.wait_ge(S.hd_hi_ready, s + 1)
                            dve.tensor_tensor(hd_lo[:, 2 * s:2 * s + 2, :], hmd[:, s % 2], hd_hi[:, 2 * s:2 * s + 2, :],
                                              ALU.subtract).then_inc(S.hd_lo_ready, 1)
                    for c in range(DC):
                        if c < DC - 1:
                            dve.wait_ge(S.down_mm, c + 1)
                        else:
                            dve.wait_ge(S.parts_used, FFNN)
                        dve.tensor_tensor(hT[:, c, :], ps[:, c, 0:T], hT[:, c, :], ALU.add).then_inc(S.h_ready, 1)

            item_low(0, 0)
            for r in range(NFLAG // NE):
                dve.tensor_copy(ev[0:1, NE * r:NE * r + NE], iotaT[0:1, 0:NE])
                dve.memset(ov[0:1, NE * r:NE * r + NE], float(CAP * (r + 1)))
            step(dve.memset(fsum[:], 0.0))
            step(dve.tensor_copy(fsum[0:1, 0, 0:NE], iotaT[0:1, 0:NE]))
            dve.wait_ge(S.lg_mm, 1)
            step(dve.tensor_copy(lgS, ps[:, 0, 0:NT * NE].rearrange("p (i e) -> p i e", e=NE)))
            for i in range(NT):
                step(dve.max(top8[:, i, :], lgS[:, i, :]))
                step(dve.max_index(idx8[:, i, :], top8[:, i, :], lgS[:, i, :]))
            dve.tensor_tensor(gw[:, :, 1], top8[:, :, 1], top8[:, :, 0], ALU.subtract).then_inc(S.gap_ready, 1)
            step(dve.tensor_copy(fidx, idx8[:, :, 0:2]))
            for j, oh in ((0, oh1), (1, oh2)):
                step(dve.tensor_tensor(oh, bc(iotaT[:, 0:NE], NT), tail(fidx[:, :, j], NE), ALU.is_equal))
            dve.tensor_tensor(sel, oh1, oh2, ALU.add).then_inc(S.sel_ready, 1)
            dve.wait_ge(S.gap_exp, 1)
            step(dve.tensor_scalar(gw[:, :, 0], gw[:, :, 1], 1.0, None, ALU.add))
            step(dve.reciprocal(gw[:, :, 0], gw[:, :, 0]))
            step(dve.tensor_tensor(gw[:, :, 1], gw[:, :, 1], gw[:, :, 0], ALU.mult))
            for j, oh in ((0, oh1), (1, oh2)):
                step(dve.tensor_tensor(oh, oh, tail(gw[:, :, j], NE), ALU.mult))
            step(dve.tensor_tensor(gates, oh1, oh2, ALU.add))
            dve.wait_ge(S.pos_mm, 1)
            step(dve.tensor_copy(posx, ps[:, 1, 0:NT * NE].rearrange("p (i e) -> p i e", e=NE)))
            step(dve.scalar_tensor_tensor(out=posx, in0=posx, scalar=1.0, in1=sel, op0=ALU.add, op1=ALU.mult))
            step(dve.tensor_scalar(posx, posx, -1.0, None, ALU.add))
            def one_hot(k):
                if k is None:
                    e, first = 0, 0
                else:
                    e = dve.value_load(tab[0:1, 0, bass.ds(k, 1)], min_val=0, max_val=NE - 1)
                    first = dve.value_load(tab[0:1, 1, bass.ds(k, 1)], min_val=0, max_val=wide - CAP)
                for i, (t0, n) in enumerate(OUT_TILES):
                    dve.tensor_scalar(oneh[0:n, i, :], iotaT[0:n, bass.ds(first, CAP)], posx[0:n, i, bass.ds(e, 1)],
                                      None, ALU.is_equal)
                dve.tensor_copy(gsel, gates[:, :, bass.ds(e, 1)]).then_inc(S.oneh_ready, 1)

            def gathered_low(i):
                for half in range(2):
                    dve.wait_ge(S.xm_hi_ready, 2 * i + (half + 1))
                    dve.tensor_tensor(xm_lo[:, 4 * half:4 * half + 4, :],
                                      ps[:, 4 + half, 0:4 * CAP].rearrange("p (c t) -> p c t", c=4),
                                      xm_hi[:, 4 * half:4 * half + 4, :], ALU.subtract).then_inc(S.xm_lo_ready, 1)

            def slot_gates(i):
                dve.wait_ge(S.gslot_mm, i + 1)
                dve.tensor_copy(gslot[0:CAP, :], ps[0:CAP, 7, 0:1]).then_inc(S.gslot_ready, 1)

            assert PARTS == 3
            step(dve.tensor_copy(cnt[0:1, 0:NE], ps[0:1, 1, NT * NE:(NT + 1) * NE]))
            one_hot(None)
            for r in range(NFLAG // NE):
                step(dve.tensor_scalar(flag[0:1, NE * r:NE * r + NE], cnt[0:1, 0:NE], float(CAP * (r + 1)), None,
                                       ALU.is_gt))
            step(dve.tensor_tensor_scan(incl[0:1, :], C.ones[0:1, 0:NFLAG], flag[0:1, :], 0.0, ALU.mult, ALU.add))
            step(dve.tensor_scalar(ntab[:], incl[0:1, NFLAG - 1:NFLAG], float(NE), None, ALU.add))
            step(dve.tensor_tensor(incl[0:1, :], incl[0:1, :], flag[0:1, :], ALU.mult))
            step(dve.tensor_tensor(eqg[0:1], bc(incl[0:1, :], MAXO), tail(iotaT[0:1, 1:1 + MAXO], NFLAG), ALU.is_equal))
            for row, values in ((0, ev), (1, ov)):
                step(dve.tensor_tensor(pick[0:1], eqg[0:1], bc(values[0:1, :], MAXO), ALU.mult))
                step(dve.tensor_reduce(fsum[0:1, row, NE:NE + MAXO], pick[0:1], AXX, ALU.add))
            dve.tensor_copy(tab[:], fsum[:]).then_inc(S.table_ready, 1)
            dve.tensor_copy(small[:, 10:11], small[:, 9:10]).then_inc(S.h_item, DC)
            gathered_low(0)
            for j in range(1, PARTS):
                item_low(0, j)
            dve.wait_ge(S.table_ready, 1)
            slot_gates(0)
            n_items = dve.value_load(ntab[0:1, 0:1], min_val=NE, max_val=NE + MAXO)
            with dve.Fori(0, n_items) as i:
                for j in range(FFNN):
                    s = j // 2
                    if j + PARTS < FFNN:
                        item_low(i, j + PARTS)
                    elif j + PARTS == FFNN:
                        item_low(i + 1, 0)
                    if j == FC + 2:
                        one_hot(i + 1)
                    if j % 2 and s < FC // 2:
                        dve.wait_ge(S.msilu_ready, i * (FC // 2) + (s + 1))
                        dve.tensor_tensor(hmTok[0:CAP, s % 2, :], ps[0:CAP, 2 + s % 2, 0:PIECE], sgm[0:CAP, s % 2, :],
                                          ALU.mult).then_inc(S.mhid_prod, 1)
                    if j % 2 and 1 <= s <= FC // 2:
                        dve.wait_ge(S.hm_hi_ready, i * (FC // 2) + s)
                        dve.tensor_tensor(hm_lo[:, 2 * s - 2:2 * s, :],
                                          ps[:, 4 + (s - 1) % 2, 0:2 * CAP].rearrange("p (c t) -> p c t", c=2),
                                          hm_hi[:, 2 * s - 2:2 * s, :], ALU.subtract).then_inc(S.hm_lo_ready, 1)
                for z in range(2):
                    dve.wait_ge(S.y_hi_ready, 2 * i + (z + 1))
                    dve.scalar_tensor_tensor(out=y_lo[0:CAP, 512 * z:512 * z + 512], in0=ps[0:CAP, 6 + z, :],
                                             scalar=gslot[0:CAP, :], in1=y_hi[0:CAP, 512 * z:512 * z + 512],
                                             op0=ALU.mult, op1=ALU.subtract).then_inc(S.y_lo_ready, 1)
                item_low(i + 1, 1)
                gathered_low(i + 1)
                for c in range(DC):
                    dve.wait_ge(S.scat_mm, DC * i + (c + 1))
                    dve.tensor_tensor(hT[:, c, META:T], ps[:, c % 4, 0:SEQ], hT[:, c, META:T],
                                      ALU.add).then_inc(S.h_item, 1)
                slot_gates(i + 1)
                item_low(i + 1, 2)
            for i, (t0, n) in enumerate(OUT_TILES):
                dve.wait_ge(S.out_mm, 2 * i + 2)
                dve.tensor_copy(hnTok[0:n, i, 512:1024], ps[0:n, 2 * (i % 2) + 1, :]).then_inc(S.out_dve, 1)

        @block.tensor
        def _(pe):
            mm = pe.matmul

            def group(out, pairs, start=True, stop=True, **kw):
                pairs = list(pairs)
                for k, (a, b) in enumerate(pairs):
                    ins = mm(out, a, b, start=start and k == 0, stop=stop and k == len(pairs) - 1, **kw)
                return ins

            def piece_view(k, n):
                return slot(slot_of[k])[:, 0:DC * n].rearrange("p (c n) -> p c n", c=DC)

            def norm_sum(idx):
                for c in range(DC):
                    for k, (a, b) in enumerate(SQUARED):
                        if c == a:
                            pe.wait_ge(S.sq_ready, len(SQUARED) * idx + k + 1)
                    ins = mm(ps[:, NORM_BANK[idx], 0:T], C.ones, sqT[:, c, :], start=c == 0, stop=c == DC - 1)
                ins.then_inc(S.nsum_mm, 1)

            def project(l, n):
                q = n // 2
                width = min(PIECE, IN_COLS - PIECE * q)
                w = [x[:, q % IN_PARTS, 0:DC * width].rearrange("p (c n) -> p c n", c=DC) for x in (wp_hi, wp_lo)]
                if n % 2 == 0:
                    pe.wait_ge(S.wp_lo_ready, (NCH // 2 + 1) * l + q + 1)
                    if n:
                        pe.wait_ge(S.proj_act, 13 * l + n // 2)
                elif n > 1:
                    pe.wait_ge(S.proj_dve, 12 * l + n // 2)
                for c in range(DC):
                    if n == 0:
                        pe.wait_ge(S.xp_lo_ready, DC * l + c + 1)
                    ins = split_products(ps[:, n % 2, 0:T], [x[:, c, P * (n % 2):P * (n % 2) + P] for x in w],
                                         [x[:, c, :] for x in (xp_hi, xp_lo)], c == 0, c == DC - 1)
                ins.then_inc(S.proj_mm, 1)

            def rwkv_lora(l):
                pe.wait_ge(S.lora_w_in, 48 * (l + 1))
                pe.wait_ge(S.lora_act, 3 * l + 3)
                pe.wait_ge(S.lora_sig, l + 1)
                for k, (a, b) in enumerate(((0, 32), (32, 64), (64, 128))):
                    for p in range(2):
                        ins = mm(ps[:, 2 + 2 * k + p, 0:T], lora_w[a:b, P * p:P * p + P], lora[a:b, :],
                                 start=True, stop=True)
                    ins.then_inc(S.lora_mm, 1)

            def head_sums(bank, x, signal):
                for p in range(x.shape[1]):
                    ins = mm(ps[:, bank + p, 0:T], C.blk, x[:, p, :], start=True, stop=True)
                ins.then_inc(signal, 1)

            def token_rows(l):
                V = hxT[:, 4:6, :]
                k = 0
                for i, (t0, n) in enumerate(TILES):
                    for bank, (x, y) in ((4, (AtT, V)), (5, (bT, KhT)))[:2 if i < 2 else 1]:
                        if k == 0:
                            pe.wait_ge(S.til_ready, 6 * l + 6)
                        if i:
                            pe.wait_ge(S.tok_ready, 5 * l + k - 1)
                        for j, z in enumerate((x, y)):
                            for p in range(2):
                                ins = pe.transpose(ps[0:n, bank, 256 * j + P * p:256 * j + P * p + P],
                                                   z[:, p, t0:t0 + n], C.ident)
                        ins.then_inc(S.tok_mm, 1)
                        k += 1

            def matrices(l, i):
                t0, n = TILES[i]
                g = 3 * l + i
                lm, la, ld = lvl(LVM, l, i), lvl(LVA, l, i), lvl(LVD, l, i)

                def products(bank, x, y):
                    for p in range(2):
                        for q in range(2):
                            ins = mm(ps[0:n, bank + q, P * p:P * p + n], x[64 * q:64 * q + 64, p, t0:t0 + n],
                                     y[64 * q:64 * q + 64, p, t0:t0 + n], start=True, stop=True)
                    ins.then_inc(S.mat_mm, 1)

                def quad(bank, x, y):
                    for h in range(4):
                        ins = mm(ps[0:n, bank, P * h:P * h + n], x[0:n, h, 0:n], y[0:n, h, 0:n], start=True, stop=True)
                    ins.then_inc(S.lvl_mm, 1)

                def half(k):
                    x, y = ((KtT, AtT), (BtT, RtT), (KtT, RtT))[k // 2]
                    q = k % 2
                    pe.wait_ge(S.mat_ev, (3 + HALVES) * g + 3 + k)
                    for p in range(2):
                        ins = mm(ps[0:n, 7, P * p:P * p + n], x[64 * q:64 * q + 64, p, t0:t0 + n],
                                 y[64 * q:64 * q + 64, p, t0:t0 + n], start=True, stop=True)
                    ins.then_inc(S.mat_mm, 1)

                if i:
                    pe.wait_ge(S.wt_act, 2 * g)
                    pe.wait_ge(S.mat_ev, (3 + HALVES) * g)
                    pe.wait_ge(S.nv_ready, g)
                else:
                    pe.wait_ge(S.tok_ready, 5 * l + 5)
                products(4, BtT, AtT)
                products(6, AtT, BtT)
                yield
                pe.wait_ge(S.mat_ev, (3 + HALVES) * g + 3)
                quad(4, m16, mt16)
                quad(5, mt16, m16)
                half(0)
                yield
                pe.wait_ge(S.q1_ready, g + 1)
                pe.wait_ge(S.lvl_act, la + 2)
                quad(6, m2, qm)
                quad(4, m2, mt2)
                quad(5, mt2, m2)
                half(1)
                yield
                pe.wait_ge(S.lvl_act, la + 4)
                pe.wait_ge(S.lvl_dve, ld + 1)
                quad(6, m16, qm)
                quad(5, mt16, m16)
                half(2)
                yield
                pe.wait_ge(S.lvl_act, la + 5)
                pe.wait_ge(S.lvl_dve, ld + 2)
                quad(6, m2, qm)
                half(3)
                yield
                pe.wait_ge(S.lvl_dve, ld + 3)
                if i < 2:
                    for h in range(4):
                        ins = pe.transpose(ps[0:n, 4, P * h:P * h + n], qm[0:n, h, 0:n], C.ident[0:n, 0:n])
                    ins.then_inc(S.lvl_mm, 1)
                    quad(5, moff, qm)
                half(4)
                yield
                if i < 2:
                    pe.wait_ge(S.lvl_act, la + 6)
                    pe.wait_ge(S.lvl_dve, ld + 4)
                    quad(6, mt2, m16)
                half(5)
                yield
                if i < 2:
                    pe.wait_ge(S.lvl_dve, ld + 5)
                for h in range(4):
                    p, q = h // 2, 64 * (h % 2)
                    ins = mm(ps[q:q + 64, 4, P * p:P * p + n], tokAV[0:n, i, 0, 64 * h:64 * h + 64], qm[0:n, h, 0:n],
                             start=True, stop=True)
                ins.then_inc(S.wt_mm, 1)
                for h in range(4):
                    ins = mm(ps[0:n, 5, 64 * h:64 * h + 64], ntm[0:n, h, 0:n], tokAV[0:n, i, 1, 64 * h:64 * h + 64],
                             start=True, stop=True)
                ins.then_inc(S.wt_mm, 1)
                yield
                pe.wait_ge(S.nv_ready, g + 1)
                for h in range(4):
                    ins = mm(ps[0:n, 6, 64 * h:64 * h + 64], qm[0:n, h, 0:n], nv[0:n, 64 * h:64 * h + 64],
                             start=True, stop=True)
                ins.then_inc(S.wt_mm, 1)
                yield

            def y_within(i):
                t0, n = TILES[i]
                for h in range(4):
                    q = 64 * (h % 2)
                    mm(ps[q:q + 64, h, t0:t0 + n], tokAV[0:n, i, 1, 64 * h:64 * h + 64], rkm[i][0:n, h, 0:n],
                       start=i == 0, stop=False, skip_group_check=True)
                    mm(ps[q:q + 64, h, t0:t0 + n], uTok[0:n, i, 64 * h:64 * h + 64], rbm[i][0:n, h, 0:n],
                       start=False, stop=False, skip_group_check=True)

            def y_carried(c):
                t0, n = CH * c, min(CH, T - CH * c)
                for h in range(4):
                    p, q = h // 2, 64 * (h % 2)
                    ins = mm(ps[q:q + 64, h, t0:t0 + n], stT[q:q + 64, c, p, :], RtT[q:q + 64, p, t0:t0 + n],
                             start=False, stop=True, skip_group_check=True)
                return ins

            def chain(l):
                pe.wait_ge(S.wt_act, 6 * l + 6)
                for c in range(NCHUNK):
                    i, r, n = c // 4, CH * (c % 4), min(CH, T - CH * c)
                    if c:
                        pe.wait_ge(S.st_ready, 8 * l + c)
                        for h in range(4):
                            p, q = h // 2, 64 * (h % 2)
                            ins = mm(ps[r:r + n, 4 + h % 2, 64 * p:64 * p + 64], wT[q:q + 64, p, CH * c:CH * c + n],
                                     stT[q:q + 64, c, p, :], start=True, stop=True)
                        ins.then_inc(S.u_mm, 1)
                    if c >= NCHUNK - 3:
                        y_carried((1, 4, 6)[c - (NCHUNK - 3)])
                    yield
                    if c == NCHUNK - 1:
                        break
                    for h in range(4):
                        p, q = h // 2, 64 * (h % 2)
                        mm(ps[q:q + 64, 6, 64 * p:64 * p + 64], tokBK[r:r + n, i, 1, 64 * h:64 * h + 64],
                           tokAV[r:r + n, i, 1, 64 * h:64 * h + 64], start=p == 0, stop=False, skip_group_check=True)
                    pe.wait_ge(S.u_ready, NCHUNK * l + c + 1)
                    for h in range(4):
                        p, q = h // 2, 64 * (h % 2)
                        ins = mm(ps[q:q + 64, 6, 64 * p:64 * p + 64], tokBK[r:r + n, i, 0, 64 * h:64 * h + 64],
                                 uTok[r:r + n, i, 64 * h:64 * h + 64], start=False, stop=True, skip_group_check=True)
                    ins.then_inc(S.st_mm, 1)
                    if c == NCHUNK - 4:
                        pe.wait_ge(S.p_ready, 24 * (l + 1))
                        pe.wait_ge(S.pt_ready, 12 * (l + 1))
                        pe.wait_ge(S.ob_root, 4 * (l + 1))
                        y_within(0)
                    if c == NCHUNK - 3:
                        y_carried(2)
                        y_carried(3)
                    if c == NCHUNK - 2:
                        y_carried(5)
                    yield

            def outputs(l):
                pe.wait_ge(S.u_ready, NCHUNK * (l + 1))
                y_within(1)
                yield
                y_within(2)
                yield
                y_carried(NCHUNK - 2)
                yield
                y_carried(NCHUNK - 1).then_inc(S.y_mm, 1)
                yield
                project_early(l, 0)
                pe.wait_ge(S.y_sb, 2 * l + 2)
                head_sums(0, eT, S.gn_mm)
                project_early(l, 1)
                yield
                pe.wait_ge(S.gn_sq, l + 1)
                head_sums(2, cumT, S.gn_mm)
                project_early(l, 2)
                yield
                project_early(l, 3)
                yield

            def rwkv(l):
                token_rows(l)
                yield
                for i in range(3):
                    yield from matrices(l, i)
                yield from chain(l)
                yield from outputs(l)

            def attention(l):
                yield
                for i, (t0, n) in enumerate(TILES):
                    for h in range(4):
                        ins = pe.transpose(ps[0:n, i, P * h:P * h + P], cur(V_CH + h)[:, 0, t0:t0 + n], C.ident)
                    ins.then_inc(S.vt_mm, 1)
                yield
                for k in range(2):
                    pe.wait_ge(S.qk_sq, 2 * l + k + 1)
                    if k == 0:
                        pe.wait_ge(S.vt_ready, 3 * l + 3)
                    else:
                        pe.wait_ge(S.rot_read, 2 * l + 1)
                    head_sums(0, sqT[:, 4 * k:4 * k + 4, :], S.qk_mm)
                    yield
                    pe.wait_ge(S.qg_ready, 8 * l + 4 * k + 4)
                    pe.wait_ge(S.root_ready, NORMS * l + 3 + k)
                    for c in range(4):
                        ins = mm(ps[:, c, 0:T], C.rope, hnT[:, 4 * k + c, :], start=True, stop=True)
                    ins.then_inc(S.rot_mm, 1)
                    yield
                    yield

                def scores(u):
                    h, i = u // 3, u % 3
                    t0, n = TILES[i]
                    b, m = u % 2, t0 + n
                    if u >= 1:
                        pe.wait_ge(S.p_ready, 24 * l + 2 * u)
                    for c in range(2):
                        q = 64 * c
                        mm(ps[0:n, c, 0:m], projT[q:q + 64, Q_CH + h, 2 + t0:2 + t0 + n],
                           projT[q:q + 64, K_CH + h, 2:2 + m], start=True, stop=False, skip_group_check=True)
                        ins = mm(ps[0:n, c, t0:m], C.ident[0:n, 0:n], C.causal[0:n, 0:n],
                                 start=False, stop=True, skip_group_check=True)
                    ins.then_inc(S.sc_mm, 1)

                def turn(u):
                    h, i = u // 3, u % 3
                    t0, n = TILES[i]
                    pe.wait_ge(S.pd_ready, 12 * l + u + 1)
                    if u:
                        pe.wait_ge(S.pt_ready, 12 * l + u)
                    for k in range(i + 1):
                        k0, kn = TILES[k]
                        ins = pe.transpose(ps[0:kn, 2, P * k:P * k + n], pd[0:n, u % 2, k0:k0 + kn], C.ident[0:n, 0:n])
                    ins.then_inc(S.pt_mm, 1)

                def values(h):
                    pe.wait_ge(S.pt_ready, 12 * l + 3 * h + 3)
                    if h:
                        pe.wait_ge(S.ob_root, 4 * l + h)
                    for k, (k0, kn) in enumerate(TILES):
                        ins = mm(ps[:, 3, k0:T], vTok[0:kn, k, P * h:P * h + P], pT[0:kn, k, k0:T],
                                 start=k == 0, stop=k == 2, skip_group_check=True)
                    ins.then_inc(S.o_mm, 1)

                pe.wait_ge(S.qk_ready, 2 * l + 2)
                for u in range(14):
                    if u < 12:
                        scores(u)
                    if u >= 4 and u % 3 == 1:
                        values(u // 3 - 1)
                    yield
                    if 1 <= u < 13:
                        turn(u - 1)
                    if u >= 4 and u % 3 == 1:
                        h = u // 3 - 1
                        pe.wait_ge(S.osq_ready, 4 * l + h + 1)
                        mm(ps[:, 3, 0:T], C.ones, sqT[:, h, :], start=True, stop=True).then_inc(S.ob_mm, 1)
                    yield

            EARLY = 4

            def w_out_chunk(l, d):
                k = (MIXN + FFNN) * l + -(-IN_COLS // PIECE) + d // 2
                if d % 2 == 0:
                    pe.wait_ge(loaded[slot_of[k]], 16 * load_value[k])
                return piece_view(k, PIECE)[:, :, P * (d % 2):P * (d % 2) + P]

            def project_early(l, d):
                if d == 0:
                    pe.wait_ge(S.oc_ready, l + 1)
                    pe.wait_ge(S.ob_ready, 4 * l + 4)
                w = w_out_chunk(l, d)
                group(ps[:, 4 + d, 0:T], ((w[:, c, :], oT[:, c, :]) for c in range(2, DC)), stop=False,
                      skip_group_check=True)

            def project_out(l):
                pe.wait_ge(S.oa_ready, l + 1)
                for d in range(DC):
                    if d < EARLY:
                        k = (MIXN + FFNN) * l + -(-IN_COLS // PIECE) + d // 2
                        w = piece_view(k, PIECE)[:, :, P * (d % 2):P * (d % 2) + P]
                    else:
                        w = w_out_chunk(l, d)
                    ins = group(ps[:, (4 + d) % 8, 0:T], ((w[:, c, :], oT[:, c, :]) for c in range(2 if d < EARLY else DC)),
                                start=d >= EARLY, skip_group_check=True)
                    ins.then_inc(S.wout_mm, 1)

            def split_products(out, lhs, rhs, first, last):
                pairs = ((0, 0), (0, 1), (1, 0))
                for k, (a, b) in enumerate(pairs):
                    ins = mm(out, lhs[a], rhs[b], start=first and k == 0, stop=last and k == 2)
                return ins

            def weights(j, width):
                return [w[:, j % PARTS, :].rearrange("p (c n) -> p c n", n=width) for w in (w_hi, w_lo)]

            pe.wait_ge(S.consts_in, 16)
            pe.wait_ge(S.x_in, 64)
            for c in range(DC):
                if c >= 2:
                    pe.wait_ge(S.h_ready, c - 1)
                for i, (t0, n) in enumerate(TILES):
                    ins = pe.transpose(ps[:, c % 2, t0:t0 + n], xTok[0:n, i, P * c:P * c + P], C.ident[0:n, 0:n])
                ins.then_inc(S.x_mm, 1)
            norm_sum(0)
            pe.wait_ge(S.params_act, 16 * len(tall))
            pe.wait_ge(S.params_pool, 16 * len(halves))
            nr = DEPTH * ROWS
            pe.transpose(ps[:, 2, 0:nr], vrow[0:nr, :], C.ident[0:nr, 0:nr]).then_inc(S.vcol_mm, 1)
            pe.wait_ge(S.lam_prod, DEPTH)
            mm(ps[:, 3, 0:DEPTH], C.ones[0:64, :], small[0:64, 0:DEPTH], start=True, stop=True).then_inc(S.lam_mm, 1)
            mm(ps[:, 4, 0:DEPTH], C.ones[64:P, :], small[64:P, 0:DEPTH], start=True, stop=True).then_inc(S.lam_mm, 1)

            for l in range(DEPTH):
                if l:
                    norm_sum(2 * l)
                for n in range(NCH):
                    project(l, n)
                    if n == 9:
                        if l == 0:
                            pe.wait_ge(S.lam_exp, 2)
                        rwkv_lora(l)
                    if n == 15:
                        pe.wait_ge(S.kk_sq, l + 1)
                        pe.wait_ge(S.lora_out, 5 * l + 5)
                        head_sums(2, kks, S.kk_mm)
                    if n == 19:
                        pe.wait_ge(S.bonus_pre, l + 1)
                        head_sums(4, bonusT, S.bonus_mm)
                together(rwkv(l), attention(l))
                project_out(l)
                norm_sum(2 * l + 1)
                if l == 0:
                    for j in range(2 * (FC // 2)):
                        s, z = j // 2, j % 2
                        pe.wait_ge(S.lo_ready, j + 1)
                        w = weights(j, PIECE)
                        if z == 0 and s >= 2:
                            pe.wait_ge(S.hid_prod, s - 1)
                        for half in range(2):
                            for c in range(DC):
                                if j == 0 and half == 0:
                                    pe.wait_ge(S.xd_lo_ready, c + 1)
                                ins = split_products(ps[:, 4 * (s % 2) + 2 * z + half, 0:T],
                                                     [x[:, c, P * half:P * half + P] for x in w],
                                                     [x[:, c, :] for x in (xd_hi, xd_lo)], c == 0, c == DC - 1)
                        ins.then_inc(S.parts_used, 1)
                    for f in range(FC):
                        j = FC + f // 2
                        if f % 2 == 0:
                            pe.wait_ge(S.lo_ready, j + 1)
                            w = weights(j, D)
                        if f == 0:
                            pe.wait_ge(S.hid_prod, FC // 2)
                        if f == FC - 4:
                            pe.wait_ge(S.hd_lo_ready, FC // 2 - 1)
                        if f == FC - 2:
                            pe.wait_ge(S.hd_lo_ready, FC // 2)
                        elif f == 0:
                            pe.wait_ge(S.hd_lo_ready, FC // 2 - 2)
                        for d in range(DC):
                            ins = split_products(ps[:, d, 0:T], [x[:, f % 2, P * d:P * d + P] for x in w],
                                                 [x[:, f, :] for x in (hd_hi, hd_lo)], f == 0, f == FC - 1)
                            if f == FC - 1 and d < DC - 1:
                                ins.then_inc(S.down_mm, 1)
                        if f % 2:
                            ins.then_inc(S.parts_used, 1)

            pe.wait_ge(S.hn_ready, 4 * DC)
            pe.wait_ge(S.router_in, 16)
            for i, (t0, n) in enumerate(OUT_TILES):
                ins = group(ps[0:n, 0, NE * i:NE * i + NE], ((hnT[:, c, t0:t0 + n], router[:, c, :])
                                                             for c in range(DC)))
            ins.then_inc(S.lg_mm, 1)
            for k in range(2 * NT):
                i, half = k // 2, k % 2
                t0, n = OUT_TILES[i]
                if k >= 2:
                    pe.wait_ge(S.hntok_ready, k - 1)
                for c in range(4):
                    ins = pe.transpose(ps[0:n, 2 + half, P * c:P * c + P], hnT[:, 4 * half + c, t0:t0 + n], C.ident)
                ins.then_inc(S.hntok_mm, 1)
            pe.wait_ge(S.sel_ready, 1)
            for i, (t0, n) in enumerate(OUT_TILES):
                group(ps[0:n, 1, NE * i:NE * i + NE],
                      [(C.ones[:, 0:n], sel[:, j, :]) for j in range(i)] + [(C.tri[0:n, 0:n], sel[0:n, i, :])])
            group(ps[0:1, 1, NT * NE:(NT + 1) * NE], [(C.ones[0:n, 0:1], sel[0:n, i, :]) for i, (t0, n) in enumerate(OUT_TILES)]
                  ).then_inc(S.pos_mm, 1)

            pe.wait_ge(S.hntok_ready, 2 * NT)

            def gather(i):
                pe.wait_ge(S.oneh_ready, i + 1)
                for c in range(DC):
                    ins = group(ps[:, 4 + c // 4, CAP * (c % 4):CAP * (c % 4) + CAP],
                                ((hnTok[0:n, i, P * c:P * c + P], oneh[0:n, i, :])
                                 for i, (t0, n) in enumerate(OUT_TILES)))
                    if c % 4 == 3:
                        ins.then_inc(S.gather_mm, 1)

            def turn_slots():
                for i, (t0, n) in enumerate(OUT_TILES):
                    ins = pe.transpose(ps[0:CAP, 6, t0 - META:t0 - META + n], oneh[0:n, i, :], C.ident[0:n, 0:n])
                ins.then_inc(S.oht_mm, 1)
                group(ps[0:CAP, 7, 0:1], ((oneh[0:n, i, :], gsel[0:n, i, :]) for i, (t0, n) in enumerate(OUT_TILES))
                      ).then_inc(S.gslot_mm, 1)

            gather(0)
            turn_slots()
            pe.wait_ge(S.table_ready, 1)
            n_items = pe.value_load(ntab[0:1, 0:1], min_val=NE, max_val=NE + MAXO)
            with pe.Fori(0, n_items) as it:
                pairs = FC // 2
                for j in range(FFNN):
                    pe.wait_ge(S.lo_ready, it * FFNN + (FFNN + j + 1))
                    s, z = j // 2, j % 2
                    if j < 2 * pairs:
                        w = weights(j, PIECE)
                        if z == 0 and s >= 2:
                            pe.wait_ge(S.mhid_prod, it * pairs + (s - 1))
                        if s < 2:
                            pe.wait_ge(S.h_item, it * DC + (5, 7, 7, 8)[j])
                        for c in range(DC):
                            if j == 0 and c % 4 == 0:
                                pe.wait_ge(S.xm_lo_ready, 2 * it + (c // 4 + 1))
                            ins = split_products(ps[0:CAP, 2 * z + s % 2, 0:PIECE], [x[:, c, :] for x in (xm_hi, xm_lo)],
                                                 [x[:, c, :] for x in w], c == 0, c == DC - 1)
                    else:
                        w = weights(j, D)
                        if j == 2 * pairs:
                            pe.wait_ge(S.oht_ready, it + 1)
                            pe.wait_ge(S.gslot_ready, it + 1)
                        q = j - 2 * pairs
                        pe.wait_ge(S.hm_lo_ready, it * pairs + (q + 1))
                        for f in (2 * q, 2 * q + 1):
                            for y in range(2):
                                ins = split_products(ps[0:CAP, 6 + y, :], [x[:, f, :] for x in (hm_hi, hm_lo)],
                                                     [x[:, f % 2, 512 * y:512 * y + 512] for x in w],
                                                     f == 0, f == FC - 1)
                    ins.then_inc(S.parts_used, 1)
                    if z == 1 and 1 <= s <= pairs:
                        pe.wait_ge(S.mhid_prod, it * pairs + s)
                        if s >= 3:
                            pe.wait_ge(S.hm_lo_ready, it * pairs + (s - 2))
                        for half in range(2):
                            ins = pe.transpose(ps[:, 4 + (s - 1) % 2, CAP * half:CAP * half + CAP],
                                               hmTok[0:CAP, (s - 1) % 2, P * half:P * half + P], C.ident[0:CAP, 0:CAP])
                        ins.then_inc(S.ht_mm, 1)
                gather(it + 1)
                for c in range(DC):
                    if c % 4 == 0:
                        pe.wait_ge(S.y_lo_ready, 2 * it + (c // 4 + 1))
                    if c == 4:
                        turn_slots()
                    if c >= 4:
                        pe.wait_ge(S.h_item, DC * it + (DC + c - 3))
                    for part, y in enumerate((y_hi, y_lo)):
                        ins = mm(ps[:, c % 4, 0:SEQ], y[0:CAP, P * c:P * c + P], ohT[0:CAP, :],
                                 start=part == 0, stop=part == 1)
                    ins.then_inc(S.scat_mm, 1)
            pe.wait_ge(S.h_item, n_items * DC + DC)

            for i, (t0, n) in enumerate(OUT_TILES):
                for half in range(2):
                    for c in range(4):
                        ins = pe.transpose(ps[0:n, 2 * (i % 2) + half, P * c:P * c + P], hT[:, 4 * half + c, t0:t0 + n],
                                           C.ident)
                    ins.then_inc(S.out_mm, 1)


_OUT = (1, SEQ, D)


def kernel(**inputs):
    import concourse.bacc as _bacc
    from concourse.bass_utils import run_bass_kernel_spmd as _run

    nc = _bacc.Bacc("TRN2", target_bir_lowering=False, num_devices=1)
    arrays, A = {}, {}
    for name, value in list(inputs.items()) + [("consts", constants())]:
        a = np.ascontiguousarray(value)
        arrays[f"in_{name}"] = a
        A[name] = nc.dram_tensor(f"in_{name}", a.shape, mybir.dt.from_np(a.dtype), kind="ExternalInput").ap()
    out = nc.dram_tensor("out_0", _OUT, F32, kind="ExternalOutput").ap()
    build(nc, A, out)
    r = _run(nc, [arrays], core_ids=[0])
    return r.results[0]["out_0"]
```
